# Optimizing a Trainium2 kernel written in Bass

```python
import math
import jax, jax.numpy as jnp
from jax import lax
import numpy as np

D_MODEL = 2048
BATCH = 1
SEQ = 512
DEPTH = 1
DEC_BATCH = 8
DEC_SEQ = 8
PAST_LEN = 2048
PAGE_SIZE = 128

D_MIX = D_MODEL
W_A = D_MIX // 2
W_B = D_MIX - W_A
HD_A = 128
H_A = W_A // HD_A
CHUNK = 128
H_B = 8
DV_B = W_B // H_B
DH_B = DV_B // 2
D_IN = 2 * W_A + 3 * W_B
D_FF = (11 * D_MODEL) // 4
CONV_W = 3
Q_BLOCK = 128
EPS = 1e-6
SPARE_NUM = 5
SPARE_DEN = 4

kernel_name = 'hymba_gmlp_diffattn_convffn_step'

def rmsnorm(x, g):
    xf = x.astype(jnp.float32)
    y = xf * lax.rsqrt(jnp.mean(xf * xf, axis=-1, keepdims=True) + EPS)
    return (y * g.astype(jnp.float32)).astype(x.dtype)

def diff_lambda(lq1, lk1, lq2, lk2, lam_init):
    f = lambda a: a.astype(jnp.float32)
    return jnp.exp(jnp.sum(f(lq1) * f(lk1))) - jnp.exp(jnp.sum(f(lq2) * f(lk2))) + lam_init

def diff_attend(q, k, v, q_pos, k_pos, lam):
    scale = DH_B ** -0.5
    mask = k_pos[None, :] <= q_pos[:, None]

    def probs(qh, kh):
        s = jnp.einsum('bqhd,bkhd->bhqk', qh, kh).astype(jnp.float32) * scale
        return jax.nn.softmax(jnp.where(mask, s, -jnp.inf), axis=-1)

    w = probs(q[..., :DH_B], k[..., :DH_B]) - lam * probs(q[..., DH_B:], k[..., DH_B:])
    return jnp.einsum('bhqk,bkhe->bqhe', w.astype(v.dtype), v)

def prompt_attend(q, k, v, lam):
    B, S = q.shape[:2]
    nb = S // Q_BLOCK
    qb = q.reshape(B, nb, Q_BLOCK, H_B, DV_B).transpose(1, 0, 2, 3, 4)
    k_pos = jnp.arange(S)

    def block(args):
        qi, start = args
        return diff_attend(qi, k, v, start + jnp.arange(Q_BLOCK), k_pos, lam)

    o = lax.map(block, (qb, jnp.arange(nb) * Q_BLOCK))
    return o.transpose(1, 0, 2, 3, 4).reshape(B, S, H_B, DV_B)

def sample_attend(q, k_new, v_new, k_cache, v_cache, page_table, lam):
    DB, T = q.shape[:2]
    past = page_table.shape[1] * PAGE_SIZE
    k_past = k_cache[page_table].reshape(DB, past, H_B, DV_B)
    v_past = v_cache[page_table].reshape(DB, past, H_B, DV_B)
    k = jnp.concatenate([k_past, k_new.astype(k_past.dtype)], axis=1)
    v = jnp.concatenate([v_past, v_new.astype(v_past.dtype)], axis=1)
    return diff_attend(q, k, v, past + jnp.arange(T), jnp.arange(past + T), lam)

def chunk_gmlp(u, va, w_s, b_s):
    B, T = va.shape[:2]
    pad = (-T) % CHUNK
    nc = (T + pad) // CHUNK
    vc = jnp.pad(va, ((0, 0), (0, pad), (0, 0), (0, 0))).reshape(B, nc, CHUNK, H_A, HD_A)
    w = w_s * jnp.tril(jnp.ones((CHUNK, CHUNK), w_s.dtype))
    mixed = jnp.einsum('hts,bcshd->bcthd', w, vc) + b_s.T[:, :, None]
    mixed = mixed.reshape(B, nc * CHUNK, H_A, HD_A)[:, :T]
    return (u.reshape(B, T, H_A, HD_A) * mixed).reshape(B, T, W_A)

def causal_dwconv(hist, up, w_conv, b_conv):
    T = up.shape[1]
    hp = jnp.concatenate([hist.astype(up.dtype), up], axis=1)
    out = b_conv + sum(hp[:, j:j + T] * w_conv[j] for j in range(CONV_W))
    return out, hp[:, T:]

def layer(x, conv_hist, attend, lp, lam, lam_init):
    B, T, _ = x.shape
    z = rmsnorm(x, lp['g_pre_mix']) @ lp['w_in']
    u, va, q, k, vb = jnp.split(z, [W_A, 2 * W_A, 2 * W_A + W_B, 2 * W_A + 2 * W_B], axis=-1)
    u = jax.nn.gelu(u)
    va = rmsnorm(jax.nn.gelu(va).reshape(B, T, H_A, HD_A), lp['g_v_a'])
    q = q.reshape(B, T, H_B, DV_B)
    k = k.reshape(B, T, H_B, DV_B)
    vb = vb.reshape(B, T, H_B, DV_B)
    a_out = chunk_gmlp(u, va, lp['w_s'], lp['b_s'])
    o = attend(q, k, vb, lam)
    b_out = (rmsnorm(o, lp['g_subln']) * (1.0 - lam_init)).reshape(B, T, W_B)
    mix = jnp.concatenate([a_out, b_out.astype(a_out.dtype)], axis=-1) @ lp['w_out']
    h = x + rmsnorm(mix, lp['g_post_mix'])
    up = rmsnorm(h, lp['g_pre_ffn']) @ lp['w_up']
    c, new_hist = causal_dwconv(conv_hist, up, lp['w_conv'], lp['b_conv'])
    gate, val = jnp.split(c, 2, axis=-1)
    y = (jax.nn.gelu(gate) * val) @ lp['w_down']
    return h + rmsnorm(y, lp['g_post_ffn']), k, vb, new_hist, va

def setup_inputs(seed: int = 0) -> dict:
    key = jax.random.key(seed)
    ks = jax.random.split(key, 26)
    n_pages = PAST_LEN // PAGE_SIZE
    n_phys = (DEC_BATCH * n_pages * SPARE_NUM) // SPARE_DEN
    f32 = jnp.float32
    nrm = lambda k, shape, s: jax.random.normal(k, shape, f32) * s
    gain = lambda k, n: 1.0 + 0.05 * jax.random.normal(k, (DEPTH, n), f32)
    perm = jax.random.permutation(ks[5], n_phys)[:DEC_BATCH * n_pages]
    return {
        'x_prompt': nrm(ks[0], (BATCH, SEQ, D_MODEL), 1.0),
        'x_sample': nrm(ks[1], (DEC_BATCH, DEC_SEQ, D_MODEL), 1.0),
        'cache_k': nrm(ks[2], (DEPTH, n_phys, PAGE_SIZE, H_B, DV_B), 1.0),
        'cache_v': nrm(ks[3], (DEPTH, n_phys, PAGE_SIZE, H_B, DV_B), 1.0),
        'state_conv': nrm(ks[4], (DEPTH, DEC_BATCH, CONV_W - 1, 2 * D_FF), 1.0),
        'page_table': perm.reshape(DEC_BATCH, n_pages).astype(jnp.int32),
        'g_pre_mix': gain(ks[6], D_MODEL),
        'w_in': nrm(ks[7], (DEPTH, D_MODEL, D_IN), D_MODEL ** -0.5),
        'g_v_a': 1.0 + 0.05 * jax.random.normal(ks[8], (DEPTH, H_A, HD_A), f32),
        'w_s': nrm(ks[9], (DEPTH, H_A, CHUNK, CHUNK), CHUNK ** -0.5),
        'b_s': 1.0 + 0.1 * jax.random.normal(ks[10], (DEPTH, H_A, CHUNK), f32),
        'lam_q1': nrm(ks[11], (DEPTH, DH_B), 0.1),
        'lam_k1': nrm(ks[12], (DEPTH, DH_B), 0.1),
        'lam_q2': nrm(ks[13], (DEPTH, DH_B), 0.1),
        'lam_k2': nrm(ks[14], (DEPTH, DH_B), 0.1),
        'g_subln': gain(ks[15], DV_B),
        'w_out': nrm(ks[16], (DEPTH, D_MIX, D_MODEL), D_MIX ** -0.5),
        'g_post_mix': gain(ks[17], D_MODEL),
        'g_pre_ffn': gain(ks[18], D_MODEL),
        'w_up': nrm(ks[19], (DEPTH, D_MODEL, 2 * D_FF), D_MODEL ** -0.5),
        'w_conv': nrm(ks[20], (DEPTH, CONV_W, 2 * D_FF), CONV_W ** -0.5),
        'b_conv': nrm(ks[21], (DEPTH, 2 * D_FF), 0.02),
        'w_down': nrm(ks[22], (DEPTH, D_FF, D_MODEL), D_FF ** -0.5),
        'g_post_ffn': gain(ks[23], D_MODEL),
    }

def reference(x_prompt, x_sample, cache_k, cache_v, state_conv, page_table,
              g_pre_mix, w_in, g_v_a, w_s, b_s, lam_q1, lam_k1, lam_q2, lam_k2,
              g_subln, w_out, g_post_mix, g_pre_ffn, w_up, w_conv, b_conv, w_down,
              g_post_ffn):
    xp, xs = x_prompt, x_sample
    kp_l, vp_l, cp_l, ks_l, vs_l, cs_l, gs_l = [], [], [], [], [], [], []
    for l in range(DEPTH):
        lp = {'g_pre_mix': g_pre_mix[l], 'w_in': w_in[l], 'g_v_a': g_v_a[l],
              'w_s': w_s[l], 'b_s': b_s[l], 'g_subln': g_subln[l], 'w_out': w_out[l],
              'g_post_mix': g_post_mix[l], 'g_pre_ffn': g_pre_ffn[l], 'w_up': w_up[l],
              'w_conv': w_conv[l], 'b_conv': b_conv[l], 'w_down': w_down[l],
              'g_post_ffn': g_post_ffn[l]}
        lam_init = 0.8 - 0.6 * math.exp(-0.3 * l)
        lam = diff_lambda(lam_q1[l], lam_k1[l], lam_q2[l], lam_k2[l], lam_init)
        hist0 = jnp.zeros((xp.shape[0], CONV_W - 1, 2 * D_FF), xp.dtype)
        xp, kp, vp, cp, _ = layer(xp, hist0, prompt_attend, lp, lam, lam_init)
        kc, vc = cache_k[l], cache_v[l]
        attend_s = lambda q, k, v, lm, kc=kc, vc=vc: sample_attend(q, k, v, kc, vc, page_table, lm)
        xs, ksn, vsn, csn, gsn = layer(xs, state_conv[l], attend_s, lp, lam, lam_init)
        kp_l.append(kp); vp_l.append(vp); cp_l.append(cp)
        ks_l.append(ksn); vs_l.append(vsn); cs_l.append(csn); gs_l.append(gsn)
    k_prompt = jnp.stack(kp_l, 0)
    v_prompt = jnp.stack(vp_l, 0)
    conv_prompt = jnp.stack(cp_l, 0)
    k_sample = jnp.stack(ks_l, 0)
    v_sample = jnp.stack(vs_l, 0)
    conv_sample = jnp.stack(cs_l, 0)
    gmlp_v_sample = jnp.stack(gs_l, 0)
    return (xp, xs, k_prompt, v_prompt, conv_prompt, k_sample, v_sample, conv_sample, gmlp_v_sample)


_drawn_inputs = setup_inputs


def setup_inputs(seed=0):
    import zlib

    import numpy as np

    out = dict(_drawn_inputs(seed))
    spreads = {}
    factors = {'b_conv': 3.502}
    for name, (base, spread) in spreads.items():
        noise = np.random.default_rng([zlib.crc32(name.encode()), seed]).standard_normal(out[name].shape)
        drawn = base * np.exp(spread * noise) if base else spread * noise
        out[name] = __import__('jax').numpy.asarray(drawn.astype(out[name].dtype))
    for name, factor in factors.items():
        out[name] = (out[name] * factor).astype(out[name].dtype)
    return out
```

```python
import numpy as np

import concourse.bass as bass
from concourse import mybir

P = 128
ALU = mybir.AluOpType
ACT = mybir.ActivationFunctionType
AX = mybir.AxisListType
F32 = mybir.dt.float32
F32R = mybir.dt.float32r
I32 = mybir.dt.int32

D = 2048
SEQ = 512
DB, DT = 8, 8
NS = DB * DT
T = SEQ + NS
TH = T // 2
KD = D // P
H = 8
HD = 128
DH = HD // 2
PAGES = 16
N_PHYS = 160
FF = 5632
KF = FF // P
GRP = 4
ROUNDS = KF // GRP
EPS = 1e-6
SCALE = DH ** -0.5
LAM_INIT = 0.8 - 0.6
NEG = -1.0e30

UNIT = 1024
RAW = 2
HL = 4
U_QK, U_V, U_HEADS, U_OUT, U_FFN = 0, 32, 48, 80, 112
UNITS = U_FFN + 2 * 2 * KF + KF * KD // 8
PSLOTS = 8
C_PRE, C_POST, C_FFN, C_LAST = 0, 16, 32, 48
C_VA, C_SUB, C_B, C_W = 64, 72, 73, 73 + 2 * KF
C_ALL = C_W + 3 * 2 * KF
UB = 2 + SEQ + DB * (2 + DT)
NC_ = UB - 2


class Chain:

    def __init__(self, eng, sem, base, per=0, j=0):
        self.eng, self.sem, self.base, self.per, self.j, self.c = eng, sem, base, per, j, 0

    def link(self, ins):
        self.c += 1
        ins.then_inc(self.sem, 1)
        self.eng.wait_ge(self.sem, self.base + self.c + (self.per * self.j if self.per else 0))

    def close(self, n):
        assert self.c == n, (self.c, n)


def build(nc, xT, wstream, kpages, vpages, state, ptab, consts, lams, wsT, wblk, bs,
          y_out, k_out, v_out, vs_out, va_out, hist_out):
    zq_d = nc.dram_tensor("zq_d", (H, P, T), F32, kind="Internal").ap()
    qs_d = nc.dram_tensor("qs_d", (P, DB, H * 16), F32, kind="Internal").ap()
    ks_d = nc.dram_tensor("ks_d", (P, DB, H * DT), F32, kind="Internal").ap()
    mix_d = nc.dram_tensor("mix_d", (P, KD, T), F32, kind="Internal").ap()
    h_d = nc.dram_tensor("h_d", (P, KD, T), F32, kind="Internal").ap()

    top = [16512]

    def sb(name, shape, dt=F32, at=None):
        size = int(np.prod(shape[1:])) * 4
        size = (size + 31) // 32 * 32
        if at is None:
            off = top[0]
            top[0] += size
        else:
            off = at[0]
            at[0] += size
            at[1] = max(at[1], at[0])
        return nc.alloc_sbuf_tensor_at(name, shape, dt, offset=off)

    xh_at = top[0]
    xh = sb("xh", [P, KD, T], F32R)
    xl = sb("xl", [P, KD, T], F32R)
    wraw = sb("wraw", [P, RAW, UNIT])
    wh = sb("wh", [P, HL, UNIT], F32R)
    wl = sb("wl", [P, HL, UNIT], F32R)
    cs = sb("cs", [P, C_ALL])
    ident = sb("ident", [P, P])
    ones = sb("ones", [P, P])
    R = sb("R", [P, T])
    neglam = sb("neglam", [P, 1])
    gsub = sb("gsub", [P, 1])
    lt = sb("lt", [P, 4])
    ptab_sb = sb("ptab_sb", [1, DB * PAGES], I32)
    free0 = top[0]

    a = [free0, 0]
    xraw = sb("xraw", [P, KD, T], at=a)
    lamin = sb("lamin", [P, 4, DH], at=a)
    sq0 = sb("sq0", [P, 2, T], at=a)
    b = [a[0], a[0]]
    zt = [sb(f"zt{i}", [P, T], at=b) for i in range(2)]
    vt = [sb(f"vt{i}", [P, 5, P], at=b) for i in range(2)]
    qbd = sb("qbd", [P, DB, H, 16], at=b)
    kns = sb("kns", [P, DB, H, DT], at=b)

    c = [free0, 0]
    pg = sb("pg", [P, PSLOTS, H * P], at=c)
    ET = sb("ET", [P, PAGES, P], at=c)
    SCn = sb("SCn", [DT, P], at=c)
    W = sb("W", [P, 1280], at=c)
    E2 = sb("E2", [P, SEQ], at=c)
    wT = sb("wT", [P, 1280], at=c)
    qT = sb("qT", [P, SEQ], at=c)
    kT = sb("kT", [P, SEQ], at=c)
    V = sb("V", [P, 4, P], at=c)
    vnew = sb("vnew", [DT, H * P], at=c)
    ws = sb("ws", [P, P], at=c)
    wb = sb("wb", [NS, NS], at=c)
    bsb = sb("bsb", [P, P], at=c)
    vg = sb("vg", [P, T], at=c)
    vq = sb("vq", [P, T], at=c)
    vaT = sb("vaT", [P, T], at=c)
    ug = sb("ug", [P, T], at=c)
    ao = sb("ao", [P, T], at=c)
    po = sb("po", [P, SEQ], at=c)
    vtok = sb("vtok", [P, 5, P], at=c)
    bsmp = sb("bsmp", [P, H, NS], at=c)
    qb = sb("qb", [P, H, 16], at=c)
    knew = sb("knew", [P, H, DT], at=c)
    esum = sb("esum", [P, P], at=c)
    inv = sb("inv", [P, P], at=c)
    oT = sb("oT", [P, P], at=c)
    osm = sb("osm", [P, NS], at=c)
    osq = sb("osq", [P, NS], at=c)
    pmx = sb("pmx", [P, 2], at=c)
    pneg = sb("pneg", [P, 2], at=c)
    psm = sb("psm", [P, 8], at=c)
    prs = sb("prs", [P, 2], at=c)
    mx4 = sb("mx4", [P, 5], at=c)
    mx = sb("mx", [P, 1], at=c)
    maskd = sb("maskd", [P, P], at=c)
    maskn = sb("maskn", [DT, H, 2, DT], at=c)

    d = [free0, 0]
    area1 = d[0]
    mixf = sb("mixf", [P, KD, T], at=d)
    area2 = d[0]
    mix = sb("mix", [P, KD, T], at=d)
    sqt = sb("sqt", [P, 2, T], at=d)
    acc = sb("acc", [P, T], at=d)
    e = [area1, 0]
    xres = sb("xres", [P, KD, T], at=e)
    y = nc.alloc_sbuf_tensor_at("y", [P, KD, T], F32, offset=area1)
    f = [area2, 0]
    gh = sb("gh", [P, GRP, T], F32R, at=f)
    gl = sb("gl", [P, GRP, T], F32R, at=f)
    ub = [sb(f"ub{i}", [P, UB], at=f) for i in range(2)]
    cv = [sb(f"cv{i}", [P, UB], at=f) for i in range(2)]
    gv = sb("gv", [P, T], at=f)
    st = sb("st", [P, 2 * KF, 16], at=f)
    hs = sb("hs", [P, 2 * KF, 18], at=f)
    hres = nc.alloc_sbuf_tensor_at("hres", [P, KD, T], F32, offset=xh_at)
    g = [xh_at + KD * T * 4, 0]
    sql = sb("sql", [P, 2, T], at=g)
    accl = sb("accl", [P, T], at=g)
    for z in (a, b, c, d, e, f):
        assert z[1] <= 229344, z

    pb = nc.alloc_psum_tensor("pb", [P, 8, 512], F32)


    def sem(name):
        return nc.alloc_semaphore(name)

    w_landed = [sem(f"w_landed{i}") for i in range(RAW)]
    w_hi, w_lo, w_used = sem("w_hi"), sem("w_lo"), sem("w_used")
    c_landed, p_landed, ready = sem("c_landed"), sem("p_landed"), sem("consts_ready")
    x_landed = [sem(f"x_landed{i}") for i in range(4)]
    x_sq, x_hi, x_lo, x_ssq_mm = sem("x_sq"), sem("x_hi"), sem("x_lo"), sem("x_sq_used")
    sq_root, R_ready = sem("sq_root"), sem("R_ready")
    dve_c, pool_c, lam_sum, lam_exp = sem("dve_chain"), sem("pool_chain"), sem("lam_sum"), sem("lam_exp")
    q_evac, k_evac, smp = sem("q_evac"), sem("k_evac"), sem("sample_cols")
    q_stored, k_stored, s_stored = sem("q_stored"), sem("k_stored"), sem("sample_stored")
    v_evac, vT_ready, vt_evac = sem("v_evac"), sem("vT_ready"), sem("vt_evac")
    v_stored = [sem("v_stored0"), sem("v_stored1")]
    pg_landed = [sem(f"page_landed{i}") for i in range(PSLOTS)]
    pg_used = [sem(f"page_used{i}") for i in range(PSLOTS)]
    hq_landed, sq_landed, hv_landed, sv_landed, g_landed = (sem(x) for x in (
        "head_qk_landed", "sample_q_landed", "head_v_landed", "sample_v_landed", "gmlp_landed"))
    names_h = ("st_copied pscore_ready pexp_done pneg_ready pw_done stT_ready mx_part snew_ready "
               "scn_ready snT_ready mx_ready mb_ready etsub eexp esum_ready sums_ready wT_ready wT_copied "
               "u_evac ugelu va_evac vgelu vsq_ready vssq_ready vsd_done va_norm vaT_ready "
               "vtok_copied ws_masked spv_ready pv_ready po_copied posq pss_ready psd_done ssq_ready sss_ready "
               "ssd_done gm_ready ao_prompt a_done b_done bs_done va_stored a_stored b_stored bs_stored").split()
    s = {n: sem(n) for n in names_h}
    m_landed = [sem(f"mix_landed{i}") for i in range(4)]
    m_hi, m_lo, m_acc, acc_zero = (sem(x) for x in (
        "mix_hi", "mix_lo", "out_acc", "acc_zero"))
    m_copied = [sem(f"out_copied{t}") for t in range(2)]
    m_sq = [sem(f"out_sq{t}") for t in range(2)]
    r_landed = [sem(f"res_landed{i}") for i in range(4)]
    h_tmp, h_done, h_hi, h_lo, h_sq, h_acc, h_stored = (sem(x) for x in (
        "h_scaled", "h_done", "h_hi", "h_lo", "h_sq", "h_acc", "h_stored"))
    st_landed, st_in, hist_cp, tap, tap1, cv_done, gelu_done, gv_done, g_hi, g_lo = (sem(x) for x in (
        "state_landed", "state_in", "hist_out", "tap2_done", "tap1_done", "conv_done",
        "gelu_done", "gv_done", "g_hi", "g_lo"))
    up_evac = [sem("gate_evac"), sem("value_evac")]
    ub_zero = sem("prompt_history_zero")
    dn_even, dn_done, hist_stored, y_zero = sem("down_even_ready"), sem("down_added"), sem("hist_stored"), sem("y_zero")
    hr_landed = [sem(f"hr_landed{i}") for i in range(4)]
    y_sq, y_tmp, y_acc, y_done, y_stored, ssq_mm = sem("y_sq"), sem("y_scaled"), sem("y_acc"), sem("y_done"), sem("y_stored"), sem("ssq_mm")

    v, sc, pl, te, sy = nc.vector, nc.scalar, nc.gpsimd, nc.tensor, nc.sync

    def halves(ap):
        return ap.rearrange("p (c n) -> p c n", c=2)

    def w_load(base, c, per=0, j=0):
        u = base + c
        sy.wait_ge(w_lo, u + 5 + (per * j if per else 0))
        off = (u + 6) * P + (per * P * j if per else 0)
        sy.dma_start(wraw[:, c % RAW, :], wstream[bass.ds(off, P), :]).then_inc(w_landed[c % RAW], 16)

    def w_split_hi(base, c, per=0, j=0):
        u = base + c
        sc.wait_ge(w_landed[c % RAW], 16 * ((u + 4) // RAW + 1) + (16 * (per // RAW) * j if per else 0))
        sc.wait_ge(w_used, u + 1 + (per * j if per else 0))
        sc.activation(wh[:, c % HL, :], wraw[:, c % RAW, :], ACT.Copy).then_inc(w_hi, 1)

    def w_split_lo(base, c, per=0, j=0):
        pl.wait_ge(w_hi, base + c + 5 + (per * j if per else 0))
        pl.tensor_tensor(wl[:, c % HL, :], wraw[:, c % RAW, :], wh[:, c % HL, :].bitcast(F32),
                         ALU.subtract).then_inc(w_lo, 1)

    def unit_mm(bank, base, c, hi, lo, k0, nk, first, last, col=0, per=0, j=0, k_sem=None):
        te.wait_ge(w_lo, base + c + 1 + (per * j if per else 0))
        slot = c % HL
        for kt in range(nk):
            if k_sem is not None:
                te.wait_ge(k_sem, k0 + kt + 1)
            whk = wh[:, slot, col + kt * P:col + (kt + 1) * P]
            wlk = wl[:, slot, col + kt * P:col + (kt + 1) * P]
            a0, z0 = first and kt == 0, last and kt == nk - 1
            for n in range(2):
                te.matmul(pb[:, bank + n, 0:TH], whk, hi[:, k0 + kt, n * TH:(n + 1) * TH], start=a0, stop=False)
            for n in range(2):
                te.matmul(pb[:, bank + n, 0:TH], whk, lo[:, k0 + kt, n * TH:(n + 1) * TH], start=False, stop=False)
            for n in range(2):
                m = te.matmul(pb[:, bank + n, 0:TH], wlk, hi[:, k0 + kt, n * TH:(n + 1) * TH],
                              start=False, stop=z0)
        return m

    def tile_mm(bank, base, c, per=0, j=0, k_sem=None):
        unit_mm(bank, base, c, xh, xl, 0, 8, True, False, per=per, j=j, k_sem=k_sem).then_inc(w_used, 1)
        unit_mm(bank, base, c + 1, xh, xl, 8, 8, False, True, per=per, j=j, k_sem=k_sem).then_inc(w_used, 1)

    def tile_done(eng, base, c, per=0, j=0):
        eng.wait_ge(w_used, base + c + 2 + (per * j if per else 0))

    def tile_out(bank):
        return pb[:, bank:bank + 2, 0:TH]

    block = nc.Block().__enter__()

    @block.sync
    def _(sp):
        sp.dma_start(cs[:], consts).then_inc(c_landed, 16)
        sp.dma_start(lamin[:], lams.to_broadcast([P, 4, DH])).then_inc(c_landed, 16)
        for q in range(4):
            sp.dma_start(xraw[:, 4 * q:4 * q + 4, :], xT[:, 4 * q:4 * q + 4, :]).then_inc(x_landed[q], 16)
            if q < RAW:
                sp.dma_start(wraw[:, q, :], wstream[q * P:(q + 1) * P, :]).then_inc(w_landed[q], 16)
        for u in range(RAW, 6):
            sp.wait_ge(w_lo, u - RAW + 1)
            sp.dma_start(wraw[:, u % RAW, :], wstream[u * P:(u + 1) * P, :]).then_inc(w_landed[u % RAW], 16)

        with sp.Fori(0, H) as j:
            w_load(U_QK, 0, 4, j)
            w_load(U_QK, 1, 4, j)
            sp.wait_ge(q_evac, j + 1)
            sp.dma_start(zq_d[bass.ds(j, 1)].rearrange("a p n -> (a p) n"), zt[0][:]).then_inc(q_stored, 16)
            w_load(U_QK, 2, 4, j)
            w_load(U_QK, 3, 4, j)
            sp.wait_ge(k_evac, j + 1)
            sp.dma_start(k_out[bass.ds(j, 1)].rearrange("a p n -> (a p) n"), zt[1][:]).then_inc(k_stored, 16)
        sp.wait_ge(smp, 3 * H)
        sp.dma_start(qs_d, qbd[:].rearrange("p b h n -> p b (h n)")).then_inc(s_stored, 16)
        sp.dma_start(ks_d, kns[:].rearrange("p b h n -> p b (h n)")).then_inc(s_stored, 16)
        with sp.Fori(0, H // 2) as i:
            for c in range(4):
                w_load(U_V, c, 4, i)
            for t in range(2):
                sp.wait_ge(vt_evac, 2 * i + t + 1)
                sp.dma_start(v_out[bass.ds(2 * i + t, 1)].rearrange("a b p n -> p (a b) n"),
                             vt[t][:, 0:4, :]).then_inc(v_stored[t], 16)
                sp.dma_start(vs_out[:, bass.ds(2 * i + t, 1), :].rearrange("p a n -> p (a n)"),
                             vt[t][0:NS, 4, :]).then_inc(v_stored[t], 16)
        sp.wait_ge(q_stored, 16 * H)
        sp.wait_ge(k_stored, 16 * H)
        sp.wait_ge(s_stored, 32)
        sp.wait_ge(v_stored[0], 16 * H)
        sp.wait_ge(v_stored[1], 16 * H)
        sp.wait_ge(p_landed, 16)
        with sp.Fori(0, DB) as j:
            sp.wait_ge(s["pscore_ready"], 4 * j)
            sp.dma_start(qT[:], zq_d[bass.ds(j, 1), :, 0:SEQ].rearrange("a p n -> (a p) n")).then_inc(hq_landed, 16)
            sp.dma_start(kT[:], k_out[bass.ds(j, 1), :, 0:SEQ].rearrange("a p n -> (a p) n")).then_inc(hq_landed, 16)
            sp.wait_ge(s["snew_ready"], j)
            sp.dma_start(qb[:].rearrange("p h n -> p (h n)"),
                         qs_d[:, bass.ds(j, 1), :].rearrange("p a n -> p (a n)")).then_inc(sq_landed, 16)
            sp.dma_start(knew[:].rearrange("p h n -> p (h n)"),
                         ks_d[:, bass.ds(j, 1), :].rearrange("p a n -> p (a n)")).then_inc(sq_landed, 16)

            def page(n, j=j):
                slot = n % PSLOTS
                phys = sp.value_load(ptab_sb[0:1, bass.ds(PAGES * j + n % PAGES, 1)], min_val=0, max_val=N_PHYS - 1)
                sp.wait_ge(pg_used[slot], 4 * j + n // PSLOTS)
                src = kpages if n < PAGES else vpages
                sp.dma_start(pg[:, slot, :], src[bass.ds(phys, 1)].rearrange("a p n -> (a p) n")
                             ).then_inc(pg_landed[slot], 16)

            for n in range(8):
                page(n)
            sp.wait_ge(s["gm_ready"], j)
            sp.wait_ge(s["a_done"], j)
            sp.dma_start(ws[:], wsT[bass.ds(j, 1)].rearrange("a p n -> (a p) n")).then_inc(g_landed, 16)
            sp.dma_start(wb[:], wblk[bass.ds(j, 1)].rearrange("a p n -> (a p) n")).then_inc(g_landed, 16)
            sp.dma_start(bsb[:], bs[bass.ds(j, 1), :].to_broadcast([P, P])).then_inc(g_landed, 16)
            for n in range(8, 16):
                page(n)
            sp.wait_ge(s["pv_ready"], j)
            sp.dma_start(V[:], v_out[bass.ds(j, 1)].rearrange("a b p n -> p (a b) n")).then_inc(hv_landed, 16)
            sp.wait_ge(s["spv_ready"], j)
            sp.dma_start(vnew[:], vs_out[bass.ds(DT * j, DT)].rearrange("t h n -> t (h n)")).then_inc(sv_landed, 16)
            for n in range(16, 24):
                page(n)
            for c in range(4):
                w_load(U_HEADS, c, 4, j)
            for n in range(24, 32):
                page(n)

        sp.wait_ge(s["a_stored"], 16 * H)
        sp.wait_ge(s["va_stored"], 16 * H)
        for q in range(2):
            sp.dma_start(mixf[:, 4 * q:4 * q + 4, :], mix_d[:, 4 * q:4 * q + 4, :]).then_inc(m_landed[q], 16)
        sp.wait_ge(s["b_stored"], 16 * H)
        sp.wait_ge(s["bs_stored"], 16)
        for q in range(2, 4):
            sp.dma_start(mixf[:, 4 * q:4 * q + 4, :], mix_d[:, 4 * q:4 * q + 4, :]).then_inc(m_landed[q], 16)
        for q in range(4):
            sp.wait_ge(m_lo, 4 * q + 4)
            sp.dma_start(xres[:, 4 * q:4 * q + 4, :], xT[:, 4 * q:4 * q + 4, :]).then_inc(r_landed[q], 16)
        with sp.Fori(0, KD // 2) as i:
            for c in range(4):
                w_load(U_OUT, c, 4, i)
        for q in range(4):
            sp.wait_ge(h_done, 4 * q + 4)
            sp.dma_start(h_d[:, 4 * q:4 * q + 4, :], mix[:, 4 * q:4 * q + 4, :]).then_inc(h_stored, 16)
        sp.wait_ge(h_stored, 64)
        sp.wait_ge(h_lo, KD)
        sp.wait_ge(h_sq, KD)
        sp.wait_ge(h_hi, KD)
        sp.wait_ge(h_acc, KD)
        sp.dma_start(st[:], state).then_inc(st_landed, 16)

        for c in range(4):
            w_load(U_FFN, c)
        with sp.Fori(0, ROUNDS - 1) as i:
            for c in range(24):
                w_load(U_FFN + 4, c, 24, i)
        for c in range(20 - 6):
            w_load(UNITS - 20, c)
        sp.wait_ge(hist_cp, 2 * KF)
        sp.dma_start(hist_out, hs[:]).then_inc(hist_stored, 16)
        sp.wait_ge(w_used, UNITS - 8)
        for q in range(4):
            sp.dma_start(hres[:, 4 * q:4 * q + 4, :], h_d[:, 4 * q:4 * q + 4, :]).then_inc(hr_landed[q], 16)
        for q in range(4):
            sp.wait_ge(y_done, 4 * q + 4)
            sp.dma_start(y_out[:, 4 * q:4 * q + 4, :], y[:, 4 * q:4 * q + 4, :]).then_inc(y_stored, 16)
        sp.wait_ge(y_stored, 64)
        sp.wait_ge(hist_stored, 16)

    @block.scalar
    def _(act):
        for u in range(RAW):
            sc.wait_ge(w_landed[u], 16)
            sc.activation(wh[:, u, :], wraw[:, u, :], ACT.Copy).then_inc(w_hi, 1)
        act.wait_ge(c_landed, 32)
        act.wait_ge(lam_sum, 2)
        sc.activation(lt[:, 2:4], lt[:, 0:2], ACT.Exp).then_inc(lam_exp, 1)
        for q in range(4):
            act.wait_ge(x_landed[q], 16)
            with act.Fori(0, 4) as k:
                sc.activation(xh[:, bass.ds(4 * q + k, 1), :].rearrange("p a n -> p (a n)"),
                              xraw[:, bass.ds(4 * q + k, 1), :].rearrange("p a n -> p (a n)"), ACT.Copy,
                              scale=cs[:, bass.ds(C_PRE + 4 * q + k, 1)]).then_inc(x_hi, 1)
            if q == 0:
                for u in range(RAW, 4):
                    act.wait_ge(w_landed[u % RAW], 32)
                    sc.activation(wh[:, u, :], wraw[:, u % RAW, :], ACT.Copy).then_inc(w_hi, 1)
        act.wait_ge(x_ssq_mm, KD)
        sc.activation(halves(R[:]), tile_out(6), ACT.Sqrt, scale=1.0 / D, bias=EPS).then_inc(sq_root, 1)

        with act.Fori(0, H) as j:
            w_split_hi(U_QK, 0, 4, j)
            w_split_hi(U_QK, 1, 4, j)
            act.wait_ge(q_evac, j + 1)
            act.wait_ge(pool_c, 2)
            for z in range(2):
                sc.activation(
                    qbd[DH * z:DH * z + DH, :, bass.ds(j, 1), DT * z:DT * z + DT].rearrange("p b a n -> p b (a n)"),
                    zt[0][DH * z:DH * z + DH, SEQ:T].rearrange("p (b n) -> p b n", b=DB), ACT.Copy).then_inc(smp, 1)
            w_split_hi(U_QK, 2, 4, j)
            w_split_hi(U_QK, 3, 4, j)
            act.wait_ge(k_evac, j + 1)
            act.wait_ge(pool_c, 2)
            sc.activation(kns[:, :, bass.ds(j, 1), :].rearrange("p b a n -> p b (a n)"),
                          zt[1][:, SEQ:T].rearrange("p (b n) -> p b n", b=DB), ACT.Copy).then_inc(smp, 1)
        with act.Fori(0, H // 2) as i:
            for c in range(4):
                w_split_hi(U_V, c, 4, i)

        with act.Fori(0, DB) as j:
            act.wait_ge(s["spv_ready"], j)
            for g_ in range(4):
                n = (g_ + 1) * P
                o = g_ * (g_ + 1) // 2 * P
                last = 4 * g_ + 3
                act.wait_ge(pg_used[last % PSLOTS], 4 * j + last // PSLOTS + 1)
                sc.activation(ET[:, 4 * g_:4 * g_ + 4, :], pb[:, 2, :].rearrange("p (g n) -> p g n", g=4),
                              ACT.Copy).then_inc(s["st_copied"], 1)
                act.wait_ge(s["pneg_ready"], 4 * j + g_ + 1)
                act.wait_ge(s["wT_ready"], 4 * j)
                sc.activation(W[:, o:o + n], pb[:, 6, 0:n], ACT.Exp, scale=SCALE, bias=pneg[:, 0:1],
                              accum_out=psm[:, 2 * g_:2 * g_ + 1]).then_inc(s["pexp_done"], 1)
                act.wait_ge(s["pw_done"], 4 * j + g_)
                act.wait_ge(s["psd_done"], j)
                act.wait_ge(s["b_done"], j)
                sc.activation(E2[:, 0:n], pb[:, 7, 0:n], ACT.Exp, scale=SCALE, bias=pneg[:, 1:2],
                              accum_out=psm[:, 2 * g_ + 1:2 * g_ + 2]).then_inc(s["pexp_done"], 1)
            w_split_hi(U_HEADS, 0, 4, j)
            for g_ in range(4):
                act.wait_ge(s["etsub"], 5 * j + g_ + 1)
                sc.activation(ET[:, 4 * g_:4 * g_ + 4, :], ET[:, 4 * g_:4 * g_ + 4, :], ACT.Exp,
                              scale=SCALE).then_inc(s["eexp"], 1)
            act.wait_ge(s["etsub"], 5 * j + 5)
            sc.activation(SCn[:], SCn[:], ACT.Exp, scale=SCALE).then_inc(s["eexp"], 1)
            w_split_hi(U_HEADS, 1, 4, j)
            act.wait_ge(s["u_evac"], j + 1)
            sc.activation(ug[:], ug[:], ACT.Gelu_apprx_tanh).then_inc(s["ugelu"], 1)
            w_split_hi(U_HEADS, 2, 4, j)
            w_split_hi(U_HEADS, 3, 4, j)
            act.wait_ge(s["va_evac"], j + 1)
            sc.activation(vg[:], vg[:], ACT.Gelu_apprx_tanh).then_inc(s["vgelu"], 1)
            act.wait_ge(s["vgelu"], j + 1)
            sc.activation(vq[:], vg[:], ACT.Square).then_inc(s["vsq_ready"], 1)
            act.wait_ge(s["vssq_ready"], j + 1)
            sc.activation(halves(vq[:]), tile_out(2), ACT.Sqrt, scale=1.0 / HD, bias=EPS).then_inc(s["vsd_done"], 1)
            act.wait_ge(s["po_copied"], j + 1)
            act.wait_ge(s["pw_done"], 4 * j + 4)
            sc.activation(E2[:], po[:], ACT.Square).then_inc(s["posq"], 1)
            act.wait_ge(s["pss_ready"], j + 1)
            sc.activation(E2[:], pb[:, 0, :], ACT.Sqrt, scale=1.0 / HD, bias=EPS).then_inc(s["psd_done"], 1)
            act.wait_ge(s["sss_ready"], j + 1)
            sc.activation(osq[:], pb[:, 5, 384:384 + NS], ACT.Sqrt, scale=1.0 / HD, bias=EPS).then_inc(s["ssd_done"], 1)

        for q in range(4):
            act.wait_ge(m_landed[q], 16)
            if q == 0:
                act.wait_ge(w_used, U_OUT)
            with act.Fori(0, 4) as k:
                sc.activation(xh[:, bass.ds(4 * q + k, 1), :].rearrange("p a n -> p (a n)"),
                              mixf[:, bass.ds(4 * q + k, 1), :].rearrange("p a n -> p (a n)"),
                              ACT.Copy).then_inc(m_hi, 1)
        with act.Fori(0, KD // 2) as i:
            for t in range(2):
                w_split_hi(U_OUT, 2 * t, 4, i)
                w_split_hi(U_OUT, 2 * t + 1, 4, i)
                act.wait_ge(m_copied[t], i + 1)
                act.wait_ge(m_acc, 2 * i)
                act.wait_ge(c_landed, 32)
                sc.activation(sqt[:, t, :], mix[:, bass.ds(2 * i + t, 1), :].rearrange("p a n -> p (a n)"),
                              ACT.Square).then_inc(m_sq[t], 1)
        act.wait_ge(ssq_mm, 1)
        sc.activation(halves(R[:]), tile_out(4), ACT.Sqrt, scale=1.0 / D, bias=EPS).then_inc(sq_root, 1)
        with act.Fori(0, KD // 2) as i:
            for t in range(2):
                act.wait_ge(h_acc, 2 * i)
                act.wait_ge(h_done, 2 * i + t + 1)
                act.wait_ge(c_landed, 32)
                sc.activation(xh[:, bass.ds(2 * i + t, 1), :].rearrange("p a n -> p (a n)"),
                              mix[:, bass.ds(2 * i + t, 1), :].rearrange("p a n -> p (a n)"), ACT.Copy,
                              scale=cs[:, bass.ds(C_FFN + 2 * i + t, 1)]).then_inc(h_hi, 1)
                sc.activation(sqt[:, t, :], mix[:, bass.ds(2 * i + t, 1), :].rearrange("p a n -> p (a n)"),
                              ACT.Square).then_inc(h_sq, 1)
        act.wait_ge(ssq_mm, 2)
        act.wait_ge(h_lo, KD)
        sc.activation(halves(R[:]), tile_out(6), ACT.Sqrt, scale=1.0 / D, bias=EPS).then_inc(sq_root, 1)

        def conv_tap2(p, t, n):
            act.wait_ge(up_evac[t], n + 1)
            act.wait_ge(st_in, 2 * n + t + 1)
            act.wait_ge(gv_done, n)
            act.wait_ge(c_landed, 32)
            f = p + KF * t
            sc.activation(cv[t][:, 0:NC_], ub[t][:, 2:UB], ACT.Identity, scale=cs[:, bass.ds(C_W + 4 * KF + f, 1)],
                          bias=cs[:, bass.ds(C_B + f, 1)]).then_inc(tap, 1)

        def pair_act(p, n, splits):
            splits[0]()
            conv_tap2(p, 0, n)
            act.wait_ge(cv_done, 2 * n + 1)
            sc.activation(cv[0][:, 0:NC_], cv[0][:, 0:NC_], ACT.Gelu_apprx_tanh).then_inc(gelu_done, 1)
            splits[1]()
            conv_tap2(p, 1, n)

        def g_split_hi(n, slot, groups):
            act.wait_ge(gv_done, n + 1)
            act.wait_ge(w_used, U_FFN + 4 + 24 * groups)
            sc.activation(gh[:, slot, :], gv[:], ACT.Copy).then_inc(g_hi, 1)

        def pair_splits(base, c, per=0, i=0):
            return [lambda k=k: (w_split_hi(base, c + 2 * k, per, i), w_split_hi(base, c + 2 * k + 1, per, i))
                    for k in range(2)]

        pair_act(0, 0, pair_splits(U_FFN, 0))
        g_split_hi(0, 0, 0)
        with act.Fori(0, ROUNDS - 1) as i:
            for t in range(3):
                pair_act(GRP * i + 1 + t, GRP * i + 1 + t, pair_splits(U_FFN + 4, 4 * t, 24, i))
                g_split_hi(GRP * i + 1 + t, 1 + t, i)
            pair_act(GRP * i + 4, GRP * i + 4, pair_splits(U_FFN + 4, 12, 24, i))
            for c in range(16, 24):
                w_split_hi(U_FFN + 4, c, 24, i)
            g_split_hi(GRP * i + 4, 0, i + 1)
        for t in range(3):
            pair_act(KF - 3 + t, KF - 3 + t, pair_splits(UNITS - 20, 4 * t))
            g_split_hi(KF - 3 + t, 1 + t, ROUNDS - 1)
        for c in range(12, 16):
            w_split_hi(UNITS - 20, c)
        act.wait_ge(dn_done, KD * ROUNDS)
        with act.Fori(0, KD // 2) as i:
            for t in range(2):
                act.wait_ge(y_acc, 2 * i)
                act.wait_ge(c_landed, 32)
                sc.activation(sql[:, t, :], y[:, bass.ds(2 * i + t, 1), :].rearrange("p a n -> p (a n)"),
                              ACT.Square).then_inc(y_sq, 1)
        act.wait_ge(ssq_mm, 3)
        sc.activation(halves(R[:]), tile_out(0), ACT.Sqrt, scale=1.0 / D, bias=EPS).then_inc(sq_root, 1)

    @block.gpsimd
    def _(pool):
        pl.memset(ones[:], 1.0).then_inc(ready, 1)
        pl.memset(ident[:], 0.0).then_inc(pool_c, 1)
        pool.wait_ge(pool_c, 1)
        pl.affine_select(out=ident[:], in_=ident[:], compare_op=ALU.not_equal, fill=1.0, base=0,
                         pattern=[[-1, P]], channel_multiplier=1).then_inc(ready, 1)
        pool.wait_ge(w_hi, 1)
        pl.tensor_tensor(wl[:, 0, :], wraw[:, 0, :], wh[:, 0, :].bitcast(F32), ALU.subtract).then_inc(w_lo, 1)
        pool.wait_ge(w_hi, 2)
        pl.tensor_tensor(wl[:, 1, :], wraw[:, 1, :], wh[:, 1, :].bitcast(F32), ALU.subtract).then_inc(w_lo, 1)
        for q in range(4):
            pool.wait_ge(x_landed[q], 16)
            with pool.Fori(0, 2) as i:
                for t in range(2):
                    pool.wait_ge(x_ssq_mm, 4 * q + 2 * i)
                    xk = xraw[:, bass.ds(4 * q + 2 * i + t, 1), :].rearrange("p a n -> p (a n)")
                    pl.tensor_tensor(sq0[:, t, :], xk, xk, ALU.mult).then_inc(x_sq, 1)
        for u in range(2, 4):
            pool.wait_ge(w_hi, u + 1)
            pl.tensor_tensor(wl[:, u, :], wraw[:, u % RAW, :], wh[:, u, :].bitcast(F32),
                             ALU.subtract).then_inc(w_lo, 1)
        pl.memset(qbd[:], 0.0).then_inc(pool_c, 1)
        with pool.Fori(0, H) as j:
            for c in range(4):
                w_split_lo(U_QK, c, 4, j)
        pool.dma_start(ptab_sb[:], ptab).then_inc(p_landed, 16)
        with pool.Fori(0, H // 2) as i:
            for c in range(4):
                w_split_lo(U_V, c, 4, i)
        pool.wait_ge(s_stored, 32)
        pl.memset(maskd[:], 0.0).then_inc(pool_c, 1)
        pl.memset(maskn[:], 0.0).then_inc(pool_c, 1)
        pool.wait_ge(pool_c, 4)
        pl.affine_select(out=maskd[:], in_=maskd[:], compare_op=ALU.is_ge, fill=NEG, base=0,
                         pattern=[[-1, P]], channel_multiplier=1).then_inc(ready, 1)
        pl.affine_select(out=maskn[:], in_=maskn[:], compare_op=ALU.is_ge, fill=NEG, base=0,
                         pattern=[[0, H], [0, 2], [1, DT]], channel_multiplier=-1).then_inc(ready, 1)
        with pool.Fori(0, DB) as j:
            pool.wait_ge(g_landed, 48 * j + 48)
            w_split_lo(U_HEADS, 0, 4, j)
            pl.affine_select(out=ws[:], in_=ws[:], compare_op=ALU.is_ge, fill=0.0, base=0,
                             pattern=[[1, P]], channel_multiplier=-1).then_inc(s["ws_masked"], 1)
            pl.affine_select(out=wb[:], in_=wb[:], compare_op=ALU.is_ge, fill=0.0, base=0,
                             pattern=[[1, NS]], channel_multiplier=-1).then_inc(s["ws_masked"], 1)
            for c in range(1, 4):
                w_split_lo(U_HEADS, c, 4, j)
            pool.wait_ge(s["va_norm"], j + 1)
            pool.dma_start(va_out[bass.ds(j, 1)].rearrange("a p n -> (a p) n"), vaT[:, SEQ:T]
                           ).then_inc(s["va_stored"], 16)
            pool.wait_ge(s["a_done"], j + 1)
            pool.dma_start(mix_d[:, bass.ds(j, 1), :].rearrange("p a n -> p (a n)"), ao[:]).then_inc(s["a_stored"], 16)
            pool.wait_ge(s["b_done"], j + 1)
            pool.dma_start(mix_d[:, bass.ds(H + j, 1), 0:SEQ].rearrange("p a n -> p (a n)"), po[:]
                           ).then_inc(s["b_stored"], 16)
        pool.wait_ge(s["bs_done"], DB)
        pool.dma_start(mix_d[:, H:2 * H, SEQ:T], bsmp[:]).then_inc(s["bs_stored"], 16)
        with pool.Fori(0, KD // 2) as i:
            for c in range(4):
                w_split_lo(U_OUT, c, 4, i)
        pool.wait_ge(h_done, KD)
        pl.memset(y[:], 0.0).then_inc(y_zero, 1)

        def hist(p, n):
            for t in range(2):
                f = p + KF * t
                if n is not None:
                    pool.wait_ge(cv_done, 2 * n)
                pl.tensor_copy(ub[t][:, 2 + SEQ:UB].rearrange("p (b n) -> p b n", b=DB)[:, :, 0:2],
                               st[:, bass.ds(f, 1), :].rearrange("p a (b n) -> p (a b) n", b=DB)).then_inc(st_in, 1)

        def hist_new(p, n):
            for t in range(2):
                f = p + KF * t
                pool.wait_ge(up_evac[t], n + 1)
                pl.tensor_copy(hs[:, bass.ds(f, 1), 0:2].rearrange("p a n -> p (a n)"),
                               ub[t][:, SEQ:SEQ + 2])
                pl.tensor_copy(hs[:, bass.ds(f, 1), 2:18].rearrange("p a (b n) -> p (a b) n", b=DB),
                               ub[t][:, 2 + SEQ:UB].rearrange("p (b n) -> p b n", b=DB)[:, :, DT:DT + 2]
                               ).then_inc(hist_cp, 1)

        def g_split_lo(n, slot):
            pool.wait_ge(g_hi, n + 1)
            pl.tensor_tensor(gl[:, slot, :], gv[:], gh[:, slot, :].bitcast(F32), ALU.subtract).then_inc(g_lo, 1)

        pool.wait_ge(st_landed, 16)
        hist(0, None)
        for c in range(4):
            w_split_lo(U_FFN, c)
        hist_new(0, 0)
        g_split_lo(0, 0)
        with pool.Fori(0, ROUNDS - 1) as i:
            for t in range(4):
                p = GRP * i + 1 + t
                hist(p, p)
                for c in range(4):
                    w_split_lo(U_FFN + 4, 4 * t + c, 24, i)
                hist_new(p, p)
                if t < 3:
                    g_split_lo(p, 1 + t)
            for c in range(16, 24):
                w_split_lo(U_FFN + 4, c, 24, i)
            g_split_lo(GRP * i + 4, 0)
        for t in range(3):
            p = KF - 3 + t
            hist(p, p)
            for c in range(4):
                w_split_lo(UNITS - 20, 4 * t + c)
            hist_new(p, p)
            g_split_lo(p, 1 + t)
        for c in range(12, 16):
            w_split_lo(UNITS - 20, c)

    @block.vector
    def _(dve):
        dve.wait_ge(c_landed, 32)
        for z in range(2):
            v.tensor_tensor_reduce(out=lamin[:, 2 * z, :], in0=lamin[:, 2 * z, :], in1=lamin[:, 2 * z + 1, :],
                                   scale=1.0, scalar=0.0, op0=ALU.mult, op1=ALU.add,
                                   accum_out=lt[:, z:z + 1]).then_inc(lam_sum, 1)
        ch = Chain(dve, dve_c, 0)
        ch.link(v.tensor_scalar(gsub[:], cs[:, C_SUB:C_SUB + 1], 1.0 - LAM_INIT, None, ALU.mult))
        for q in range(4):
            dve.wait_ge(x_landed[q], 16)
            with dve.Fori(0, 4) as k:
                dve.wait_ge(x_hi, 4 * q + k + 1)
                v.scalar_tensor_tensor(out=xl[:, bass.ds(4 * q + k, 1), :].rearrange("p a n -> p (a n)"),
                                       in0=xraw[:, bass.ds(4 * q + k, 1), :].rearrange("p a n -> p (a n)"),
                                       scalar=cs[:, bass.ds(C_PRE + 4 * q + k, 1)],
                                       in1=xh[:, bass.ds(4 * q + k, 1), :].rearrange("p a n -> p (a n)").bitcast(F32),
                                       op0=ALU.mult, op1=ALU.subtract).then_inc(x_lo, 1)
        dve.wait_ge(lam_exp, 1)
        ch.link(v.tensor_tensor(lt[:, 0:1], lt[:, 3:4], lt[:, 2:3], ALU.subtract))
        ch.link(v.tensor_scalar(neglam[:], lt[:, 0:1], -LAM_INIT, None, ALU.add))
        dve.wait_ge(sq_root, 1)
        v.reciprocal(R[:], R[:]).then_inc(R_ready, 1)
        dve.wait_ge(R_ready, 1)
        Rh = halves(R[:])
        with dve.Fori(0, H) as j:
            tile_done(dve, U_QK, 0, 4, j)
            dve.wait_ge(q_stored, 16 * j)
            dve.wait_ge(smp, 3 * j)
            v.tensor_tensor(halves(zt[0][:]), tile_out(0), Rh, ALU.mult).then_inc(q_evac, 1)
            tile_done(dve, U_QK, 2, 4, j)
            dve.wait_ge(k_stored, 16 * j)
            v.tensor_tensor(halves(zt[1][:]), tile_out(2), Rh, ALU.mult).then_inc(k_evac, 1)
        dve.wait_ge(q_stored, 16 * H)
        dve.wait_ge(k_stored, 16 * H)
        dve.wait_ge(smp, 3 * H)
        with dve.Fori(0, H // 2) as i:
            for t in range(2):
                tile_done(dve, U_V, 2 * t, 4, i)
                dve.wait_ge(vT_ready, 2 * i)
                v.tensor_tensor(halves(zt[t][:]), tile_out(2 * t), Rh, ALU.mult).then_inc(v_evac, 1)
            for t in range(2):
                dve.wait_ge(vT_ready, 2 * i + t + 1)
                dve.wait_ge(v_stored[t], 32 * i)
                v.tensor_copy(vt[t][:, 0:4, :], pb[:, 4 + t, :].rearrange("p (b n) -> p b n", b=4)
                              )
                v.tensor_copy(vt[t][0:NS, 4, :], pb[0:NS, 6 + t, 0:P]).then_inc(vt_evac, 1)

        dve.wait_ge(ready, 4)
        dve.wait_ge(v_stored[0], 16 * H)
        dve.wait_ge(v_stored[1], 16 * H)
        base = ch.c
        NCH = 28
        with dve.Fori(0, DB) as j:
            ch = Chain(dve, dve_c, base, NCH, j)

            def combine(g_):
                n = (g_ + 1) * P
                o = g_ * (g_ + 1) // 2 * P
                dve.wait_ge(s["pexp_done"], 8 * j + 2 * g_ + 2)
                ch.link(v.reciprocal(prs[:], psm[:, 2 * g_:2 * g_ + 2]))
                ch.link(v.tensor_tensor(prs[:, 1:2], prs[:, 1:2], neglam[:], ALU.mult))
                ch.link(v.tensor_scalar(W[:, o:o + n], W[:, o:o + n], prs[:, 0:1], None, ALU.mult))
                v.scalar_tensor_tensor(out=W[:, o:o + n], in0=E2[:, 0:n], scalar=prs[:, 1:2], in1=W[:, o:o + n],
                                       op0=ALU.mult, op1=ALU.add).then_inc(s["pw_done"], 1)

            def st_max(g_):
                dve.wait_ge(s["stT_ready"], 4 * j + g_ + 1)
                v.tensor_reduce(mx4[:, g_:g_ + 1], pb[:, 4, :], AX.X, ALU.max).then_inc(s["mx_part"], 1)

            for g_ in range(4):
                n = (g_ + 1) * P
                dve.wait_ge(s["pscore_ready"], 4 * j + g_ + 1)
                diag = pb[:, 6:8, g_ * P:n]
                ch.link(v.tensor_tensor(diag, diag, maskd[:].rearrange("p (a n) -> p a n", a=1)
                                        .to_broadcast([P, 2, P]), ALU.add))
                ch.link(v.tensor_reduce(pmx[:], pb[:, 6:8, 0:n], AX.X, ALU.max))
                dve.wait_ge(s["pexp_done"], 8 * j + 2 * g_)
                v.tensor_scalar(pneg[:], pmx[:], -SCALE, None, ALU.mult).then_inc(s["pneg_ready"], 1)
                if g_ >= 1:
                    st_max(g_ - 1)
                    combine(g_ - 1)
            dve.wait_ge(s["snew_ready"], j + 1)
            v.tensor_tensor(SCn[:], pb[0:DT, 5, 0:P], maskn[:].rearrange("p h z n -> p (h z n)"), ALU.add
                            ).then_inc(s["scn_ready"], 1)
            combine(3)
            st_max(3)
            dve.wait_ge(s["snT_ready"], j + 1)
            ch.link(v.tensor_reduce(mx4[:, 4:5], pb[:, 5, P:P + DT], AX.X, ALU.max))
            dve.wait_ge(s["mx_part"], 4 * j + 4)
            v.tensor_reduce(mx[:], mx4[:], AX.X, ALU.max).then_inc(s["mx_ready"], 1)

            def copy_wT(g_):
                n = (g_ + 1) * P
                o = g_ * (g_ + 1) // 2 * P
                dve.wait_ge(s["wT_ready"], 4 * j + g_ + 1)
                dve.wait_ge(s["pv_ready"], j)
                v.tensor_copy(wT[:, o:o + n], pb[:, 6 + g_ % 2, 0:n]).then_inc(s["wT_copied"], 1)

            copy_wT(0)
            copy_wT(1)
            dve.wait_ge(s["mb_ready"], j + 1)
            mb = pb[:, 5, 2 * P:3 * P]
            for g_ in range(4):
                v.tensor_tensor(ET[:, 4 * g_:4 * g_ + 4, :], ET[:, 4 * g_:4 * g_ + 4, :],
                                mb.rearrange("p (a n) -> p a n", a=1).to_broadcast([P, 4, P]), ALU.subtract
                                ).then_inc(s["etsub"], 1)
            dve.wait_ge(s["scn_ready"], j + 1)
            v.tensor_tensor(SCn[:], SCn[:], pb[0:DT, 5, 2 * P:3 * P], ALU.subtract).then_inc(s["etsub"], 1)
            tile_done(dve, U_HEADS, 0, 4, j)
            dve.wait_ge(s["a_done"], j)
            v.tensor_tensor(halves(ug[:]), tile_out(0), Rh, ALU.mult).then_inc(s["u_evac"], 1)
            copy_wT(2)
            copy_wT(3)
            dve.wait_ge(s["eexp"], 5 * j + 5)
            v.tensor_reduce(esum[:], ET[:].rearrange("p g n -> p n g"), AX.X, ALU.add).then_inc(s["esum_ready"], 1)
            tile_done(dve, U_HEADS, 2, 4, j)
            v.tensor_tensor(halves(vg[:]), tile_out(0), Rh, ALU.mult).then_inc(s["va_evac"], 1)
            dve.wait_ge(s["sums_ready"], j + 1)
            ch.link(v.reciprocal(inv[:], pb[:, 5, 0:P]))
            dve.wait_ge(s["vsd_done"], j + 1)
            ch.link(v.reciprocal(vq[:], vq[:]))
            dve.wait_ge(s["va_stored"], 16 * j)
            v.scalar_tensor_tensor(out=vaT[:], in0=vg[:], scalar=cs[:, bass.ds(C_VA + j, 1)], in1=vq[:],
                                   op0=ALU.mult, op1=ALU.mult).then_inc(s["va_norm"], 1)
            dve.wait_ge(s["vaT_ready"], j + 1)
            v.tensor_copy(vtok[:, 0:4, :], pb[:, 2, :].rearrange("p (b n) -> p b n", b=4)
                          ).then_inc(s["vtok_copied"], 1)
            v.tensor_copy(vtok[0:NS, 4, :], pb[0:NS, 3, 0:P]).then_inc(s["vtok_copied"], 1)
            dve.wait_ge(s["spv_ready"], j + 1)
            ch.link(v.tensor_tensor(oT[:], pb[:, 4, 0:P], inv[:], ALU.mult))
            o4 = oT[:].rearrange("p (h z n) -> p h z n", h=H, z=2)
            ch.link(v.scalar_tensor_tensor(out=osm[:].rearrange("p (h n) -> p h n", h=H), in0=o4[:, :, 1, :],
                                           scalar=neglam[:, 0:1], in1=o4[:, :, 0, :], op0=ALU.mult, op1=ALU.add))
            v.tensor_tensor(osq[:], osm[:], osm[:], ALU.mult).then_inc(s["ssq_ready"], 1)
            dve.wait_ge(s["pv_ready"], j + 1)
            dve.wait_ge(s["b_stored"], 16 * j)
            v.tensor_copy(po[:], pb[:, 7, :]).then_inc(s["po_copied"], 1)
            dve.wait_ge(s["gm_ready"], j + 1)
            dve.wait_ge(g_landed, 48 * j + 48)
            dve.wait_ge(s["a_stored"], 16 * j)
            v.tensor_tensor(ao[:, 0:SEQ].rearrange("p (b n) -> p b n", b=4),
                            pb[:, 6, :].rearrange("p (b n) -> p b n", b=4),
                            bsb[:].rearrange("p (a n) -> p a n", a=1).to_broadcast([P, 4, P]), ALU.add
                            ).then_inc(s["ao_prompt"], 1)
            ch.link(v.tensor_tensor(ao[:, SEQ:T].rearrange("p (b n) -> p b n", b=DB),
                                    pb[:, 3, P:P + NS].rearrange("p (b n) -> p b n", b=DB),
                                    bsb[:, 0:DT].rearrange("p (a n) -> p a n", a=1).to_broadcast([P, DB, DT]),
                                    ALU.add))
            dve.wait_ge(s["ao_prompt"], j + 1)
            dve.wait_ge(s["ugelu"], j + 1)
            v.tensor_tensor(ao[:], ao[:], ug[:], ALU.mult).then_inc(s["a_done"], 1)
            dve.wait_ge(s["psd_done"], j + 1)
            dve.wait_ge(s["po_copied"], j + 1)
            ch.link(v.reciprocal(E2[:], E2[:]))
            v.scalar_tensor_tensor(out=po[:], in0=po[:], scalar=gsub[:, 0:1], in1=E2[:],
                                   op0=ALU.mult, op1=ALU.mult).then_inc(s["b_done"], 1)
            dve.wait_ge(s["ssd_done"], j + 1)
            ch.link(v.reciprocal(osq[:], osq[:]))
            v.scalar_tensor_tensor(out=bsmp[:, :, bass.ds(DT * j, DT)],
                                   in0=osm[:].rearrange("p (h n) -> p h n", h=H), scalar=gsub[:, 0:1],
                                   in1=osq[:].rearrange("p (h n) -> p h n", h=H),
                                   op0=ALU.mult, op1=ALU.mult).then_inc(s["bs_done"], 1)
            ch.close(NCH)

        for q in range(4):
            dve.wait_ge(m_landed[q], 16)
            with dve.Fori(0, 4) as k:
                dve.wait_ge(m_hi, 4 * q + k + 1)
                v.tensor_tensor(xl[:, bass.ds(4 * q + k, 1), :].rearrange("p a n -> p (a n)"),
                                mixf[:, bass.ds(4 * q + k, 1), :].rearrange("p a n -> p (a n)"),
                                xh[:, bass.ds(4 * q + k, 1), :].rearrange("p a n -> p (a n)").bitcast(F32),
                                ALU.subtract).then_inc(m_lo, 1)
        v.memset(acc[:], 0.0).then_inc(acc_zero, 1)
        dve.wait_ge(acc_zero, 1)
        with dve.Fori(0, KD // 2) as i:
            for t in range(2):
                tile_done(dve, U_OUT, 2 * t, 4, i)
                v.tensor_copy(halves(mix[:, bass.ds(2 * i + t, 1), :].rearrange("p a n -> p (a n)")),
                              tile_out(2 * t)).then_inc(m_copied[t], 1)
                dve.wait_ge(m_sq[t], i + 1)
                dve.wait_ge(m_acc, 2 * i + t)
                v.tensor_tensor(acc[:], acc[:], sqt[:, t, :], ALU.add).then_inc(m_acc, 1)
        dve.wait_ge(sq_root, 2)
        v.reciprocal(R[:], R[:]).then_inc(R_ready, 1)
        dve.wait_ge(R_ready, 2)
        v.memset(acc[:], 0.0).then_inc(acc_zero, 1)
        dve.wait_ge(acc_zero, 2)
        dve.wait_ge(m_copied[0], KD // 2)
        dve.wait_ge(m_copied[1], KD // 2)
        for q in range(4):
            dve.wait_ge(r_landed[q], 16)
            with dve.Fori(0, 2) as i:
                for t in range(2):
                    k = 4 * q + 2 * i + t
                    mk = mix[:, bass.ds(k, 1), :].rearrange("p a n -> p (a n)")
                    v.tensor_tensor(mk, mk, R[:], ALU.mult).then_inc(h_tmp, 1)
                    dve.wait_ge(h_tmp, k + 1)
                    v.scalar_tensor_tensor(out=mk, in0=mk, scalar=cs[:, bass.ds(C_POST + k, 1)],
                                           in1=xres[:, bass.ds(k, 1), :].rearrange("p a n -> p (a n)"),
                                           op0=ALU.mult, op1=ALU.add).then_inc(h_done, 1)
                    dve.wait_ge(h_done, k + 1)
                    dve.wait_ge(h_hi, k + 1)
                    v.scalar_tensor_tensor(out=xl[:, bass.ds(k, 1), :].rearrange("p a n -> p (a n)"),
                                           in0=mk, scalar=cs[:, bass.ds(C_FFN + k, 1)],
                                           in1=xh[:, bass.ds(k, 1), :].rearrange("p a n -> p (a n)").bitcast(F32),
                                           op0=ALU.mult, op1=ALU.subtract).then_inc(h_lo, 1)
                    dve.wait_ge(h_sq, k + 1)
                    dve.wait_ge(h_acc, k)
                    v.tensor_tensor(acc[:], acc[:], sqt[:, t, :], ALU.add).then_inc(h_acc, 1)
        dve.wait_ge(sq_root, 3)
        v.reciprocal(R[:], R[:]).then_inc(R_ready, 1)
        dve.wait_ge(R_ready, 3)
        dve.wait_ge(h_stored, 64)
        for t in range(2):
            v.memset(ub[t][:, 0:2], 0.0).then_inc(ub_zero, 1)
        dve.wait_ge(ub_zero, 2)

        def evac_up(t, n, base, c, per, i):
            tile_done(dve, base, c + 2 * t, per, i)
            dve.wait_ge(cv_done, 2 * n)
            dve.wait_ge(hist_cp, 2 * n)
            lo_, hi_ = pb[:, 2 * t, 0:TH], pb[:, 2 * t + 1, 0:TH]
            v.tensor_tensor(ub[t][:, 2:2 + TH], lo_, R[:, 0:TH], ALU.mult)
            v.tensor_tensor(ub[t][:, 2 + TH:2 + SEQ], hi_[:, 0:SEQ - TH], R[:, TH:SEQ], ALU.mult)
            v.tensor_tensor(ub[t][:, 2 + SEQ:UB].rearrange("p (b n) -> p b n", b=DB)[:, :, 2:2 + DT],
                            hi_[:, SEQ - TH:TH].rearrange("p (b n) -> p b n", b=DB),
                            R[:, SEQ:T].rearrange("p (b n) -> p b n", b=DB), ALU.mult).then_inc(up_evac[t], 1)

        def conv(p, t, n):
            f = p + KF * t
            dve.wait_ge(tap, 2 * n + t + 1)
            v.scalar_tensor_tensor(out=cv[t][:, 0:NC_], in0=ub[t][:, 1:UB - 1],
                                   scalar=cs[:, bass.ds(C_W + 2 * KF + f, 1)],
                                   in1=cv[t][:, 0:NC_], op0=ALU.mult, op1=ALU.add).then_inc(tap1, 1)
            dve.wait_ge(tap1, 2 * n + t + 1)
            v.scalar_tensor_tensor(out=cv[t][:, 0:NC_], in0=ub[t][:, 0:NC_],
                                   scalar=cs[:, bass.ds(C_W + f, 1)],
                                   in1=cv[t][:, 0:NC_], op0=ALU.mult, op1=ALU.add).then_inc(cv_done, 1)

        def smp_cols(ap):
            return ap[:, SEQ:SEQ + DB * 10].rearrange("p (b n) -> p b n", b=DB)[:, :, 2:2 + DT]

        def pair_dve(p, n, base, c, per=0, i=0):
            for t in range(2):
                evac_up(t, n, base, c, per, i)
                conv(p, t, n)
            dve.wait_ge(gelu_done, n + 1)
            dve.wait_ge(cv_done, 2 * n + 2)
            dve.wait_ge(g_lo, n)
            v.tensor_tensor(gv[:, 0:SEQ], cv[0][:, 0:SEQ], cv[1][:, 0:SEQ], ALU.mult)
            v.tensor_tensor(gv[:, SEQ:T].rearrange("p (b n) -> p b n", b=DB), smp_cols(cv[0]), smp_cols(cv[1]),
                            ALU.mult).then_inc(gv_done, 1)

        def down_dve(r, base, c, per=0, i=0):
            for m in range(KD):
                if m % 2:
                    dve.wait_ge(w_used, base + c + m // 2 + 1 + (per * i if per else 0))
                else:
                    dve.wait_ge(dn_even, KD // 2 * r + m // 2 + 1)
                ym = halves(y[:, m, :])
                v.tensor_tensor(ym, ym, tile_out(4 + 2 * (m % 2)), ALU.add).then_inc(dn_done, 1)

        pair_dve(0, 0, U_FFN, 0)
        dve.wait_ge(y_zero, 1)
        with dve.Fori(0, ROUNDS - 1) as i:
            for t in range(4):
                pair_dve(GRP * i + 1 + t, GRP * i + 1 + t, U_FFN + 4, 4 * t, 24, i)
            dve.wait_ge(dn_done, KD * i)
            down_dve(i, U_FFN + 4, 16, 24, i)
        for t in range(3):
            pair_dve(KF - 3 + t, KF - 3 + t, UNITS - 20, 4 * t)
        dve.wait_ge(dn_done, KD * (ROUNDS - 1))
        down_dve(ROUNDS - 1, UNITS - 20, 12)
        dve.wait_ge(w_used, UNITS - 8)
        v.memset(accl[:], 0.0).then_inc(acc_zero, 1)
        dve.wait_ge(acc_zero, 3)
        with dve.Fori(0, KD // 2) as i:
            for t in range(2):
                dve.wait_ge(y_sq, 2 * i + t + 1)
                dve.wait_ge(y_acc, 2 * i + t)
                v.tensor_tensor(accl[:], accl[:], sql[:, t, :], ALU.add).then_inc(y_acc, 1)
        dve.wait_ge(sq_root, 4)
        v.reciprocal(R[:], R[:]).then_inc(R_ready, 1)
        dve.wait_ge(R_ready, 4)
        for q in range(4):
            dve.wait_ge(hr_landed[q], 16)
            with dve.Fori(0, 4) as i:
                k = 4 * q + i
                yk = y[:, bass.ds(k, 1), :].rearrange("p a n -> p (a n)")
                v.tensor_tensor(yk, yk, R[:], ALU.mult).then_inc(y_tmp, 1)
                dve.wait_ge(y_tmp, k + 1)
                v.scalar_tensor_tensor(out=yk, in0=yk, scalar=cs[:, bass.ds(C_LAST + k, 1)],
                                       in1=hres[:, bass.ds(k, 1), :].rearrange("p a n -> p (a n)"),
                                       op0=ALU.mult, op1=ALU.add).then_inc(y_done, 1)

    @block.tensor
    def _(pe):
        pe.wait_ge(ready, 2)
        for k in range(KD):
            pe.wait_ge(x_sq, k + 1)
            for n in range(2):
                m = te.matmul(pb[:, 6 + n, 0:TH], ones[:], sq0[:, k % 2, n * TH:(n + 1) * TH],
                              start=(k == 0), stop=(k == KD - 1))
            m.then_inc(x_ssq_mm, 1)
        with pe.Fori(0, H) as j:
            pe.wait_ge(q_evac, j)
            tile_mm(0, U_QK, 0, 4, j, x_lo)
            pe.wait_ge(k_evac, j)
            tile_mm(2, U_QK, 2, 4, j)
        pe.wait_ge(q_evac, H)
        pe.wait_ge(k_evac, H)
        pe.wait_ge(sq_root, 1)
        with pe.Fori(0, H // 2) as i:
            pe.wait_ge(v_evac, 2 * i)
            for t in range(2):
                tile_mm(2 * t, U_V, 2 * t, 4, i)
            for t in range(2):
                pe.wait_ge(v_evac, 2 * i + t + 1)
                pe.wait_ge(vt_evac, 2 * i)
                for b4 in range(4):
                    te.transpose(pb[:, 4 + t, b4 * P:(b4 + 1) * P], zt[t][:, b4 * P:(b4 + 1) * P], ident[:])
                te.transpose(pb[0:NS, 6 + t, 0:P], zt[t][:, SEQ:T], ident[:]).then_inc(vT_ready, 1)
        pe.wait_ge(v_evac, H)
        pe.wait_ge(vt_evac, H)

        with pe.Fori(0, DB) as j:
            def st_turn(g_):
                pe.wait_ge(s["st_copied"], 4 * j + g_ + 1)
                if g_ == 0:
                    pe.wait_ge(s["ssq_ready"], j)
                else:
                    pe.wait_ge(s["mx_part"], 4 * j + g_)
                for i in range(4):
                    m = te.transpose(pb[:, 4, i * P:(i + 1) * P], ET[:, 4 * g_ + i, :], ident[:])
                m.then_inc(s["stT_ready"], 1)

            pe.wait_ge(sq_landed, 32 * j + 32)
            for g_ in range(4):
                n = (g_ + 1) * P
                pe.wait_ge(s["st_copied"], 4 * j + g_)
                if g_ == 0:
                    pe.wait_ge(s["vtok_copied"], 2 * j)
                for i in range(4):
                    page = 4 * g_ + i
                    slot = page % PSLOTS
                    pe.wait_ge(pg_landed[slot], 64 * j + 16 * (page // PSLOTS) + 16)
                    for h in range(H):
                        m = te.matmul(pb[:, 2, i * P + 16 * h:i * P + 16 * h + 16], pg[:, slot, h * P:(h + 1) * P],
                                      qb[:, h, :], start=True, stop=True)
                    m.then_inc(pg_used[slot], 1)
                if g_ == 0:
                    pe.wait_ge(hq_landed, 32 * j + 32)
                    pe.wait_ge(s["a_done"], j)
                    pe.wait_ge(s["po_copied"], j)
                pe.wait_ge(s["pexp_done"], 8 * j + 2 * g_)
                te.matmul(pb[:, 6, 0:n], qT[0:DH, g_ * P:n], kT[0:DH, 0:n], start=True, stop=True)
                te.matmul(pb[:, 7, 0:n], qT[DH:P, g_ * P:n], kT[DH:P, 0:n], start=True, stop=True
                          ).then_inc(s["pscore_ready"], 1)
                if g_ >= 1:
                    st_turn(g_ - 1)
            pe.wait_ge(s["ssd_done"], j)
            for h in range(H):
                m = te.matmul(pb[0:DT, 5, 16 * h:16 * h + 16], knew[:, h, :], qb[:, h, :], start=True, stop=True)
            m.then_inc(s["snew_ready"], 1)
            st_turn(3)
            pe.wait_ge(s["psd_done"], j)
            unit_mm(0, U_HEADS, 0, xh, xl, 0, 8, True, False, per=4, j=j).then_inc(w_used, 1)

            def w_turn(g_):
                o = g_ * (g_ + 1) // 2 * P
                pe.wait_ge(s["pw_done"], 4 * j + g_ + 1)
                pe.wait_ge(s["pexp_done"], 8 * j + 8)
                if g_ >= 2:
                    pe.wait_ge(s["wT_copied"], 4 * j + g_ - 1)
                for kb in range(g_ + 1):
                    m = te.transpose(pb[:, 6 + g_ % 2, kb * P:(kb + 1) * P], W[:, o + kb * P:o + (kb + 1) * P],
                                     ident[:])
                m.then_inc(s["wT_ready"], 1)

            pe.wait_ge(s["scn_ready"], j + 1)
            w_turn(0)
            te.transpose(pb[:, 5, P:P + DT], SCn[:], ident[0:DT, 0:DT]).then_inc(s["snT_ready"], 1)
            w_turn(1)
            pe.wait_ge(s["mx_ready"], j + 1)
            te.matmul(pb[:, 5, 2 * P:3 * P], mx[:, 0:1].to_broadcast([P, P]), ident[:], start=True, stop=True
                      ).then_inc(s["mb_ready"], 1)
            unit_mm(0, U_HEADS, 1, xh, xl, 8, 8, False, True, per=4, j=j).then_inc(w_used, 1)
            w_turn(2)
            w_turn(3)
            pe.wait_ge(s["u_evac"], j + 1)
            tile_mm(0, U_HEADS, 2, 4, j)

            def v_pages(a0, z0):
                for page in range(a0, z0):
                    slot = page % PSLOTS
                    pe.wait_ge(pg_landed[slot], 64 * j + 16 * (2 + page // PSLOTS) + 16)
                    pe.wait_ge(s["eexp"], 5 * j + page // 4 + 1)
                    for h in range(H):
                        m = te.matmul(pb[:, 4, 16 * h:16 * h + 16], pg[:, slot, h * P:(h + 1) * P],
                                      ET[:, page, 16 * h:16 * h + 16], start=(page == 0 and h == 0), stop=False,
                                      skip_group_check=True)
                    m.then_inc(pg_used[slot], 1)

            pe.wait_ge(s["mx_part"], 4 * j + 4)
            v_pages(0, 8)
            pe.wait_ge(s["esum_ready"], j + 1)
            te.matmul(pb[:, 5, 0:P], ones[:], esum[:], start=True, stop=False)
            te.matmul(pb[:, 5, 0:P], ones[0:DT, :], SCn[:], start=False, stop=True).then_inc(s["sums_ready"], 1)
            pe.wait_ge(s["vsq_ready"], j + 1)
            pe.wait_ge(s["a_done"], j)
            for n in range(2):
                m = te.matmul(pb[:, 2 + n, 0:TH], ones[:], vq[:, n * TH:(n + 1) * TH], start=True, stop=True)
            m.then_inc(s["vssq_ready"], 1)
            v_pages(8, 12)
            pe.wait_ge(s["va_norm"], j + 1)
            pe.wait_ge(s["vsd_done"], j + 1)
            for b4 in range(4):
                te.transpose(pb[:, 2, b4 * P:(b4 + 1) * P], vaT[:, b4 * P:(b4 + 1) * P], ident[:])
            te.transpose(pb[0:NS, 3, 0:P], vaT[:, SEQ:T], ident[:]).then_inc(s["vaT_ready"], 1)
            v_pages(12, 16)
            pe.wait_ge(sv_landed, 16 * j + 16)
            pe.wait_ge(s["eexp"], 5 * j + 5)
            for h in range(H):
                m = te.matmul(pb[:, 4, 16 * h:16 * h + 16], vnew[:, h * P:(h + 1) * P],
                              SCn[:, 16 * h:16 * h + 16], start=False, stop=(h == H - 1), skip_group_check=True)
            m.then_inc(s["spv_ready"], 1)
            pe.wait_ge(s["wT_copied"], 4 * j + 4)
            pe.wait_ge(hv_landed, 16 * j + 16)
            for g_ in range(4):
                o = g_ * (g_ + 1) // 2 * P
                for kb in range(g_ + 1):
                    m = te.matmul(pb[:, 7, g_ * P:(g_ + 1) * P], V[:, kb, :], wT[:, o + kb * P:o + (kb + 1) * P],
                                  start=(kb == 0), stop=(kb == g_))
            m.then_inc(s["pv_ready"], 1)
            pe.wait_ge(s["vtok_copied"], 2 * j + 2)
            pe.wait_ge(s["ws_masked"], 2 * j + 2)
            for b4 in range(4):
                te.matmul(pb[:, 6, b4 * P:(b4 + 1) * P], vtok[:, b4, :], ws[:], start=True, stop=True)
            te.matmul(pb[:, 3, P:P + NS], vtok[0:NS, 4, :], wb[:], start=True, stop=True
                      ).then_inc(s["gm_ready"], 1)
            pe.wait_ge(s["ssq_ready"], j + 1)
            te.matmul(pb[:, 5, 384:384 + NS], ones[:], osq[:], start=True, stop=True).then_inc(s["sss_ready"], 1)
            pe.wait_ge(s["posq"], j + 1)
            pe.wait_ge(s["va_evac"], j + 1)
            te.matmul(pb[:, 0, :], ones[:], E2[:], start=True, stop=True).then_inc(s["pss_ready"], 1)

        pe.wait_ge(s["psd_done"], DB)
        pe.wait_ge(s["a_done"], DB)
        with pe.Fori(0, KD // 2) as i:
            for t in range(2):
                pe.wait_ge(m_copied[t], i)
                tile_mm(2 * t, U_OUT, 2 * t, 4, i, m_lo if t == 0 else None)

        def sum_squares(a, bank):
            for n in range(2):
                m = te.matmul(pb[:, bank + n, 0:TH], ones[:], a[:, n * TH:(n + 1) * TH], start=True, stop=True)
            m.then_inc(ssq_mm, 1)

        pe.wait_ge(m_acc, KD)
        pe.wait_ge(s["ssd_done"], DB)
        sum_squares(acc, 4)
        pe.wait_ge(h_acc, KD)
        sum_squares(acc, 6)
        pe.wait_ge(m_copied[0], KD // 2)
        pe.wait_ge(m_copied[1], KD // 2)

        def pair_pe(n, base, c, per=0, i=0, k_sem=None):
            for t in range(2):
                pe.wait_ge(up_evac[t], n)
                tile_mm(2 * t, base, c + 2 * t, per, i, k_sem)

        def down_pe(r, base, c, per=0, i=0):
            pe.wait_ge(g_lo, GRP * r + GRP)
            for mm in range(KD // 2):
                for a in range(2):
                    m = 2 * mm + a
                    pe.wait_ge(dn_done, KD * r + (m - 1 if m >= 2 else 0))
                    ins = unit_mm(4 + 2 * a, base, c + mm, gh, gl, 0, GRP, True, True, col=a * GRP * P,
                                  per=per, j=i)
                    ins.then_inc(w_used if a else dn_even, 1)

        pair_pe(0, U_FFN, 0, k_sem=h_lo)
        pe.wait_ge(sq_root, 3)
        with pe.Fori(0, ROUNDS - 1) as i:
            for t in range(4):
                pair_pe(GRP * i + 1 + t, U_FFN + 4, 4 * t, 24, i)
            down_pe(i, U_FFN + 4, 16, 24, i)
        for t in range(3):
            pair_pe(KF - 3 + t, UNITS - 20, 4 * t)
        down_pe(ROUNDS - 1, UNITS - 20, 12)
        pe.wait_ge(y_acc, KD)
        pe.wait_ge(up_evac[0], KF)
        sum_squares(accl, 0)

    block.__exit__(None, None, None)


_OUTS = [((P, KD, T), "y"), ((H, P, T), "k"), ((H, 4, P, P), "v"), ((NS, H, P), "vs"), ((H, P, NS), "va"),
         ((P, 2 * KF, 18), "hist")]


def _tiles(w):
    return w.reshape(w.shape[0] // P, P, w.shape[1] // P, P).transpose(2, 0, 1, 3)


def _units(tiles):
    n = tiles.shape[0]
    return tiles.reshape(n, 2, 8, P, P).transpose(0, 1, 3, 2, 4).reshape(2 * n, P, UNIT)


def _weights(w_in, w_out, w_up, w_down):
    w = _tiles(w_in)
    parts = [_units(w[[o + h for h in range(H) for o in (16, 24)]]), _units(w[32:40]),
             _units(w[[o + h for h in range(H) for o in (0, 8)]]), _units(_tiles(w_out))]
    up = _tiles(w_up)
    pairs = [_units(up[[p, KF + p]]) for p in range(KF)]
    dn = _tiles(w_down).reshape(KD // 2, 2, ROUNDS, GRP, P, P).transpose(2, 0, 4, 1, 3, 5)
    dn = dn.reshape(ROUNDS, KD // 2, P, UNIT)
    parts.append(pairs[0])
    for r in range(ROUNDS - 1):
        parts += pairs[GRP * r + 1:GRP * r + 5] + [dn[r]]
    parts += pairs[KF - 3:] + [dn[ROUNDS - 1]]
    return np.concatenate(parts).reshape(UNITS * P, UNIT)


def _feature_major(prompt, sample):
    x = np.concatenate([prompt, sample]).T
    return x.reshape(x.shape[0] // P, P, T).transpose(1, 0, 2)


def kernel(**inputs):
    import concourse.bacc as _bacc
    from concourse.bass_utils import run_bass_kernel_spmd as _run

    i = {k: np.asarray(a) for k, a in inputs.items()}
    col = lambda a: a.reshape(-1, P).T
    wb = np.zeros((H, DB, DT, DB, DT), np.float32)
    wst = i["w_s"][0].transpose(0, 2, 1)
    for b in range(DB):
        wb[:, b, :, b, :] = wst[:, 0:DT, 0:DT]
    lay = {
        "xT": _feature_major(i["x_prompt"][0], i["x_sample"].reshape(NS, D)),
        "wstream": _weights(i["w_in"][0], i["w_out"][0], i["w_up"][0], i["w_down"][0]),
        "kpages": i["cache_k"][0].transpose(0, 3, 2, 1).reshape(N_PHYS, P, H * P),
        "vpages": i["cache_v"][0].reshape(N_PHYS, P, H * P),
        "state": i["state_conv"][0].reshape(DB * 2, 2 * KF, P).transpose(2, 1, 0),
        "ptab": i["page_table"].reshape(1, DB * PAGES),
        "consts": np.concatenate([col(i["g_pre_mix"]), col(i["g_post_mix"]), col(i["g_pre_ffn"]),
                                  col(i["g_post_ffn"]), i["g_v_a"][0].T, col(i["g_subln"]), col(i["b_conv"]),
                                  col(i["w_conv"][0])], axis=1),
        "lams": np.stack([i[n][0] for n in ("lam_q1", "lam_k1", "lam_q2", "lam_k2")])[None],
        "wsT": wst,
        "wblk": wb.reshape(H, NS, NS),
        "bs": i["b_s"][0],
    }
    nc = _bacc.Bacc("TRN2", target_bir_lowering=False, num_devices=1)
    arrays, args = {}, []
    for name, x in lay.items():
        x = np.ascontiguousarray(x)
        arrays[f"in_{name}"] = x
        args.append(nc.dram_tensor(f"in_{name}", x.shape, mybir.dt.from_np(x.dtype), kind="ExternalInput").ap())
    for shape, name in _OUTS:
        args.append(nc.dram_tensor(f"out_{name}", shape, F32, kind="ExternalOutput").ap())
    build(nc, *args)
    r = _run(nc, [arrays], core_ids=[0]).results[0]
    y, k, v, vs, va, hist = (r[f"out_{name}"] for _, name in _OUTS)
    y = y.transpose(2, 1, 0).reshape(T, D)
    k = k.transpose(2, 0, 1)
    v = v.transpose(1, 2, 0, 3).reshape(SEQ, H, HD)
    hist = hist.transpose(2, 1, 0).reshape(18, 2 * FF)
    out = (y[:SEQ].reshape(1, SEQ, D), y[SEQ:].reshape(DB, DT, D),
           k[:SEQ].reshape(1, 1, SEQ, H, HD), v.reshape(1, 1, SEQ, H, HD), hist[:2].reshape(1, 1, 2, 2 * FF),
           k[SEQ:].reshape(1, DB, DT, H, HD), vs.reshape(1, DB, DT, H, HD), hist[2:].reshape(1, DB, 2, 2 * FF),
           va.transpose(2, 0, 1).reshape(1, DB, DT, H, HD))
    return tuple(np.ascontiguousarray(a) for a in out)
```

```python
import numpy as np

import concourse.bass as bass
from concourse import mybir

P = 128
ALU = mybir.AluOpType
ACT = mybir.ActivationFunctionType
AX = mybir.AxisListType
F32 = mybir.dt.float32
F32R = mybir.dt.float32r
I32 = mybir.dt.int32

D = 2048
SEQ = 512
DB, DT = 8, 8
NS = DB * DT
T = SEQ + NS
TH = T // 2
KD = D // P
H = 8
HD = 128
DH = HD // 2
PAGES = 16
N_PHYS = 160
FF = 5632
KF = FF // P
GRP = 4
ROUNDS = KF // GRP
EPS = 1e-6
SCALE = DH ** -0.5
LAM_INIT = 0.8 - 0.6
NEG = -1.0e30

UNIT = 1024
RAW = 2
HL = 4
U_QK, U_V, U_HEADS, U_OUT, U_FFN = 0, 32, 48, 80, 112
UNITS = U_FFN + 2 * 2 * KF + KF * KD // 8
PSLOTS = 8
C_PRE, C_POST, C_FFN, C_LAST = 0, 16, 32, 48
C_VA, C_SUB, C_B, C_W = 64, 72, 73, 73 + 2 * KF
C_MASK = C_W + 3 * 2 * KF
C_SEL = C_MASK + DT
C_ALL = C_SEL + 2
UB = 2 + SEQ + DB * (2 + DT)
NC_ = UB - 2


class Chain:

    def __init__(self, eng, sem, base, per=0, j=0):
        self.eng, self.sem, self.base, self.per, self.j, self.c = eng, sem, base, per, j, 0

    def link(self, ins):
        self.c += 1
        ins.then_inc(self.sem, 1)
        self.eng.wait_ge(self.sem, self.base + self.c + (self.per * self.j if self.per else 0))

    def close(self, n):
        assert self.c == n, (self.c, n)


def build(nc, xT, wstream, kpages, vpages, state, ptab, consts, lams, wsT, wblk, bs,
          y_out, k_out, v_out, vs_out, va_out, hist_out):
    zq_d = nc.dram_tensor("zq_d", (H, P, T), F32, kind="Internal").ap()
    qs_d = nc.dram_tensor("qs_d", (P, DB, H * 32), F32, kind="Internal").ap()
    ks_d = nc.dram_tensor("ks_d", (P, DB, H * DT), F32, kind="Internal").ap()
    mix_d = nc.dram_tensor("mix_d", (P, KD, T), F32, kind="Internal").ap()
    h_d = nc.dram_tensor("h_d", (P, KD, T), F32, kind="Internal").ap()

    top = [16512]

    def sb(name, shape, dt=F32, at=None):
        size = int(np.prod(shape[1:])) * 4
        size = (size + 31) // 32 * 32
        if at is None:
            off = top[0]
            top[0] += size
        else:
            off = at[0]
            at[0] += size
            at[1] = max(at[1], at[0])
        return nc.alloc_sbuf_tensor_at(name, shape, dt, offset=off)

    xh_at = top[0]
    xh = sb("xh", [P, KD, T], F32R)
    xl = sb("xl", [P, KD, T], F32R)
    wraw = sb("wraw", [P, RAW, UNIT])
    wh = sb("wh", [P, HL, UNIT], F32R)
    wl = sb("wl", [P, HL, UNIT], F32R)
    cs = sb("cs", [P, C_ALL])
    ident = sb("ident", [P, P])
    ones = sb("ones", [P, P])
    R = sb("R", [P, T])
    neglam = sb("neglam", [P, 1])
    gsub = sb("gsub", [P, 1])
    sgn = sb("sgn", [P, 1])
    lt = sb("lt", [P, 4])
    ptab_sb = sb("ptab_sb", [1, DB * PAGES], I32)
    free0 = top[0]

    a = [free0, 0]
    xraw = sb("xraw", [P, KD, T], at=a)
    lamin = sb("lamin", [P, 4, DH], at=a)
    sq0 = sb("sq0", [P, 2, T], at=a)
    b = [a[0], a[0]]
    zt = [sb(f"zt{i}", [P, T], at=b) for i in range(2)]
    vt = [sb(f"vt{i}", [P, 5, P], at=b) for i in range(2)]
    qbd = sb("qbd", [P, DB, H, 32], at=b)
    kns = sb("kns", [P, DB, H, DT], at=b)

    c = [free0, 0]
    pg = sb("pg", [P, PSLOTS, H * P], at=c)
    S = sb("S", [P, PAGES * P + DT], at=c)
    En = sb("En", [DT, P], at=c)
    W = sb("W", [P, 1280], at=c)
    E2 = sb("E2", [P, SEQ], at=c)
    wT = sb("wT", [P, 1280], at=c)
    qT = sb("qT", [P, SEQ], at=c)
    kT = sb("kT", [P, SEQ], at=c)
    V = sb("V", [P, 4, P], at=c)
    vnew = sb("vnew", [DT, H * P], at=c)
    ws = sb("ws", [P, P], at=c)
    wb = sb("wb", [NS, NS], at=c)
    bsb = sb("bsb", [P, P], at=c)
    vg = sb("vg", [P, T], at=c)
    vq = sb("vq", [P, T], at=c)
    vaT = sb("vaT", [P, T], at=c)
    ug = sb("ug", [P, T], at=c)
    ao = sb("ao", [P, T], at=c)
    po = sb("po", [P, SEQ], at=c)
    vtok = sb("vtok", [P, 5, P], at=c)
    bsmp = sb("bsmp", [P, H, NS], at=c)
    qb = sb("qb", [P, H, 32], at=c)
    knew = sb("knew", [P, H, DT], at=c)
    osb = sb("osb", [P, 2 * P], at=c)
    oT = sb("oT", [P, 2 * P], at=c)
    osm = sb("osm", [P, NS], at=c)
    osq = sb("osq", [P, NS], at=c)
    pmx = sb("pmx", [P, 2], at=c)
    pneg = sb("pneg", [P, 2], at=c)
    psm = sb("psm", [P, 8], at=c)
    prs = sb("prs", [P, 2], at=c)
    mx4 = sb("mx4", [P, 5], at=c)
    mx = sb("mx", [P, 1], at=c)
    nmx = sb("nmx", [P, 1], at=c)
    ssm = sb("ssm", [P, 5], at=c)
    rs = sb("rs", [P, 2], at=c)
    maskd = sb("maskd", [P, P], at=c)

    d = [free0, 0]
    area1 = d[0]
    mixf = sb("mixf", [P, KD, T], at=d)
    area2 = d[0]
    mix = sb("mix", [P, KD, T], at=d)
    sqt = sb("sqt", [P, 2, T], at=d)
    acc = sb("acc", [P, T], at=d)
    e = [area1, 0]
    xres = sb("xres", [P, KD, T], at=e)
    y = nc.alloc_sbuf_tensor_at("y", [P, KD, T], F32, offset=area1)
    f = [area2, 0]
    gh = sb("gh", [P, GRP, T], F32R, at=f)
    gl = sb("gl", [P, GRP, T], F32R, at=f)
    ub = [sb(f"ub{i}", [P, UB], at=f) for i in range(2)]
    cv = [sb(f"cv{i}", [P, UB], at=f) for i in range(2)]
    gv = sb("gv", [P, T], at=f)
    st = sb("st", [P, 2 * KF, 16], at=f)
    hs = sb("hs", [P, 2 * KF, 18], at=f)
    hres = nc.alloc_sbuf_tensor_at("hres", [P, KD, T], F32, offset=xh_at)
    g = [xh_at + KD * T * 4, 0]
    sql = sb("sql", [P, 2, T], at=g)
    accl = sb("accl", [P, T], at=g)
    for z in (a, b, c, d, e, f):
        assert z[1] <= 229344, z

    pb = nc.alloc_psum_tensor("pb", [P, 8, 512], F32)


    def sem(name):
        return nc.alloc_semaphore(name)

    w_landed = [sem(f"w_landed{i}") for i in range(RAW)]
    w_hi, w_lo, w_used = sem("w_hi"), sem("w_lo"), sem("w_used")
    c_landed, p_landed, ready = sem("c_landed"), sem("p_landed"), sem("consts_ready")
    x_landed = [sem(f"x_landed{i}") for i in range(4)]
    x_sq, x_hi, x_lo, x_ssq_mm = sem("x_sq"), sem("x_hi"), sem("x_lo"), sem("x_sq_used")
    sq_root, R_ready = sem("sq_root"), sem("R_ready")
    dve_c, pool_c, lam_sum, lam_exp = sem("dve_chain"), sem("pool_chain"), sem("lam_sum"), sem("lam_exp")
    q_evac, k_evac, smp = sem("q_evac"), sem("k_evac"), sem("sample_cols")
    q_stored, k_stored, s_stored = sem("q_stored"), sem("k_stored"), sem("sample_stored")
    v_evac, vT_ready, vt_evac = sem("v_evac"), sem("vT_ready"), sem("vt_evac")
    v_stored = [sem("v_stored0"), sem("v_stored1")]
    pg_landed = [sem(f"pages_landed{i}") for i in range(2)]
    pg_used = [sem(f"pages_used{i}") for i in range(2)]
    hq_landed, sq_landed, hv_landed, sv_landed, g_landed = (sem(x) for x in (
        "head_qk_landed", "sample_q_landed", "head_v_landed", "sample_v_landed", "gmlp_landed"))
    names_h = ("st_copied s_max pscore_ready pexp_done pneg_ready pw_done snew_ready snew_masked nmx_ready "
               "sexp sT_ready sT_copied wT_ready wT_copied u_evac ugelu va_evac vgelu vsq_ready vssq_ready "
               "vsd_done va_norm vaT_ready vtok_copied ws_masked spv_ready osb_ready oT_ready pv_ready po_copied "
               "posq pss_ready psd_done ssq_ready sss_ready ssd_done gm_ready ao_prompt a_done b_done bs_done "
               "va_stored a_stored b_stored bs_stored").split()
    s = {n: sem(n) for n in names_h}
    m_landed = [sem(f"mix_landed{i}") for i in range(4)]
    m_hi, m_lo, m_acc, acc_zero = (sem(x) for x in (
        "mix_hi", "mix_lo", "out_acc", "acc_zero"))
    m_copied = [sem(f"out_copied{t}") for t in range(2)]
    m_sq = [sem(f"out_sq{t}") for t in range(2)]
    r_landed = [sem(f"res_landed{i}") for i in range(4)]
    h_tmp, h_done, h_hi, h_lo, h_sq, h_acc, h_stored = (sem(x) for x in (
        "h_scaled", "h_done", "h_hi", "h_lo", "h_sq", "h_acc", "h_stored"))
    st_landed, st_in, hist_cp, tap, tap1, cv_done, gelu_done, gv_done, g_hi, g_lo = (sem(x) for x in (
        "state_landed", "state_in", "hist_out", "tap2_done", "tap1_done", "conv_done",
        "gelu_done", "gv_done", "g_hi", "g_lo"))
    up_evac = [sem("gate_evac"), sem("value_evac")]
    ub_zero = sem("prompt_history_zero")
    dn_even, dn_done, hist_stored, y_zero = sem("down_even_ready"), sem("down_added"), sem("hist_stored"), sem("y_zero")
    hr_landed = [sem(f"hr_landed{i}") for i in range(4)]
    y_sq, y_tmp, y_acc, y_done, y_stored, ssq_mm = sem("y_sq"), sem("y_scaled"), sem("y_acc"), sem("y_done"), sem("y_stored"), sem("ssq_mm")

    v, sc, pl, te, sy = nc.vector, nc.scalar, nc.gpsimd, nc.tensor, nc.sync

    def halves(ap):
        return ap.rearrange("p (c n) -> p c n", c=2)

    def w_load(base, c, per=0, j=0):
        u = base + c
        sy.wait_ge(w_lo, u + 5 + (per * j if per else 0))
        off = (u + 6) * P + (per * P * j if per else 0)
        sy.dma_start(wraw[:, c % RAW, :], wstream[bass.ds(off, P), :]).then_inc(w_landed[c % RAW], 16)

    def w_split_hi(base, c, per=0, j=0):
        u = base + c
        sc.wait_ge(w_landed[c % RAW], 16 * ((u + 4) // RAW + 1) + (16 * (per // RAW) * j if per else 0))
        sc.wait_ge(w_used, u + 1 + (per * j if per else 0))
        sc.activation(wh[:, c % HL, :], wraw[:, c % RAW, :], ACT.Copy).then_inc(w_hi, 1)

    def w_split_lo(base, c, per=0, j=0):
        pl.wait_ge(w_hi, base + c + 5 + (per * j if per else 0))
        pl.tensor_tensor(wl[:, c % HL, :], wraw[:, c % RAW, :], wh[:, c % HL, :].bitcast(F32),
                         ALU.subtract).then_inc(w_lo, 1)

    def unit_mm(bank, base, c, hi, lo, k0, nk, first, last, col=0, per=0, j=0, k_sem=None):
        te.wait_ge(w_lo, base + c + 1 + (per * j if per else 0))
        slot = c % HL
        for kt in range(nk):
            if k_sem is not None:
                te.wait_ge(k_sem, k0 + kt + 1)
            whk = wh[:, slot, col + kt * P:col + (kt + 1) * P]
            wlk = wl[:, slot, col + kt * P:col + (kt + 1) * P]
            a0, z0 = first and kt == 0, last and kt == nk - 1
            for n in range(2):
                te.matmul(pb[:, bank + n, 0:TH], whk, hi[:, k0 + kt, n * TH:(n + 1) * TH], start=a0, stop=False)
            for n in range(2):
                te.matmul(pb[:, bank + n, 0:TH], whk, lo[:, k0 + kt, n * TH:(n + 1) * TH], start=False, stop=False)
            for n in range(2):
                m = te.matmul(pb[:, bank + n, 0:TH], wlk, hi[:, k0 + kt, n * TH:(n + 1) * TH],
                              start=False, stop=z0)
        return m

    def tile_mm(bank, base, c, per=0, j=0, k_sem=None):
        unit_mm(bank, base, c, xh, xl, 0, 8, True, False, per=per, j=j, k_sem=k_sem).then_inc(w_used, 1)
        unit_mm(bank, base, c + 1, xh, xl, 8, 8, False, True, per=per, j=j, k_sem=k_sem).then_inc(w_used, 1)

    def tile_done(eng, base, c, per=0, j=0):
        eng.wait_ge(w_used, base + c + 2 + (per * j if per else 0))

    def tile_out(bank):
        return pb[:, bank:bank + 2, 0:TH]

    block = nc.Block().__enter__()

    @block.sync
    def _(sp):
        sp.dma_start(cs[:], consts).then_inc(c_landed, 16)
        sp.dma_start(lamin[:], lams.to_broadcast([P, 4, DH])).then_inc(c_landed, 16)
        for q in range(4):
            sp.dma_start(xraw[:, 4 * q:4 * q + 4, :], xT[:, 4 * q:4 * q + 4, :]).then_inc(x_landed[q], 16)
            if q < RAW:
                sp.dma_start(wraw[:, q, :], wstream[q * P:(q + 1) * P, :]).then_inc(w_landed[q], 16)
        for u in range(RAW, 6):
            sp.wait_ge(w_lo, u - RAW + 1)
            sp.dma_start(wraw[:, u % RAW, :], wstream[u * P:(u + 1) * P, :]).then_inc(w_landed[u % RAW], 16)

        with sp.Fori(0, H) as j:
            w_load(U_QK, 0, 4, j)
            w_load(U_QK, 1, 4, j)
            sp.wait_ge(q_evac, j + 1)
            sp.dma_start(zq_d[bass.ds(j, 1)].rearrange("a p n -> (a p) n"), zt[0][:]).then_inc(q_stored, 16)
            w_load(U_QK, 2, 4, j)
            w_load(U_QK, 3, 4, j)
            sp.wait_ge(k_evac, j + 1)
            sp.dma_start(k_out[bass.ds(j, 1)].rearrange("a p n -> (a p) n"), zt[1][:]).then_inc(k_stored, 16)
        sp.wait_ge(smp, 3 * H)
        sp.dma_start(qs_d, qbd[:].rearrange("p b h n -> p b (h n)")).then_inc(s_stored, 16)
        sp.dma_start(ks_d, kns[:].rearrange("p b h n -> p b (h n)")).then_inc(s_stored, 16)
        with sp.Fori(0, H // 2) as i:
            for c in range(4):
                w_load(U_V, c, 4, i)
            for t in range(2):
                sp.wait_ge(vt_evac, 2 * i + t + 1)
                sp.dma_start(v_out[bass.ds(2 * i + t, 1)].rearrange("a b p n -> p (a b) n"),
                             vt[t][:, 0:4, :]).then_inc(v_stored[t], 16)
                sp.dma_start(vs_out[:, bass.ds(2 * i + t, 1), :].rearrange("p a n -> p (a n)"),
                             vt[t][0:NS, 4, :]).then_inc(v_stored[t], 16)
        sp.wait_ge(q_stored, 16 * H)
        sp.wait_ge(k_stored, 16 * H)
        sp.wait_ge(s_stored, 32)
        sp.wait_ge(v_stored[0], 16 * H)
        sp.wait_ge(v_stored[1], 16 * H)
        sp.wait_ge(p_landed, 16)
        with sp.Fori(0, DB) as j:
            sp.wait_ge(s["pscore_ready"], 4 * j)
            sp.dma_start(qT[:], zq_d[bass.ds(j, 1), :, 0:SEQ].rearrange("a p n -> (a p) n")).then_inc(hq_landed, 16)
            sp.dma_start(kT[:], k_out[bass.ds(j, 1), :, 0:SEQ].rearrange("a p n -> (a p) n")).then_inc(hq_landed, 16)
            sp.wait_ge(s["snew_ready"], j)
            sp.dma_start(qb[:].rearrange("p h n -> p (h n)"),
                         qs_d[:, bass.ds(j, 1), :].rearrange("p a n -> p (a n)")).then_inc(sq_landed, 16)
            sp.dma_start(knew[:].rearrange("p h n -> p (h n)"),
                         ks_d[:, bass.ds(j, 1), :].rearrange("p a n -> p (a n)")).then_inc(sq_landed, 16)

            def page(n, j=j):
                slot = n % PSLOTS
                phys = sp.value_load(ptab_sb[0:1, bass.ds(PAGES * j + n % PAGES, 1)], min_val=0, max_val=N_PHYS - 1)
                sp.wait_ge(pg_used[slot // 4], 4 * j + n // PSLOTS)
                src = kpages if n < PAGES else vpages
                sp.dma_start(pg[:, slot, :], src[bass.ds(phys, 1)].rearrange("a p n -> (a p) n")
                             ).then_inc(pg_landed[slot // 4], 16)

            for n in range(8):
                page(n)
            sp.wait_ge(s["gm_ready"], j)
            sp.wait_ge(s["a_done"], j)
            sp.dma_start(ws[:], wsT[bass.ds(j, 1)].rearrange("a p n -> (a p) n")).then_inc(g_landed, 16)
            sp.dma_start(wb[:], wblk[bass.ds(j, 1)].rearrange("a p n -> (a p) n")).then_inc(g_landed, 16)
            sp.dma_start(bsb[:], bs[bass.ds(j, 1), :].to_broadcast([P, P])).then_inc(g_landed, 16)
            sp.wait_ge(s["pv_ready"], j)
            sp.dma_start(V[:], v_out[bass.ds(j, 1)].rearrange("a b p n -> p (a b) n")).then_inc(hv_landed, 16)
            sp.wait_ge(s["spv_ready"], j)
            sp.dma_start(vnew[:], vs_out[bass.ds(DT * j, DT)].rearrange("t h n -> t (h n)")).then_inc(sv_landed, 16)
            for c in range(4):
                for n in range(8 + 4 * c, 12 + 4 * c):
                    page(n)
                w_load(U_HEADS, c, 4, j)
            for n in range(24, 32):
                page(n)

        sp.wait_ge(s["a_stored"], 16 * H)
        sp.wait_ge(s["va_stored"], 16 * H)
        for q in range(2):
            sp.dma_start(mixf[:, 4 * q:4 * q + 4, :], mix_d[:, 4 * q:4 * q + 4, :]).then_inc(m_landed[q], 16)
        sp.wait_ge(s["b_stored"], 16 * H)
        sp.wait_ge(s["bs_stored"], 16)
        for q in range(2, 4):
            sp.dma_start(mixf[:, 4 * q:4 * q + 4, :], mix_d[:, 4 * q:4 * q + 4, :]).then_inc(m_landed[q], 16)
        for q in range(4):
            sp.wait_ge(m_lo, 4 * q + 4)
            sp.dma_start(xres[:, 4 * q:4 * q + 4, :], xT[:, 4 * q:4 * q + 4, :]).then_inc(r_landed[q], 16)
        with sp.Fori(0, KD // 2) as i:
            for c in range(4):
                w_load(U_OUT, c, 4, i)
        for q in range(4):
            sp.wait_ge(h_done, 4 * q + 4)
            sp.dma_start(h_d[:, 4 * q:4 * q + 4, :], mix[:, 4 * q:4 * q + 4, :]).then_inc(h_stored, 16)
        sp.wait_ge(h_stored, 64)
        sp.wait_ge(h_lo, KD)
        sp.wait_ge(h_sq, KD)
        sp.wait_ge(h_hi, KD)
        sp.wait_ge(h_acc, KD)
        sp.dma_start(st[:], state).then_inc(st_landed, 16)

        for c in range(4):
            w_load(U_FFN, c)
        with sp.Fori(0, ROUNDS - 1) as i:
            for c in range(24):
                w_load(U_FFN + 4, c, 24, i)
        for c in range(20 - 6):
            w_load(UNITS - 20, c)
        sp.wait_ge(hist_cp, 2 * KF)
        sp.dma_start(hist_out, hs[:]).then_inc(hist_stored, 16)
        sp.wait_ge(w_used, UNITS - 8)
        for q in range(4):
            sp.dma_start(hres[:, 4 * q:4 * q + 4, :], h_d[:, 4 * q:4 * q + 4, :]).then_inc(hr_landed[q], 16)
        for q in range(4):
            sp.wait_ge(y_done, 4 * q + 4)
            sp.dma_start(y_out[:, 4 * q:4 * q + 4, :], y[:, 4 * q:4 * q + 4, :]).then_inc(y_stored, 16)
        sp.wait_ge(y_stored, 64)
        sp.wait_ge(hist_stored, 16)

    @block.scalar
    def _(act):
        for u in range(RAW):
            sc.wait_ge(w_landed[u], 16)
            sc.activation(wh[:, u, :], wraw[:, u, :], ACT.Copy).then_inc(w_hi, 1)
        act.wait_ge(c_landed, 32)
        act.wait_ge(lam_sum, 2)
        sc.activation(lt[:, 2:4], lt[:, 0:2], ACT.Exp).then_inc(lam_exp, 1)
        for q in range(4):
            act.wait_ge(x_landed[q], 16)
            with act.Fori(0, 4) as k:
                sc.activation(xh[:, bass.ds(4 * q + k, 1), :].rearrange("p a n -> p (a n)"),
                              xraw[:, bass.ds(4 * q + k, 1), :].rearrange("p a n -> p (a n)"), ACT.Copy,
                              scale=cs[:, bass.ds(C_PRE + 4 * q + k, 1)]).then_inc(x_hi, 1)
            if q == 0:
                for u in range(RAW, 4):
                    act.wait_ge(w_landed[u % RAW], 32)
                    sc.activation(wh[:, u, :], wraw[:, u % RAW, :], ACT.Copy).then_inc(w_hi, 1)
        act.wait_ge(x_ssq_mm, KD)
        sc.activation(halves(R[:]), tile_out(6), ACT.Sqrt, scale=1.0 / D, bias=EPS).then_inc(sq_root, 1)

        with act.Fori(0, H // 2) as j:
            for t in range(2):
                w_split_hi(U_QK, 4 * t, 8, j)
                w_split_hi(U_QK, 4 * t + 1, 8, j)
                act.wait_ge(q_evac, 2 * j + t + 1)
                act.wait_ge(pool_c, 2)
                for z in range(2):
                    o = 2 * DT * t + DT * z
                    sc.activation(
                        qbd[DH * z:DH * z + DH, :, bass.ds(2 * j + t, 1), o:o + DT].rearrange("p b a n -> p b (a n)"),
                        zt[0][DH * z:DH * z + DH, SEQ:T].rearrange("p (b n) -> p b n", b=DB),
                        ACT.Copy).then_inc(smp, 1)
                w_split_hi(U_QK, 4 * t + 2, 8, j)
                w_split_hi(U_QK, 4 * t + 3, 8, j)
                act.wait_ge(k_evac, 2 * j + t + 1)
                act.wait_ge(pool_c, 2)
                sc.activation(kns[:, :, bass.ds(2 * j + t, 1), :].rearrange("p b a n -> p b (a n)"),
                              zt[1][:, SEQ:T].rearrange("p (b n) -> p b n", b=DB), ACT.Copy).then_inc(smp, 1)
        with act.Fori(0, H // 2) as i:
            for c in range(4):
                w_split_hi(U_V, c, 4, i)

        with act.Fori(0, DB) as j:
            act.wait_ge(s["spv_ready"], j)
            for g_ in range(4):
                n = (g_ + 1) * P
                o = g_ * (g_ + 1) // 2 * P
                act.wait_ge(pg_used[g_ % 2], 4 * j + g_ // 2 + 1)
                sc.activation(S[:, SEQ * g_:SEQ * (g_ + 1)], pb[:, 2 + g_ % 2, :], ACT.Copy
                              ).then_inc(s["st_copied"], 1)
                act.wait_ge(s["pneg_ready"], 4 * j + g_ + 1)
                act.wait_ge(s["wT_ready"], 4 * j)
                sc.activation(W[:, o:o + n], pb[:, 6, 0:n], ACT.Exp, scale=SCALE, bias=pneg[:, 0:1],
                              accum_out=psm[:, 2 * g_:2 * g_ + 1]).then_inc(s["pexp_done"], 1)
                act.wait_ge(s["pw_done"], 4 * j + g_)
                act.wait_ge(s["b_done"], j)
                sc.activation(E2[:, 0:n], pb[:, 7, 0:n], ACT.Exp, scale=SCALE, bias=pneg[:, 1:2],
                              accum_out=psm[:, 2 * g_ + 1:2 * g_ + 2]).then_inc(s["pexp_done"], 1)
                if g_ < 3:
                    w_split_hi(U_HEADS, g_, 4, j)
            act.wait_ge(s["nmx_ready"], j + 1)
            for g_ in range(5):
                z = min(SEQ * (g_ + 1), PAGES * P + DT)
                sc.activation(S[:, SEQ * g_:z], S[:, SEQ * g_:z], ACT.Exp, scale=SCALE, bias=nmx[:, 0:1],
                              accum_out=ssm[:, g_:g_ + 1]).then_inc(s["sexp"], 1)
            w_split_hi(U_HEADS, 3, 4, j)
            act.wait_ge(s["u_evac"], j + 1)
            sc.activation(ug[:], ug[:], ACT.Gelu_apprx_tanh).then_inc(s["ugelu"], 1)
            act.wait_ge(s["va_evac"], j + 1)
            sc.activation(vg[:], vg[:], ACT.Gelu_apprx_tanh).then_inc(s["vgelu"], 1)
            act.wait_ge(s["vgelu"], j + 1)
            sc.activation(vq[:], vg[:], ACT.Square).then_inc(s["vsq_ready"], 1)
            act.wait_ge(s["vssq_ready"], j + 1)
            sc.activation(halves(vq[:]), tile_out(2), ACT.Sqrt, scale=1.0 / HD, bias=EPS).then_inc(s["vsd_done"], 1)
            act.wait_ge(s["po_copied"], j + 1)
            act.wait_ge(s["pw_done"], 4 * j + 4)
            sc.activation(E2[:], po[:], ACT.Square).then_inc(s["posq"], 1)
            act.wait_ge(s["pss_ready"], j + 1)
            sc.activation(E2[:], pb[:, 0, :], ACT.Sqrt, scale=1.0 / HD, bias=EPS).then_inc(s["psd_done"], 1)
            act.wait_ge(s["sss_ready"], j + 1)
            sc.activation(osq[:], pb[:, 5, 0:NS], ACT.Sqrt, scale=1.0 / HD, bias=EPS).then_inc(s["ssd_done"], 1)

        for q in range(4):
            act.wait_ge(m_landed[q], 16)
            if q == 0:
                act.wait_ge(w_used, U_OUT)
            with act.Fori(0, 4) as k:
                sc.activation(xh[:, bass.ds(4 * q + k, 1), :].rearrange("p a n -> p (a n)"),
                              mixf[:, bass.ds(4 * q + k, 1), :].rearrange("p a n -> p (a n)"),
                              ACT.Copy).then_inc(m_hi, 1)
        with act.Fori(0, KD // 2) as i:
            for t in range(2):
                w_split_hi(U_OUT, 2 * t, 4, i)
                w_split_hi(U_OUT, 2 * t + 1, 4, i)
                act.wait_ge(m_copied[t], i + 1)
                act.wait_ge(m_acc, 2 * i)
                act.wait_ge(c_landed, 32)
                sc.activation(sqt[:, t, :], mix[:, bass.ds(2 * i + t, 1), :].rearrange("p a n -> p (a n)"),
                              ACT.Square).then_inc(m_sq[t], 1)
        act.wait_ge(ssq_mm, 1)
        sc.activation(halves(R[:]), tile_out(4), ACT.Sqrt, scale=1.0 / D, bias=EPS).then_inc(sq_root, 1)
        with act.Fori(0, KD // 2) as i:
            for t in range(2):
                act.wait_ge(h_acc, 2 * i)
                act.wait_ge(h_done, 2 * i + t + 1)
                act.wait_ge(c_landed, 32)
                sc.activation(xh[:, bass.ds(2 * i + t, 1), :].rearrange("p a n -> p (a n)"),
                              mix[:, bass.ds(2 * i + t, 1), :].rearrange("p a n -> p (a n)"), ACT.Copy,
                              scale=cs[:, bass.ds(C_FFN + 2 * i + t, 1)]).then_inc(h_hi, 1)
                sc.activation(sqt[:, t, :], mix[:, bass.ds(2 * i + t, 1), :].rearrange("p a n -> p (a n)"),
                              ACT.Square).then_inc(h_sq, 1)
        act.wait_ge(ssq_mm, 2)
        act.wait_ge(h_lo, KD)
        sc.activation(halves(R[:]), tile_out(6), ACT.Sqrt, scale=1.0 / D, bias=EPS).then_inc(sq_root, 1)

        def conv_tap2(p, t, n):
            act.wait_ge(up_evac[t], n + 1)
            act.wait_ge(st_in, 2 * n + t + 1)
            act.wait_ge(gv_done, n)
            act.wait_ge(c_landed, 32)
            f = p + KF * t
            sc.activation(cv[t][:, 0:NC_], ub[t][:, 2:UB], ACT.Identity, scale=cs[:, bass.ds(C_W + 4 * KF + f, 1)],
                          bias=cs[:, bass.ds(C_B + f, 1)]).then_inc(tap, 1)

        def pair_act(p, n, splits):
            splits[0]()
            conv_tap2(p, 0, n)
            act.wait_ge(cv_done, 2 * n + 1)
            sc.activation(cv[0][:, 0:NC_], cv[0][:, 0:NC_], ACT.Gelu_apprx_tanh).then_inc(gelu_done, 1)
            splits[1]()
            conv_tap2(p, 1, n)

        def g_split_hi(n, slot, groups):
            act.wait_ge(gv_done, n + 1)
            act.wait_ge(w_used, U_FFN + 4 + 24 * groups)
            sc.activation(gh[:, slot, :], gv[:], ACT.Copy).then_inc(g_hi, 1)

        def pair_splits(base, c, per=0, i=0):
            return [lambda k=k: (w_split_hi(base, c + 2 * k, per, i), w_split_hi(base, c + 2 * k + 1, per, i))
                    for k in range(2)]

        pair_act(0, 0, pair_splits(U_FFN, 0))
        g_split_hi(0, 0, 0)
        with act.Fori(0, ROUNDS - 1) as i:
            for t in range(3):
                pair_act(GRP * i + 1 + t, GRP * i + 1 + t, pair_splits(U_FFN + 4, 4 * t, 24, i))
                g_split_hi(GRP * i + 1 + t, 1 + t, i)
            pair_act(GRP * i + 4, GRP * i + 4, pair_splits(U_FFN + 4, 12, 24, i))
            for c in range(16, 24):
                w_split_hi(U_FFN + 4, c, 24, i)
            g_split_hi(GRP * i + 4, 0, i + 1)
        for t in range(3):
            pair_act(KF - 3 + t, KF - 3 + t, pair_splits(UNITS - 20, 4 * t))
            g_split_hi(KF - 3 + t, 1 + t, ROUNDS - 1)
        for c in range(12, 16):
            w_split_hi(UNITS - 20, c)
        act.wait_ge(dn_done, KD * ROUNDS)
        with act.Fori(0, KD // 2) as i:
            for t in range(2):
                act.wait_ge(y_acc, 2 * i)
                act.wait_ge(c_landed, 32)
                sc.activation(sql[:, t, :], y[:, bass.ds(2 * i + t, 1), :].rearrange("p a n -> p (a n)"),
                              ACT.Square).then_inc(y_sq, 1)
        act.wait_ge(ssq_mm, 3)
        sc.activation(halves(R[:]), tile_out(0), ACT.Sqrt, scale=1.0 / D, bias=EPS).then_inc(sq_root, 1)

    @block.gpsimd
    def _(pool):
        pl.memset(ones[:], 1.0).then_inc(ready, 1)
        pl.memset(ident[:], 0.0).then_inc(pool_c, 1)
        pool.wait_ge(pool_c, 1)
        pl.affine_select(out=ident[:], in_=ident[:], compare_op=ALU.not_equal, fill=1.0, base=0,
                         pattern=[[-1, P]], channel_multiplier=1).then_inc(ready, 1)
        pool.wait_ge(w_hi, 1)
        pl.tensor_tensor(wl[:, 0, :], wraw[:, 0, :], wh[:, 0, :].bitcast(F32), ALU.subtract).then_inc(w_lo, 1)
        pool.wait_ge(w_hi, 2)
        pl.tensor_tensor(wl[:, 1, :], wraw[:, 1, :], wh[:, 1, :].bitcast(F32), ALU.subtract).then_inc(w_lo, 1)
        for q in range(4):
            pool.wait_ge(x_landed[q], 16)
            with pool.Fori(0, 2) as i:
                for t in range(2):
                    pool.wait_ge(x_ssq_mm, 4 * q + 2 * i)
                    xk = xraw[:, bass.ds(4 * q + 2 * i + t, 1), :].rearrange("p a n -> p (a n)")
                    pl.tensor_tensor(sq0[:, t, :], xk, xk, ALU.mult).then_inc(x_sq, 1)
        for u in range(2, 4):
            pool.wait_ge(w_hi, u + 1)
            pl.tensor_tensor(wl[:, u, :], wraw[:, u % RAW, :], wh[:, u, :].bitcast(F32),
                             ALU.subtract).then_inc(w_lo, 1)
        pl.memset(qbd[:], 0.0).then_inc(pool_c, 1)
        with pool.Fori(0, H) as j:
            for c in range(4):
                w_split_lo(U_QK, c, 4, j)
        pool.dma_start(ptab_sb[:], ptab).then_inc(p_landed, 16)
        with pool.Fori(0, H // 2) as i:
            for c in range(4):
                w_split_lo(U_V, c, 4, i)
        pool.wait_ge(s_stored, 32)
        pl.memset(maskd[:], 0.0).then_inc(pool_c, 1)
        pool.wait_ge(pool_c, 3)
        pl.affine_select(out=maskd[:], in_=maskd[:], compare_op=ALU.is_ge, fill=NEG, base=0,
                         pattern=[[-1, P]], channel_multiplier=1).then_inc(ready, 1)
        with pool.Fori(0, DB) as j:
            pool.wait_ge(g_landed, 48 * j + 48)
            w_split_lo(U_HEADS, 0, 4, j)
            pl.affine_select(out=ws[:], in_=ws[:], compare_op=ALU.is_ge, fill=0.0, base=0,
                             pattern=[[1, P]], channel_multiplier=-1).then_inc(s["ws_masked"], 1)
            pl.affine_select(out=wb[:], in_=wb[:], compare_op=ALU.is_ge, fill=0.0, base=0,
                             pattern=[[1, NS]], channel_multiplier=-1).then_inc(s["ws_masked"], 1)
            for c in range(1, 4):
                w_split_lo(U_HEADS, c, 4, j)
            pool.wait_ge(s["va_norm"], j + 1)
            pool.dma_start(va_out[bass.ds(j, 1)].rearrange("a p n -> (a p) n"), vaT[:, SEQ:T]
                           ).then_inc(s["va_stored"], 16)
            pool.wait_ge(s["a_done"], j + 1)
            pool.dma_start(mix_d[:, bass.ds(j, 1), :].rearrange("p a n -> p (a n)"), ao[:]).then_inc(s["a_stored"], 16)
            pool.wait_ge(s["b_done"], j + 1)
            pool.dma_start(mix_d[:, bass.ds(H + j, 1), 0:SEQ].rearrange("p a n -> p (a n)"), po[:]
                           ).then_inc(s["b_stored"], 16)
        pool.wait_ge(s["bs_done"], DB)
        pool.dma_start(mix_d[:, H:2 * H, SEQ:T], bsmp[:]).then_inc(s["bs_stored"], 16)
        with pool.Fori(0, KD // 2) as i:
            for c in range(4):
                w_split_lo(U_OUT, c, 4, i)
        pool.wait_ge(h_done, KD)
        pl.memset(y[:], 0.0).then_inc(y_zero, 1)

        def hist(p, n):
            for t in range(2):
                f = p + KF * t
                if n is not None:
                    pool.wait_ge(cv_done, 2 * n)
                pl.tensor_copy(ub[t][:, 2 + SEQ:UB].rearrange("p (b n) -> p b n", b=DB)[:, :, 0:2],
                               st[:, bass.ds(f, 1), :].rearrange("p a (b n) -> p (a b) n", b=DB)).then_inc(st_in, 1)

        def hist_new(p, n):
            for t in range(2):
                f = p + KF * t
                pool.wait_ge(up_evac[t], n + 1)
                pl.tensor_copy(hs[:, bass.ds(f, 1), 0:2].rearrange("p a n -> p (a n)"),
                               ub[t][:, SEQ:SEQ + 2])
                pl.tensor_copy(hs[:, bass.ds(f, 1), 2:18].rearrange("p a (b n) -> p (a b) n", b=DB),
                               ub[t][:, 2 + SEQ:UB].rearrange("p (b n) -> p b n", b=DB)[:, :, DT:DT + 2]
                               ).then_inc(hist_cp, 1)

        def g_split_lo(n, slot):
            pool.wait_ge(g_hi, n + 1)
            pl.tensor_tensor(gl[:, slot, :], gv[:], gh[:, slot, :].bitcast(F32), ALU.subtract).then_inc(g_lo, 1)

        pool.wait_ge(st_landed, 16)
        hist(0, None)
        for c in range(4):
            w_split_lo(U_FFN, c)
        hist_new(0, 0)
        g_split_lo(0, 0)
        with pool.Fori(0, ROUNDS - 1) as i:
            for t in range(4):
                p = GRP * i + 1 + t
                hist(p, p)
                for c in range(4):
                    w_split_lo(U_FFN + 4, 4 * t + c, 24, i)
                hist_new(p, p)
                if t < 3:
                    g_split_lo(p, 1 + t)
            for c in range(16, 24):
                w_split_lo(U_FFN + 4, c, 24, i)
            g_split_lo(GRP * i + 4, 0)
        for t in range(3):
            p = KF - 3 + t
            hist(p, p)
            for c in range(4):
                w_split_lo(UNITS - 20, 4 * t + c)
            hist_new(p, p)
            g_split_lo(p, 1 + t)
        for c in range(12, 16):
            w_split_lo(UNITS - 20, c)

    @block.vector
    def _(dve):
        dve.wait_ge(c_landed, 32)
        for z in range(2):
            v.tensor_tensor_reduce(out=lamin[:, 2 * z, :], in0=lamin[:, 2 * z, :], in1=lamin[:, 2 * z + 1, :],
                                   scale=1.0, scalar=0.0, op0=ALU.mult, op1=ALU.add,
                                   accum_out=lt[:, z:z + 1]).then_inc(lam_sum, 1)
        ch = Chain(dve, dve_c, 0)
        ch.link(v.tensor_scalar(gsub[:], cs[:, C_SUB:C_SUB + 1], 1.0 - LAM_INIT, None, ALU.mult))
        for q in range(4):
            dve.wait_ge(x_landed[q], 16)
            with dve.Fori(0, 4) as k:
                dve.wait_ge(x_hi, 4 * q + k + 1)
                v.scalar_tensor_tensor(out=xl[:, bass.ds(4 * q + k, 1), :].rearrange("p a n -> p (a n)"),
                                       in0=xraw[:, bass.ds(4 * q + k, 1), :].rearrange("p a n -> p (a n)"),
                                       scalar=cs[:, bass.ds(C_PRE + 4 * q + k, 1)],
                                       in1=xh[:, bass.ds(4 * q + k, 1), :].rearrange("p a n -> p (a n)").bitcast(F32),
                                       op0=ALU.mult, op1=ALU.subtract).then_inc(x_lo, 1)
        dve.wait_ge(lam_exp, 1)
        ch.link(v.tensor_tensor(lt[:, 0:1], lt[:, 3:4], lt[:, 2:3], ALU.subtract))
        ch.link(v.tensor_scalar(neglam[:], lt[:, 0:1], -LAM_INIT, None, ALU.add))
        ch.link(v.tensor_scalar(sgn[:], cs[:, C_SEL + 1:C_SEL + 2], neglam[:, 0:1], None, ALU.mult))
        ch.link(v.tensor_tensor(sgn[:], sgn[:], cs[:, C_SEL:C_SEL + 1], ALU.add))
        dve.wait_ge(sq_root, 1)
        v.reciprocal(R[:], R[:]).then_inc(R_ready, 1)
        dve.wait_ge(R_ready, 1)
        Rh = halves(R[:])
        with dve.Fori(0, H) as j:
            tile_done(dve, U_QK, 0, 4, j)
            dve.wait_ge(q_stored, 16 * j)
            dve.wait_ge(smp, 3 * j)
            v.tensor_tensor(halves(zt[0][:]), tile_out(0), Rh, ALU.mult).then_inc(q_evac, 1)
            tile_done(dve, U_QK, 2, 4, j)
            dve.wait_ge(k_stored, 16 * j)
            v.tensor_tensor(halves(zt[1][:]), tile_out(2), Rh, ALU.mult).then_inc(k_evac, 1)
        dve.wait_ge(q_stored, 16 * H)
        dve.wait_ge(k_stored, 16 * H)
        dve.wait_ge(smp, 3 * H)
        with dve.Fori(0, H // 2) as i:
            for t in range(2):
                tile_done(dve, U_V, 2 * t, 4, i)
                dve.wait_ge(vT_ready, 2 * i)
                v.tensor_tensor(halves(zt[t][:]), tile_out(2 * t), Rh, ALU.mult).then_inc(v_evac, 1)
            for t in range(2):
                dve.wait_ge(vT_ready, 2 * i + t + 1)
                dve.wait_ge(v_stored[t], 32 * i)
                v.tensor_copy(vt[t][:, 0:4, :], pb[:, 4 + t, :].rearrange("p (b n) -> p b n", b=4)
                              )
                v.tensor_copy(vt[t][0:NS, 4, :], pb[0:NS, 6 + t, 0:P]).then_inc(vt_evac, 1)

        dve.wait_ge(ready, 3)
        dve.wait_ge(v_stored[0], 16 * H)
        dve.wait_ge(v_stored[1], 16 * H)
        base = ch.c
        NCH = 32
        with dve.Fori(0, DB) as j:
            ch = Chain(dve, dve_c, base, NCH, j)

            def combine(g_):
                n = (g_ + 1) * P
                o = g_ * (g_ + 1) // 2 * P
                dve.wait_ge(s["pexp_done"], 8 * j + 2 * g_ + 2)
                ch.link(v.reciprocal(prs[:], psm[:, 2 * g_:2 * g_ + 2]))
                ch.link(v.tensor_tensor(prs[:, 1:2], prs[:, 1:2], neglam[:], ALU.mult))
                ch.link(v.tensor_scalar(W[:, o:o + n], W[:, o:o + n], prs[:, 0:1], None, ALU.mult))
                v.scalar_tensor_tensor(out=W[:, o:o + n], in0=E2[:, 0:n], scalar=prs[:, 1:2], in1=W[:, o:o + n],
                                       op0=ALU.mult, op1=ALU.add).then_inc(s["pw_done"], 1)

            def s_max(g_):
                dve.wait_ge(s["st_copied"], 4 * j + g_ + 1)
                v.tensor_reduce(mx4[:, g_:g_ + 1], S[:, SEQ * g_:SEQ * (g_ + 1)], AX.X, ALU.max
                                ).then_inc(s["s_max"], 1)

            def copy_wT(g_):
                n = (g_ + 1) * P
                o = g_ * (g_ + 1) // 2 * P
                dve.wait_ge(s["wT_ready"], 4 * j + g_ + 1)
                dve.wait_ge(s["pv_ready"], j)
                v.tensor_copy(wT[:, o:o + n], pb[:, 4 + g_ % 2, 0:n]).then_inc(s["wT_copied"], 1)

            def copy_sT(g_):
                dve.wait_ge(s["sT_ready"], 5 * j + g_ + 1)
                v.tensor_copy(S[:, SEQ * g_:SEQ * (g_ + 1)], pb[:, 4 + (g_ + 1) % 2, :]).then_inc(s["sT_copied"], 1)

            for g_ in range(4):
                n = (g_ + 1) * P
                dve.wait_ge(s["pscore_ready"], 4 * j + g_ + 1)
                diag = pb[:, 6:8, g_ * P:n]
                ch.link(v.tensor_tensor(diag, diag, maskd[:].rearrange("p (a n) -> p a n", a=1)
                                        .to_broadcast([P, 2, P]), ALU.add))
                ch.link(v.tensor_reduce(pmx[:], pb[:, 6:8, 0:n], AX.X, ALU.max))
                dve.wait_ge(s["pexp_done"], 8 * j + 2 * g_)
                v.tensor_scalar(pneg[:], pmx[:], -SCALE, None, ALU.mult).then_inc(s["pneg_ready"], 1)
                s_max(g_)
                if g_ >= 1:
                    combine(g_ - 1)
                if g_ == 1:
                    tile_done(dve, U_HEADS, 0, 4, j)
                    dve.wait_ge(s["a_done"], j)
                    v.tensor_tensor(halves(ug[:]), tile_out(0), Rh, ALU.mult).then_inc(s["u_evac"], 1)
                if g_ == 3:
                    copy_wT(0)
            dve.wait_ge(s["snew_ready"], j + 1)
            v.tensor_tensor(S[:, PAGES * P:], pb[:, 2, 0:DT], cs[:, C_MASK:C_MASK + DT], ALU.add
                            ).then_inc(s["snew_masked"], 1)
            dve.wait_ge(s["snew_masked"], j + 1)
            ch.link(v.tensor_reduce(mx4[:, 4:5], S[:, PAGES * P:], AX.X, ALU.max))
            dve.wait_ge(s["s_max"], 4 * j + 4)
            ch.link(v.tensor_reduce(mx[:], mx4[:], AX.X, ALU.max))
            v.tensor_scalar(nmx[:], mx[:], -SCALE, None, ALU.mult).then_inc(s["nmx_ready"], 1)
            combine(3)
            copy_wT(1)
            tile_done(dve, U_HEADS, 2, 4, j)
            v.tensor_tensor(halves(vg[:]), tile_out(0), Rh, ALU.mult).then_inc(s["va_evac"], 1)
            copy_wT(2)
            copy_sT(0)
            copy_wT(3)
            for g_ in range(1, 4):
                copy_sT(g_)
            dve.wait_ge(s["sT_ready"], 5 * j + 5)
            v.tensor_copy(En[:], pb[0:DT, 5, 0:P]).then_inc(s["sT_copied"], 1)
            dve.wait_ge(s["sexp"], 5 * j + 5)
            ch.link(v.tensor_reduce(rs[:, 0:1], ssm[:], AX.X, ALU.add))
            ch.link(v.reciprocal(rs[:, 1:2], rs[:, 0:1]))
            ch.link(v.tensor_tensor(rs[:, 0:1], rs[:, 1:2], sgn[:], ALU.mult))
            dve.wait_ge(s["vsd_done"], j + 1)
            ch.link(v.reciprocal(vq[:], vq[:]))
            dve.wait_ge(s["va_stored"], 16 * j)
            v.scalar_tensor_tensor(out=vaT[:], in0=vg[:], scalar=cs[:, bass.ds(C_VA + j, 1)], in1=vq[:],
                                   op0=ALU.mult, op1=ALU.mult).then_inc(s["va_norm"], 1)
            dve.wait_ge(s["vaT_ready"], j + 1)
            v.tensor_copy(vtok[:, 0:4, :], pb[:, 2, :].rearrange("p (b n) -> p b n", b=4)
                          ).then_inc(s["vtok_copied"], 1)
            v.tensor_copy(vtok[0:NS, 4, :], pb[0:NS, 3, 0:P]).then_inc(s["vtok_copied"], 1)
            dve.wait_ge(s["pv_ready"], j + 1)
            dve.wait_ge(s["b_stored"], 16 * j)
            v.tensor_copy(po[:], pb[:, 6, :]).then_inc(s["po_copied"], 1)
            dve.wait_ge(s["spv_ready"], j + 1)
            v.tensor_scalar(osb[:], pb[:, 7, 0:2 * P], rs[:, 0:1], None, ALU.mult).then_inc(s["osb_ready"], 1)
            dve.wait_ge(s["oT_ready"], j + 1)
            ch.link(v.tensor_copy(oT[:], pb[:, 4, 0:2 * P]))
            for z in range(2):
                o4 = oT[:, P * z:P * z + P].rearrange("p (h y k n) -> p h y k n", h=H // 2, y=2, k=2)
                ch.link(v.tensor_tensor(osm[:].rearrange("p (h y n) -> p h y n", h=H // 2, y=2)[:, :, z, :],
                                        o4[:, :, z, 0, :], o4[:, :, z, 1, :], ALU.add))
            v.tensor_tensor(osq[:], osm[:], osm[:], ALU.mult).then_inc(s["ssq_ready"], 1)
            dve.wait_ge(s["gm_ready"], j + 1)
            dve.wait_ge(g_landed, 48 * j + 48)
            dve.wait_ge(s["a_stored"], 16 * j)
            v.tensor_tensor(ao[:, 0:SEQ].rearrange("p (b n) -> p b n", b=4),
                            pb[:, 2, :].rearrange("p (b n) -> p b n", b=4),
                            bsb[:].rearrange("p (a n) -> p a n", a=1).to_broadcast([P, 4, P]), ALU.add
                            ).then_inc(s["ao_prompt"], 1)
            ch.link(v.tensor_tensor(ao[:, SEQ:T].rearrange("p (b n) -> p b n", b=DB),
                                    pb[:, 3, P:P + NS].rearrange("p (b n) -> p b n", b=DB),
                                    bsb[:, 0:DT].rearrange("p (a n) -> p a n", a=1).to_broadcast([P, DB, DT]),
                                    ALU.add))
            dve.wait_ge(s["ao_prompt"], j + 1)
            dve.wait_ge(s["ugelu"], j + 1)
            v.tensor_tensor(ao[:], ao[:], ug[:], ALU.mult).then_inc(s["a_done"], 1)
            dve.wait_ge(s["psd_done"], j + 1)
            dve.wait_ge(s["po_copied"], j + 1)
            ch.link(v.reciprocal(E2[:], E2[:]))
            v.scalar_tensor_tensor(out=po[:], in0=po[:], scalar=gsub[:, 0:1], in1=E2[:],
                                   op0=ALU.mult, op1=ALU.mult).then_inc(s["b_done"], 1)
            dve.wait_ge(s["ssd_done"], j + 1)
            ch.link(v.reciprocal(osq[:], osq[:]))
            v.scalar_tensor_tensor(out=bsmp[:, :, bass.ds(DT * j, DT)],
                                   in0=osm[:].rearrange("p (h n) -> p h n", h=H), scalar=gsub[:, 0:1],
                                   in1=osq[:].rearrange("p (h n) -> p h n", h=H),
                                   op0=ALU.mult, op1=ALU.mult).then_inc(s["bs_done"], 1)
            ch.close(NCH)

        for q in range(4):
            dve.wait_ge(m_landed[q], 16)
            with dve.Fori(0, 4) as k:
                dve.wait_ge(m_hi, 4 * q + k + 1)
                v.tensor_tensor(xl[:, bass.ds(4 * q + k, 1), :].rearrange("p a n -> p (a n)"),
                                mixf[:, bass.ds(4 * q + k, 1), :].rearrange("p a n -> p (a n)"),
                                xh[:, bass.ds(4 * q + k, 1), :].rearrange("p a n -> p (a n)").bitcast(F32),
                                ALU.subtract).then_inc(m_lo, 1)
        v.memset(acc[:], 0.0).then_inc(acc_zero, 1)
        dve.wait_ge(acc_zero, 1)
        with dve.Fori(0, KD // 2) as i:
            for t in range(2):
                tile_done(dve, U_OUT, 2 * t, 4, i)
                v.tensor_copy(halves(mix[:, bass.ds(2 * i + t, 1), :].rearrange("p a n -> p (a n)")),
                              tile_out(2 * t)).then_inc(m_copied[t], 1)
                dve.wait_ge(m_sq[t], i + 1)
                dve.wait_ge(m_acc, 2 * i + t)
                v.tensor_tensor(acc[:], acc[:], sqt[:, t, :], ALU.add).then_inc(m_acc, 1)
        dve.wait_ge(sq_root, 2)
        v.reciprocal(R[:], R[:]).then_inc(R_ready, 1)
        dve.wait_ge(R_ready, 2)
        v.memset(acc[:], 0.0).then_inc(acc_zero, 1)
        dve.wait_ge(acc_zero, 2)
        dve.wait_ge(m_copied[0], KD // 2)
        dve.wait_ge(m_copied[1], KD // 2)
        for q in range(4):
            dve.wait_ge(r_landed[q], 16)
            with dve.Fori(0, 2) as i:
                for t in range(2):
                    k = 4 * q + 2 * i + t
                    mk = mix[:, bass.ds(k, 1), :].rearrange("p a n -> p (a n)")
                    v.tensor_tensor(mk, mk, R[:], ALU.mult).then_inc(h_tmp, 1)
                    dve.wait_ge(h_tmp, k + 1)
                    v.scalar_tensor_tensor(out=mk, in0=mk, scalar=cs[:, bass.ds(C_POST + k, 1)],
                                           in1=xres[:, bass.ds(k, 1), :].rearrange("p a n -> p (a n)"),
                                           op0=ALU.mult, op1=ALU.add).then_inc(h_done, 1)
                    dve.wait_ge(h_done, k + 1)
                    dve.wait_ge(h_hi, k + 1)
                    v.scalar_tensor_tensor(out=xl[:, bass.ds(k, 1), :].rearrange("p a n -> p (a n)"),
                                           in0=mk, scalar=cs[:, bass.ds(C_FFN + k, 1)],
                                           in1=xh[:, bass.ds(k, 1), :].rearrange("p a n -> p (a n)").bitcast(F32),
                                           op0=ALU.mult, op1=ALU.subtract).then_inc(h_lo, 1)
                    dve.wait_ge(h_sq, k + 1)
                    dve.wait_ge(h_acc, k)
                    v.tensor_tensor(acc[:], acc[:], sqt[:, t, :], ALU.add).then_inc(h_acc, 1)
        dve.wait_ge(sq_root, 3)
        v.reciprocal(R[:], R[:]).then_inc(R_ready, 1)
        dve.wait_ge(R_ready, 3)
        dve.wait_ge(h_stored, 64)
        for t in range(2):
            v.memset(ub[t][:, 0:2], 0.0).then_inc(ub_zero, 1)
        dve.wait_ge(ub_zero, 2)

        def evac_up(t, n, base, c, per, i):
            tile_done(dve, base, c + 2 * t, per, i)
            dve.wait_ge(cv_done, 2 * n)
            dve.wait_ge(hist_cp, 2 * n)
            lo_, hi_ = pb[:, 2 * t, 0:TH], pb[:, 2 * t + 1, 0:TH]
            v.tensor_tensor(ub[t][:, 2:2 + TH], lo_, R[:, 0:TH], ALU.mult)
            v.tensor_tensor(ub[t][:, 2 + TH:2 + SEQ], hi_[:, 0:SEQ - TH], R[:, TH:SEQ], ALU.mult)
            v.tensor_tensor(ub[t][:, 2 + SEQ:UB].rearrange("p (b n) -> p b n", b=DB)[:, :, 2:2 + DT],
                            hi_[:, SEQ - TH:TH].rearrange("p (b n) -> p b n", b=DB),
                            R[:, SEQ:T].rearrange("p (b n) -> p b n", b=DB), ALU.mult).then_inc(up_evac[t], 1)

        def conv(p, t, n):
            f = p + KF * t
            dve.wait_ge(tap, 2 * n + t + 1)
            v.scalar_tensor_tensor(out=cv[t][:, 0:NC_], in0=ub[t][:, 1:UB - 1],
                                   scalar=cs[:, bass.ds(C_W + 2 * KF + f, 1)],
                                   in1=cv[t][:, 0:NC_], op0=ALU.mult, op1=ALU.add).then_inc(tap1, 1)
            dve.wait_ge(tap1, 2 * n + t + 1)
            v.scalar_tensor_tensor(out=cv[t][:, 0:NC_], in0=ub[t][:, 0:NC_],
                                   scalar=cs[:, bass.ds(C_W + f, 1)],
                                   in1=cv[t][:, 0:NC_], op0=ALU.mult, op1=ALU.add).then_inc(cv_done, 1)

        def smp_cols(ap):
            return ap[:, SEQ:SEQ + DB * 10].rearrange("p (b n) -> p b n", b=DB)[:, :, 2:2 + DT]

        def pair_dve(p, n, base, c, per=0, i=0):
            for t in range(2):
                evac_up(t, n, base, c, per, i)
                conv(p, t, n)
            dve.wait_ge(gelu_done, n + 1)
            dve.wait_ge(cv_done, 2 * n + 2)
            dve.wait_ge(g_lo, n)
            v.tensor_tensor(gv[:, 0:SEQ], cv[0][:, 0:SEQ], cv[1][:, 0:SEQ], ALU.mult)
            v.tensor_tensor(gv[:, SEQ:T].rearrange("p (b n) -> p b n", b=DB), smp_cols(cv[0]), smp_cols(cv[1]),
                            ALU.mult).then_inc(gv_done, 1)

        def down_dve(r, base, c, per=0, i=0):
            for m in range(KD):
                if m % 2:
                    dve.wait_ge(w_used, base + c + m // 2 + 1 + (per * i if per else 0))
                else:
                    dve.wait_ge(dn_even, KD // 2 * r + m // 2 + 1)
                ym = halves(y[:, m, :])
                v.tensor_tensor(ym, ym, tile_out(4 + 2 * (m % 2)), ALU.add).then_inc(dn_done, 1)

        pair_dve(0, 0, U_FFN, 0)
        dve.wait_ge(y_zero, 1)
        with dve.Fori(0, ROUNDS - 1) as i:
            for t in range(4):
                pair_dve(GRP * i + 1 + t, GRP * i + 1 + t, U_FFN + 4, 4 * t, 24, i)
            dve.wait_ge(dn_done, KD * i)
            down_dve(i, U_FFN + 4, 16, 24, i)
        for t in range(3):
            pair_dve(KF - 3 + t, KF - 3 + t, UNITS - 20, 4 * t)
        dve.wait_ge(dn_done, KD * (ROUNDS - 1))
        down_dve(ROUNDS - 1, UNITS - 20, 12)
        dve.wait_ge(w_used, UNITS - 8)
        v.memset(accl[:], 0.0).then_inc(acc_zero, 1)
        dve.wait_ge(acc_zero, 3)
        with dve.Fori(0, KD // 2) as i:
            for t in range(2):
                dve.wait_ge(y_sq, 2 * i + t + 1)
                dve.wait_ge(y_acc, 2 * i + t)
                v.tensor_tensor(accl[:], accl[:], sql[:, t, :], ALU.add).then_inc(y_acc, 1)
        dve.wait_ge(sq_root, 4)
        v.reciprocal(R[:], R[:]).then_inc(R_ready, 1)
        dve.wait_ge(R_ready, 4)
        for q in range(4):
            dve.wait_ge(hr_landed[q], 16)
            with dve.Fori(0, 4) as i:
                k = 4 * q + i
                yk = y[:, bass.ds(k, 1), :].rearrange("p a n -> p (a n)")
                v.tensor_tensor(yk, yk, R[:], ALU.mult).then_inc(y_tmp, 1)
                dve.wait_ge(y_tmp, k + 1)
                v.scalar_tensor_tensor(out=yk, in0=yk, scalar=cs[:, bass.ds(C_LAST + k, 1)],
                                       in1=hres[:, bass.ds(k, 1), :].rearrange("p a n -> p (a n)"),
                                       op0=ALU.mult, op1=ALU.add).then_inc(y_done, 1)

    @block.tensor
    def _(pe):
        pe.wait_ge(ready, 2)
        for k in range(KD):
            pe.wait_ge(x_sq, k + 1)
            for n in range(2):
                m = te.matmul(pb[:, 6 + n, 0:TH], ones[:], sq0[:, k % 2, n * TH:(n + 1) * TH],
                              start=(k == 0), stop=(k == KD - 1))
            m.then_inc(x_ssq_mm, 1)
        with pe.Fori(0, H) as j:
            pe.wait_ge(q_evac, j)
            tile_mm(0, U_QK, 0, 4, j, x_lo)
            pe.wait_ge(k_evac, j)
            tile_mm(2, U_QK, 2, 4, j)
        pe.wait_ge(q_evac, H)
        pe.wait_ge(k_evac, H)
        pe.wait_ge(sq_root, 1)
        with pe.Fori(0, H // 2) as i:
            pe.wait_ge(v_evac, 2 * i)
            for t in range(2):
                tile_mm(2 * t, U_V, 2 * t, 4, i)
            for t in range(2):
                pe.wait_ge(v_evac, 2 * i + t + 1)
                pe.wait_ge(vt_evac, 2 * i)
                for b4 in range(4):
                    te.transpose(pb[:, 4 + t, b4 * P:(b4 + 1) * P], zt[t][:, b4 * P:(b4 + 1) * P], ident[:])
                te.transpose(pb[0:NS, 6 + t, 0:P], zt[t][:, SEQ:T], ident[:]).then_inc(vT_ready, 1)
        pe.wait_ge(v_evac, H)
        pe.wait_ge(vt_evac, H)

        with pe.Fori(0, DB) as j:
            def unit(c):
                m = unit_mm(0, U_HEADS, c, xh, xl, 8 * (c % 2), 8, c % 2 == 0, c % 2 == 1, per=4, j=j)
                m.then_inc(w_used, 1)

            def scores(out, h, rhs):
                r = 32 * (h // 2)
                return te.matmul(out[r:r + 32], qb[:, h, :], rhs, start=(h % 2 == 0), stop=(h % 2 == 1))

            def k_pages(g_):
                slot = 4 * (g_ % 2)
                pe.wait_ge(s["st_copied"], 4 * j + max(0, g_ - 1))
                if g_ < 2:
                    pe.wait_ge(s["a_done"], j)
                pe.wait_ge(pg_landed[g_ % 2], 256 * j + 64 * (g_ // 2 + 1))
                for y in range(2):
                    for h in range(y, H, 2):
                        m = scores(pb[:, 2 + g_ % 2, :], h, pg[:, slot:slot + 4, h * P:(h + 1) * P])
                m.then_inc(pg_used[g_ % 2], 1)

            def p_scores(g_):
                n = (g_ + 1) * P
                if g_ == 0:
                    pe.wait_ge(hq_landed, 32 * j + 32)
                    pe.wait_ge(s["po_copied"], j)
                    pe.wait_ge(s["osb_ready"], j)
                pe.wait_ge(s["pexp_done"], 8 * j + 2 * g_)
                te.matmul(pb[:, 6, 0:n], qT[0:DH, g_ * P:n], kT[0:DH, 0:n], start=True, stop=True)
                te.matmul(pb[:, 7, 0:n], qT[DH:P, g_ * P:n], kT[DH:P, 0:n], start=True, stop=True
                          ).then_inc(s["pscore_ready"], 1)

            def w_turn(g_):
                o = g_ * (g_ + 1) // 2 * P
                pe.wait_ge(s["pw_done"], 4 * j + g_ + 1)
                if g_ < 2:
                    pe.wait_ge(s["ssd_done"], j)
                elif g_ == 2:
                    pe.wait_ge(s["wT_copied"], 4 * j + 1)
                else:
                    pe.wait_ge(s["sT_copied"], 5 * j + 1)
                for kb in range(g_ + 1):
                    m = te.transpose(pb[:, 4 + g_ % 2, kb * P:(kb + 1) * P], W[:, o + kb * P:o + (kb + 1) * P],
                                     ident[:])
                m.then_inc(s["wT_ready"], 1)

            def s_turn(g_):
                pe.wait_ge(s["sexp"], 5 * j + g_ + 1)
                for i in range(4):
                    o = SEQ * g_ + i * P
                    m = te.transpose(pb[:, 4 + (g_ + 1) % 2, i * P:(i + 1) * P], S[:, o:o + P], ident[:])
                m.then_inc(s["sT_ready"], 1)

            def v_pages(g_):
                slot = 4 * (g_ % 2)
                pe.wait_ge(s["sT_copied"], 5 * j + g_ + 1)
                pe.wait_ge(pg_landed[g_ % 2], 256 * j + 64 * (g_ // 2 + 3))
                for i in range(4):
                    o = SEQ * g_ + i * P
                    for y in range(4):
                        m = te.matmul(pb[32 * y:32 * y + 32, 7, 0:2 * P], S[:, o + 32 * y:o + 32 * y + 32],
                                      pg[:, slot + i, 2 * P * y:2 * P * (y + 1)], start=(g_ == 0 and i == 0),
                                      stop=False)
                m.then_inc(pg_used[g_ % 2], 1)

            pe.wait_ge(sq_landed, 32 * j + 32)
            k_pages(0)
            p_scores(0)
            pe.wait_ge(s["psd_done"], j)
            unit(0)
            k_pages(1)
            p_scores(1)
            unit(1)
            k_pages(2)
            p_scores(2)
            w_turn(0)
            pe.wait_ge(s["u_evac"], j + 1)
            unit(2)
            k_pages(3)
            p_scores(3)
            pe.wait_ge(s["st_copied"], 4 * j + 3)
            for y in range(2):
                for h in range(y, H, 2):
                    m = scores(pb[:, 2, 0:DT], h, knew[:, h, :])
            m.then_inc(s["snew_ready"], 1)
            w_turn(1)
            unit(3)
            w_turn(2)
            pe.wait_ge(s["wT_copied"], 4 * j + 2)
            s_turn(0)
            pe.wait_ge(s["wT_copied"], 4 * j + 3)
            s_turn(1)
            w_turn(3)
            pe.wait_ge(s["wT_copied"], 4 * j + 4)
            s_turn(2)
            pe.wait_ge(s["sT_copied"], 5 * j + 2)
            s_turn(3)
            pe.wait_ge(s["sexp"], 5 * j + 5)
            pe.wait_ge(s["sT_copied"], 5 * j + 3)
            te.transpose(pb[0:DT, 5, 0:P], S[:, PAGES * P:], ident[:]).then_inc(s["sT_ready"], 1)
            v_pages(0)
            v_pages(1)
            pe.wait_ge(s["vsq_ready"], j + 1)
            for n in range(2):
                m = te.matmul(pb[:, 2 + n, 0:TH], ones[:], vq[:, n * TH:(n + 1) * TH], start=True, stop=True)
            m.then_inc(s["vssq_ready"], 1)
            v_pages(2)
            pe.wait_ge(s["va_norm"], j + 1)
            for b4 in range(4):
                te.transpose(pb[:, 2, b4 * P:(b4 + 1) * P], vaT[:, b4 * P:(b4 + 1) * P], ident[:])
            te.transpose(pb[0:NS, 3, 0:P], vaT[:, SEQ:T], ident[:]).then_inc(s["vaT_ready"], 1)
            pe.wait_ge(s["wT_copied"], 4 * j + 4)
            pe.wait_ge(hv_landed, 16 * j + 16)
            for g_ in range(4):
                o = g_ * (g_ + 1) // 2 * P
                for kb in range(g_ + 1):
                    m = te.matmul(pb[:, 6, g_ * P:(g_ + 1) * P], V[:, kb, :], wT[:, o + kb * P:o + (kb + 1) * P],
                                  start=(kb == 0), stop=(kb == g_))
            m.then_inc(s["pv_ready"], 1)
            pe.wait_ge(s["vtok_copied"], 2 * j + 2)
            pe.wait_ge(s["ws_masked"], 2 * j + 2)
            for b4 in range(4):
                te.matmul(pb[:, 2, b4 * P:(b4 + 1) * P], vtok[:, b4, :], ws[:], start=True, stop=True)
            te.matmul(pb[:, 3, P:P + NS], vtok[0:NS, 4, :], wb[:], start=True, stop=True
                      ).then_inc(s["gm_ready"], 1)
            pe.wait_ge(sv_landed, 16 * j + 16)
            pe.wait_ge(s["sT_copied"], 5 * j + 5)
            v_pages(3)
            for y in range(4):
                m = te.matmul(pb[32 * y:32 * y + 32, 7, 0:2 * P], En[:, 32 * y:32 * y + 32],
                              vnew[:, 2 * P * y:2 * P * (y + 1)], start=False, stop=True)
            m.then_inc(s["spv_ready"], 1)
            pe.wait_ge(s["posq"], j + 1)
            pe.wait_ge(s["va_evac"], j + 1)
            te.matmul(pb[:, 0, :], ones[:], E2[:], start=True, stop=True).then_inc(s["pss_ready"], 1)
            pe.wait_ge(s["osb_ready"], j + 1)
            for z in range(2):
                m = te.transpose(pb[:, 4, z * P:(z + 1) * P], osb[:, z * P:(z + 1) * P], ident[:])
            m.then_inc(s["oT_ready"], 1)
            pe.wait_ge(s["ssq_ready"], j + 1)
            te.matmul(pb[:, 5, 0:NS], ones[:], osq[:], start=True, stop=True).then_inc(s["sss_ready"], 1)

        pe.wait_ge(s["psd_done"], DB)
        pe.wait_ge(s["a_done"], DB)
        with pe.Fori(0, KD // 2) as i:
            for t in range(2):
                pe.wait_ge(m_copied[t], i)
                tile_mm(2 * t, U_OUT, 2 * t, 4, i, m_lo if t == 0 else None)

        def sum_squares(a, bank):
            for n in range(2):
                m = te.matmul(pb[:, bank + n, 0:TH], ones[:], a[:, n * TH:(n + 1) * TH], start=True, stop=True)
            m.then_inc(ssq_mm, 1)

        pe.wait_ge(m_acc, KD)
        pe.wait_ge(s["ssd_done"], DB)
        sum_squares(acc, 4)
        pe.wait_ge(h_acc, KD)
        sum_squares(acc, 6)
        pe.wait_ge(m_copied[0], KD // 2)
        pe.wait_ge(m_copied[1], KD // 2)

        def pair_pe(n, base, c, per=0, i=0, k_sem=None):
            for t in range(2):
                pe.wait_ge(up_evac[t], n)
                tile_mm(2 * t, base, c + 2 * t, per, i, k_sem)

        def down_pe(r, base, c, per=0, i=0):
            pe.wait_ge(g_lo, GRP * r + GRP)
            for mm in range(KD // 2):
                for a in range(2):
                    m = 2 * mm + a
                    pe.wait_ge(dn_done, KD * r + (m - 1 if m >= 2 else 0))
                    ins = unit_mm(4 + 2 * a, base, c + mm, gh, gl, 0, GRP, True, True, col=a * GRP * P,
                                  per=per, j=i)
                    ins.then_inc(w_used if a else dn_even, 1)

        pair_pe(0, U_FFN, 0, k_sem=h_lo)
        pe.wait_ge(sq_root, 3)
        with pe.Fori(0, ROUNDS - 1) as i:
            for t in range(4):
                pair_pe(GRP * i + 1 + t, U_FFN + 4, 4 * t, 24, i)
            down_pe(i, U_FFN + 4, 16, 24, i)
        for t in range(3):
            pair_pe(KF - 3 + t, UNITS - 20, 4 * t)
        down_pe(ROUNDS - 1, UNITS - 20, 12)
        pe.wait_ge(y_acc, KD)
        pe.wait_ge(up_evac[0], KF)
        sum_squares(accl, 0)

    block.__exit__(None, None, None)


_OUTS = [((P, KD, T), "y"), ((H, P, T), "k"), ((H, 4, P, P), "v"), ((NS, H, P), "vs"), ((H, P, NS), "va"),
         ((P, 2 * KF, 18), "hist")]


def _tiles(w):
    return w.reshape(w.shape[0] // P, P, w.shape[1] // P, P).transpose(2, 0, 1, 3)


def _units(tiles):
    n = tiles.shape[0]
    return tiles.reshape(n, 2, 8, P, P).transpose(0, 1, 3, 2, 4).reshape(2 * n, P, UNIT)


def _weights(w_in, w_out, w_up, w_down):
    w = _tiles(w_in)
    parts = [_units(w[[o + h for h in range(H) for o in (16, 24)]]), _units(w[32:40]),
             _units(w[[o + h for h in range(H) for o in (0, 8)]]), _units(_tiles(w_out))]
    up = _tiles(w_up)
    pairs = [_units(up[[p, KF + p]]) for p in range(KF)]
    dn = _tiles(w_down).reshape(KD // 2, 2, ROUNDS, GRP, P, P).transpose(2, 0, 4, 1, 3, 5)
    dn = dn.reshape(ROUNDS, KD // 2, P, UNIT)
    parts.append(pairs[0])
    for r in range(ROUNDS - 1):
        parts += pairs[GRP * r + 1:GRP * r + 5] + [dn[r]]
    parts += pairs[KF - 3:] + [dn[ROUNDS - 1]]
    return np.concatenate(parts).reshape(UNITS * P, UNIT)


def _feature_major(prompt, sample):
    x = np.concatenate([prompt, sample]).T
    return x.reshape(x.shape[0] // P, P, T).transpose(1, 0, 2)


def kernel(**inputs):
    import concourse.bacc as _bacc
    from concourse.bass_utils import run_bass_kernel_spmd as _run

    i = {k: np.asarray(a) for k, a in inputs.items()}
    col = lambda a: a.reshape(-1, P).T
    wb = np.zeros((H, DB, DT, DB, DT), np.float32)
    wst = i["w_s"][0].transpose(0, 2, 1)
    for b in range(DB):
        wb[:, b, :, b, :] = wst[:, 0:DT, 0:DT]
    row = np.arange(P)
    row_consts = np.concatenate([np.where(np.arange(DT)[None] > row[:, None] % DT, NEG, 0.0),
                                 (row[:, None] // DT % 2 == np.arange(2)[None])], axis=1).astype(np.float32)
    lay = {
        "xT": _feature_major(i["x_prompt"][0], i["x_sample"].reshape(NS, D)),
        "wstream": _weights(i["w_in"][0], i["w_out"][0], i["w_up"][0], i["w_down"][0]),
        "kpages": i["cache_k"][0].transpose(0, 3, 2, 1).reshape(N_PHYS, P, H * P),
        "vpages": i["cache_v"][0].reshape(N_PHYS, P, H * P),
        "state": i["state_conv"][0].reshape(DB * 2, 2 * KF, P).transpose(2, 1, 0),
        "ptab": i["page_table"].reshape(1, DB * PAGES),
        "consts": np.concatenate([col(i["g_pre_mix"]), col(i["g_post_mix"]), col(i["g_pre_ffn"]),
                                  col(i["g_post_ffn"]), i["g_v_a"][0].T, col(i["g_subln"]), col(i["b_conv"]),
                                  col(i["w_conv"][0]), row_consts], axis=1),
        "lams": np.stack([i[n][0] for n in ("lam_q1", "lam_k1", "lam_q2", "lam_k2")])[None],
        "wsT": wst,
        "wblk": wb.reshape(H, NS, NS),
        "bs": i["b_s"][0],
    }
    nc = _bacc.Bacc("TRN2", target_bir_lowering=False, num_devices=1)
    arrays, args = {}, []
    for name, x in lay.items():
        x = np.ascontiguousarray(x)
        arrays[f"in_{name}"] = x
        args.append(nc.dram_tensor(f"in_{name}", x.shape, mybir.dt.from_np(x.dtype), kind="ExternalInput").ap())
    for shape, name in _OUTS:
        args.append(nc.dram_tensor(f"out_{name}", shape, F32, kind="ExternalOutput").ap())
    build(nc, *args)
    r = _run(nc, [arrays], core_ids=[0]).results[0]
    y, k, v, vs, va, hist = (r[f"out_{name}"] for _, name in _OUTS)
    y = y.transpose(2, 1, 0).reshape(T, D)
    k = k.transpose(2, 0, 1)
    v = v.transpose(1, 2, 0, 3).reshape(SEQ, H, HD)
    hist = hist.transpose(2, 1, 0).reshape(18, 2 * FF)
    out = (y[:SEQ].reshape(1, SEQ, D), y[SEQ:].reshape(DB, DT, D),
           k[:SEQ].reshape(1, 1, SEQ, H, HD), v.reshape(1, 1, SEQ, H, HD), hist[:2].reshape(1, 1, 2, 2 * FF),
           k[SEQ:].reshape(1, DB, DT, H, HD), vs.reshape(1, DB, DT, H, HD), hist[2:].reshape(1, DB, 2, 2 * FF),
           va.transpose(2, 0, 1).reshape(1, DB, DT, H, HD))
    return tuple(np.ascontiguousarray(a) for a in out)
```

```python
import numpy as np

import concourse.bass as bass
from concourse import mybir

P = 128
ALU = mybir.AluOpType
ACT = mybir.ActivationFunctionType
AX = mybir.AxisListType
F32 = mybir.dt.float32
F32R = mybir.dt.float32r
I32 = mybir.dt.int32

D = 2048
SEQ = 512
DB, DT = 8, 8
NS = DB * DT
T = SEQ + NS
TH = T // 2
KD = D // P
H = 8
HD = 128
DH = HD // 2
PAGES = 16
N_PHYS = 160
FF = 5632
KF = FF // P
GRP = 4
ROUNDS = KF // GRP
EPS = 1e-6
SCALE = DH ** -0.5
LAM_INIT = 0.8 - 0.6
NEG = -1.0e30

UNIT = 1024
RAW = 2
HL = 4
U_QK, U_V, U_HEADS, U_OUT, U_FFN = 0, 32, 48, 80, 112
UNITS = U_FFN + 2 * 2 * KF + KF * KD // 8
X_PARTS = ((0, 2), (2, 4), (4, 8), (8, 12), (12, 16))
MIX_ORDER = [*range(H - 1), *range(H, KD - 1), H - 1, KD - 1]
MIX_PARTS = ((0, H - 1, True, 0, 16), (H - 1, KD - 2, False, 1, 32), (KD - 2, KD - 1, False, 2, 16),
             (KD - 1, KD, False, 3, 32))
FIRST_UNITS = {1: 1, 3: 2}
POOL_H = (3, 7, 11, 15)
POOL_Y = range(2, KD, 3)
SSQ_COL = 256
PSLOTS = 8
C_PRE, C_POST, C_FFN, C_LAST = 0, 16, 32, 48
C_VA, C_SUB, C_B, C_W = 64, 72, 73, 73 + 2 * KF
C_MASK = C_W + 3 * 2 * KF
C_SEL = C_MASK + DT
C_ALL = C_SEL + 2
UB = 2 + SEQ + DB * (2 + DT)
NC_ = UB - 2


class Chain:

    def __init__(self, eng, sem, base, per=0, j=0):
        self.eng, self.sem, self.base, self.per, self.j, self.c = eng, sem, base, per, j, 0

    def link(self, ins):
        self.c += 1
        ins.then_inc(self.sem, 1)
        self.eng.wait_ge(self.sem, self.base + self.c + (self.per * self.j if self.per else 0))

    def close(self, n):
        assert self.c == n, (self.c, n)


def build(nc, xT, wstream, kpages, vpages, state, ptab, consts, lams, wsT, wblk, bs,
          y_out, k_out, v_out, vs_out, va_out, hist_out):
    zq_d = nc.dram_tensor("zq_d", (H, P, T), F32, kind="Internal").ap()
    qs_d = nc.dram_tensor("qs_d", (P, DB, H * 32), F32, kind="Internal").ap()
    ks_d = nc.dram_tensor("ks_d", (P, DB, H * DT), F32, kind="Internal").ap()
    mix_d = nc.dram_tensor("mix_d", (P, KD, T), F32, kind="Internal").ap()
    h_d = nc.dram_tensor("h_d", (P, KD, T), F32, kind="Internal").ap()

    top = [16512]

    def sb(name, shape, dt=F32, at=None):
        size = int(np.prod(shape[1:])) * 4
        size = (size + 31) // 32 * 32
        if at is None:
            off = top[0]
            top[0] += size
        else:
            off = at[0]
            at[0] += size
            at[1] = max(at[1], at[0])
        return nc.alloc_sbuf_tensor_at(name, shape, dt, offset=off)

    xh_at = top[0]
    xh = sb("xh", [P, KD, T], F32R)
    xl = sb("xl", [P, KD, T], F32R)
    wraw = sb("wraw", [P, RAW, UNIT])
    wh = sb("wh", [P, HL, UNIT], F32R)
    wl = sb("wl", [P, HL, UNIT], F32R)
    cs = sb("cs", [P, C_ALL])
    ident = sb("ident", [P, P])
    ones = sb("ones", [P, P])
    R = sb("R", [P, T])
    neglam = sb("neglam", [P, 1])
    gsub = sb("gsub", [P, 1])
    sgn = sb("sgn", [P, 1])
    lt = sb("lt", [P, 4])
    ptab_sb = sb("ptab_sb", [1, DB * PAGES], I32)
    free0 = top[0]

    a = [free0, 0]
    xraw = sb("xraw", [P, KD, T], at=a)
    lamin = sb("lamin", [P, 4, DH], at=a)
    sq0 = sb("sq0", [P, 2, T], at=a)
    acc0 = sb("acc0", [P, T], at=a)
    b = [a[0], a[0]]
    b_at = b[0]
    zt = [sb(f"zt{i}", [P, T], at=b) for i in range(2)]
    vt = [sb(f"vt{i}", [P, 5, P], at=b) for i in range(2)]
    qbd = sb("qbd", [P, DB, H, 32], at=b)
    kns = sb("kns", [P, DB, H, DT], at=b)

    c = [free0, 0]
    pg = sb("pg", [P, PSLOTS, H * P], at=c)
    qT = sb("qT", [P, SEQ], at=c)
    kT = sb("kT", [P, SEQ], at=c)
    qb = sb("qb", [P, H, 32], at=c)
    knew = sb("knew", [P, H, DT], at=c)
    loaded_early = c[0]
    V = sb("V", [P, 4, P], at=c)
    vnew = sb("vnew", [DT, H * P], at=c)
    ws = sb("ws", [P, P], at=c)
    wb = sb("wb", [NS, NS], at=c)
    bsb = sb("bsb", [P, P], at=c)
    S = sb("S", [P, PAGES * P + DT], at=c)
    En = sb("En", [DT, P], at=c)
    W = sb("W", [P, 1280], at=c)
    E2 = sb("E2", [P, SEQ], at=c)
    wT = sb("wT", [P, 1280], at=c)
    vg = sb("vg", [P, T], at=c)
    vq = sb("vq", [P, T], at=c)
    vaT = sb("vaT", [P, T], at=c)
    ug = sb("ug", [P, T], at=c)
    ao = sb("ao", [P, T], at=c)
    po = sb("po", [P, SEQ], at=c)
    vtok = sb("vtok", [P, 5, P], at=c)
    bsmp = sb("bsmp", [P, H, NS], at=c)
    osb = sb("osb", [P, 2 * P], at=c)
    oT = sb("oT", [P, 2 * P], at=c)
    osm = sb("osm", [P, NS], at=c)
    osq = sb("osq", [P, NS], at=c)
    pmx = sb("pmx", [P, 2], at=c)
    pneg = sb("pneg", [P, 2], at=c)
    psm = sb("psm", [P, 8], at=c)
    prs = sb("prs", [P, 2], at=c)
    pr4 = sb("pr4", [P, 4], at=c)
    vr = sb("vr", [P, 5], at=c)
    pon = sb("pon", [P, 4, P], at=c)
    mx4 = sb("mx4", [P, 5], at=c)
    mx = sb("mx", [P, 1], at=c)
    nmx = sb("nmx", [P, 1], at=c)
    ssm = sb("ssm", [P, 5], at=c)
    rs = sb("rs", [P, 2], at=c)
    maskd = sb("maskd", [P, P], at=c)

    d = [free0, 0]
    area1 = d[0]
    xres = sb("xres", [P, KD, T], at=d)
    early = nc.alloc_sbuf_tensor_at("early", [P, H - 1, T], F32, offset=free0)
    assert (H - 1) * T <= PSLOTS // 2 * H * P
    area2 = d[0]
    mix = sb("mix", [P, KD, T], at=d)
    sqt = sb("sqt", [P, 2, T], at=d)
    acc = sb("acc", [P, T], at=d)
    y = nc.alloc_sbuf_tensor_at("y", [P, KD, T], F32, offset=area1)
    f = [area2, 0]
    gh = sb("gh", [P, GRP, T], F32R, at=f)
    gl = sb("gl", [P, GRP, T], F32R, at=f)
    ub = [sb(f"ub{i}", [P, UB], at=f) for i in range(2)]
    cv = [sb(f"cv{i}", [P, UB], at=f) for i in range(2)]
    gv = sb("gv", [P, T], at=f)
    st = sb("st", [P, 2 * KF, 16], at=f)
    hs = sb("hs", [P, 2 * KF, 18], at=f)
    hres = nc.alloc_sbuf_tensor_at("hres", [P, KD, T], F32, offset=xh_at)
    g = [xh_at + KD * T * 4, 0]
    sql = sb("sql", [P, 2, T], at=g)
    accl = sb("accl", [P, T], at=g)
    assert loaded_early <= b_at
    for z in (a, b, c, d, f):
        assert z[1] <= 229344, z

    pb = nc.alloc_psum_tensor("pb", [P, 8, 512], F32)

    def sem(name):
        return nc.alloc_semaphore(name)

    w_landed = [sem(f"w_landed{i}") for i in range(RAW)]
    w_hi, w_lo, w_used = sem("w_hi"), sem("w_lo"), sem("w_used")
    c_landed, p_landed, ready = sem("c_landed"), sem("p_landed"), sem("consts_ready")
    x_landed = [sem(f"x_landed{i}") for i in range(len(X_PARTS))]
    x_sq, x_hi, x_lo, x_acc = sem("x_sq"), sem("x_hi"), sem("x_lo"), sem("x_acc")
    sq_root, R_ready = sem("sq_root"), sem("R_ready")
    dve_c, pool_c, lam_sum, lam_exp = sem("dve_chain"), sem("pool_chain"), sem("lam_sum"), sem("lam_exp")
    q_evac, k_evac, smp = sem("q_evac"), sem("k_evac"), sem("sample_cols")
    q_stored, k_stored, s_stored = sem("q_stored"), sem("k_stored"), sem("sample_stored")
    v_evac, vT_ready, vt_evac = sem("v_evac"), sem("vT_ready"), sem("vt_evac")
    v_stored = [sem("v_stored0"), sem("v_stored1")]
    pg_landed = [sem(f"pages_landed{i}") for i in range(PSLOTS // 2)]
    pg_used = sem("pages_used")
    hq_landed, sq_landed, hv_landed, sv_landed, g_landed = (sem(x) for x in (
        "head_qk_landed", "sample_q_landed", "head_v_landed", "sample_v_landed", "gmlp_landed"))
    names_h = ("st_copied s_max pscore_ready pexp_done pneg_ready pw_done snew_ready snew_masked nmx_ready "
               "sexp sT_ready sT_copied wT_ready wT_copied u_evac ugelu va_evac vgelu vsq_ready vssq_ready "
               "vsd_done va_gained vaT_ready vtok_copied ws_masked spv_ready osb_ready oT_ready pv_ready "
               "posq psd_done pon_ready poT_ready ssq_ready sss_ready ssd_done gm_ready ao_prompt "
               "ao_sample a_done b_done bs_done va_stored a_stored b_stored").split()
    s = {n: sem(n) for n in names_h}
    m_landed = [sem(f"mix_landed{i}") for i in range(4)]
    m_hi, m_lo, m_acc, acc_zero = (sem(x) for x in (
        "mix_hi", "mix_lo", "out_acc", "acc_zero"))
    m_copied = [sem(f"out_copied{t}") for t in range(2)]
    m_sq = [sem(f"out_sq{t}") for t in range(2)]
    r_landed = [sem(f"res_landed{i}") for i in range(4)]
    hp_tmp = sem("h_scaled_pool")
    h_tmp, h_done, h_hi, h_lo, h_sq, h_acc, h_stored = (sem(x) for x in (
        "h_scaled", "h_done", "h_hi", "h_lo", "h_sq", "h_acc", "h_stored"))
    st_landed, st_in, hist_cp, tap, tap1, cv_done, gelu_done, gv_done, g_hi, g_lo = (sem(x) for x in (
        "state_landed", "state_in", "hist_out", "tap2_done", "tap1_done", "conv_done",
        "gelu_done", "gv_done", "g_hi", "g_lo"))
    up_evac = [sem("gate_evac"), sem("value_evac")]
    ub_zero = sem("prompt_history_zero")
    dn_even, dn_done, hist_stored = sem("down_even_ready"), sem("down_added"), sem("hist_stored")
    hr_landed = [sem(f"hr_landed{i}") for i in range(4)]
    y_sq, y_gain, y_tmp, y_acc, y_done, y_stored, ssq_mm = (sem(x) for x in (
        "y_sq", "y_gain", "y_scaled", "y_acc", "y_done", "y_stored", "ssq_mm"))
    yp_tmp, yp_done = sem("y_scaled_pool"), sem("y_done_pool")

    v, sc, pl, te, sy = nc.vector, nc.scalar, nc.gpsimd, nc.tensor, nc.sync

    def halves(ap):
        return ap.rearrange("p (c n) -> p c n", c=2)

    def w_load(base, c, per=0, j=0):
        u = base + c
        sy.wait_ge(w_lo, u + 4 + (per * j if per else 0))
        off = (u + 5) * P + (per * P * j if per else 0)
        slot = (c + 5) % RAW
        sy.dma_start(wraw[:, slot, :], wstream[bass.ds(off, P), :]).then_inc(w_landed[slot], 16)

    def w_split_hi(base, c, per=0, j=0):
        u = base + c
        sc.wait_ge(w_landed[c % RAW], 16 * ((u + 4) // RAW + 1) + (16 * (per // RAW) * j if per else 0))
        sc.wait_ge(w_used, u + 1 + (per * j if per else 0))
        sc.activation(wh[:, c % HL, :], wraw[:, c % RAW, :], ACT.Copy).then_inc(w_hi, 1)

    def w_split_lo(base, c, per=0, j=0):
        pl.wait_ge(w_hi, base + c + 5 + (per * j if per else 0))
        pl.tensor_tensor(wl[:, c % HL, :], wraw[:, c % RAW, :], wh[:, c % HL, :].bitcast(F32),
                         ALU.subtract).then_inc(w_lo, 1)

    def unit_mm(bank, base, c, hi, lo, k0, nk, first, last, col=0, per=0, j=0, k_sem=None):
        te.wait_ge(w_lo, base + c + 1 + (per * j if per else 0))
        slot = c % HL
        for kt in range(nk):
            if k_sem is not None:
                te.wait_ge(k_sem, k0 + kt + 1)
            whk = wh[:, slot, col + kt * P:col + (kt + 1) * P]
            wlk = wl[:, slot, col + kt * P:col + (kt + 1) * P]
            a0, z0 = first and kt == 0, last and kt == nk - 1
            for n in range(2):
                te.matmul(pb[:, bank + n, 0:TH], whk, hi[:, k0 + kt, n * TH:(n + 1) * TH], start=a0, stop=False)
            for n in range(2):
                te.matmul(pb[:, bank + n, 0:TH], whk, lo[:, k0 + kt, n * TH:(n + 1) * TH], start=False, stop=False)
            for n in range(2):
                m = te.matmul(pb[:, bank + n, 0:TH], wlk, hi[:, k0 + kt, n * TH:(n + 1) * TH],
                              start=False, stop=z0)
        return m

    def tile_mm(bank, base, c, per=0, j=0, k_sem=None):
        unit_mm(bank, base, c, xh, xl, 0, 8, True, False, per=per, j=j, k_sem=k_sem).then_inc(w_used, 1)
        unit_mm(bank, base, c + 1, xh, xl, 8, 8, False, True, per=per, j=j, k_sem=k_sem).then_inc(w_used, 1)

    def tile_done(eng, base, c, per=0, j=0):
        eng.wait_ge(w_used, base + c + 2 + (per * j if per else 0))

    def tile_out(bank):
        return pb[:, bank:bank + 2, 0:TH]

    def wait_past(eng, sem_, n):
        if type(n) is not int or n > 0:
            eng.wait_ge(sem_, n)

    block = nc.Block().__enter__()

    @block.sync
    def _(sp):
        def first_load(u):
            if u >= RAW:
                sp.wait_ge(w_lo, u - RAW + 1)
            sp.dma_start(wraw[:, u % RAW, :], wstream[u * P:(u + 1) * P, :]).then_inc(w_landed[u % RAW], 16)

        first_load(0)
        for q, (k0, k1) in enumerate(X_PARTS):
            sp.dma_start(xraw[:, k0:k1, :], xT[:, k0:k1, :]).then_inc(x_landed[q], 16)
            if q == 0:
                sp.dma_start(cs[:], consts).then_inc(c_landed, 16)
                sp.dma_start(lamin[:], lams.to_broadcast([P, 4, DH])).then_inc(c_landed, 16)
            if q in FIRST_UNITS:
                first_load(FIRST_UNITS[q])
        for u in (3, 4):
            first_load(u)

        with sp.Fori(0, H) as j:
            w_load(U_QK, 0, 4, j)
            w_load(U_QK, 1, 4, j)
            sp.wait_ge(q_evac, j + 1)
            sp.dma_start(zq_d[bass.ds(j, 1)].rearrange("a p n -> (a p) n"), zt[0][:]).then_inc(q_stored, 16)
            w_load(U_QK, 2, 4, j)
            w_load(U_QK, 3, 4, j)
            sp.wait_ge(k_evac, j + 1)
            sp.dma_start(k_out[bass.ds(j, 1)].rearrange("a p n -> (a p) n"), zt[1][:]).then_inc(k_stored, 16)
        sp.wait_ge(smp, 3 * H)
        sp.dma_start(qs_d, qbd[:].rearrange("p b h n -> p b (h n)")).then_inc(s_stored, 16)
        sp.dma_start(ks_d, kns[:].rearrange("p b h n -> p b (h n)")).then_inc(s_stored, 16)

        def v_loads(i, first_page=None):
            for c in range(4):
                w_load(U_V, c, 4, i)
                if first_page is not None:
                    page(first_page + c, 0)
            for t in range(2):
                sp.wait_ge(vt_evac, 2 * i + t + 1)
                sp.dma_start(v_out[bass.ds(2 * i + t, 1)].rearrange("a b p n -> p (a b) n"),
                             vt[t][:, 0:4, :]).then_inc(v_stored[t], 16)
                sp.dma_start(vs_out[:, bass.ds(2 * i + t, 1), :].rearrange("p a n -> p (a n)"),
                             vt[t][0:NS, 4, :]).then_inc(v_stored[t], 16)

        def head_loads(j):
            wait_past(sp, s["pscore_ready"], 4 * j)
            sp.dma_start(qT[:], zq_d[bass.ds(j, 1), :, 0:SEQ].rearrange("a p n -> (a p) n")).then_inc(hq_landed, 16)
            sp.dma_start(kT[:], k_out[bass.ds(j, 1), :, 0:SEQ].rearrange("a p n -> (a p) n")).then_inc(hq_landed, 16)
            wait_past(sp, s["snew_ready"], j)
            sp.dma_start(qb[:].rearrange("p h n -> p (h n)"),
                         qs_d[:, bass.ds(j, 1), :].rearrange("p a n -> p (a n)")).then_inc(sq_landed, 16)
            sp.dma_start(knew[:].rearrange("p h n -> p (h n)"),
                         ks_d[:, bass.ds(j, 1), :].rearrange("p a n -> p (a n)")).then_inc(sq_landed, 16)

        def page(n, j):
            slot = n % PSLOTS
            phys = sp.value_load(ptab_sb[0:1, bass.ds(PAGES * j + n % PAGES, 1)], min_val=0, max_val=N_PHYS - 1)
            wait_past(sp, pg_used, 2 * PAGES * j + n - PSLOTS + 1)
            src = kpages if n < PAGES else vpages
            sp.dma_start(pg[:, slot, :], src[bass.ds(phys, 1)].rearrange("a p n -> (a p) n")
                         ).then_inc(pg_landed[slot // 2], 16)

        with sp.Fori(0, H // 4) as i:
            v_loads(i)
        sp.wait_ge(q_stored, 16 * H)
        sp.wait_ge(k_stored, 16 * H)
        sp.wait_ge(s_stored, 32)
        sp.wait_ge(p_landed, 16)
        v_loads(2, first_page=0)
        head_loads(0)
        v_loads(3, first_page=4)
        sp.wait_ge(v_stored[0], 16 * H)
        sp.wait_ge(v_stored[1], 16 * H)

        def batch_loads(j, last=False):
            for n in range(8, 12):
                page(n, j)
            w_load(U_HEADS, 0, 4, j)
            wait_past(sp, s["gm_ready"], j)
            wait_past(sp, s["ao_sample"], j)
            sp.dma_start(ws[:], wsT[bass.ds(j, 1)].rearrange("a p n -> (a p) n")).then_inc(g_landed, 16)
            sp.dma_start(wb[:], wblk[bass.ds(j, 1)].rearrange("a p n -> (a p) n")).then_inc(g_landed, 16)
            sp.dma_start(bsb[:], bs[bass.ds(j, 1), :].to_broadcast([P, P])).then_inc(g_landed, 16)
            wait_past(sp, s["pv_ready"], j)
            sp.dma_start(V[:], v_out[bass.ds(j, 1)].rearrange("a b p n -> p (a b) n")).then_inc(hv_landed, 16)
            wait_past(sp, s["spv_ready"], j)
            sp.dma_start(vnew[:], vs_out[bass.ds(DT * j, DT)].rearrange("t h n -> t (h n)")).then_inc(sv_landed, 16)
            for n in range(12, 24):
                page(n, j)
            for c in range(1, 3):
                w_load(U_HEADS, c, 4, j)
                for n in range(20 + 4 * c, 24 + 4 * c):
                    page(n, j)
            w_load(U_HEADS, 3, 4, j)
            if not last:
                head_loads(j + 1)
                for n in range(8):
                    page(n, j + 1)

        batch_loads(0)
        with sp.Fori(1, DB - 1) as j:
            batch_loads(j)
        batch_loads(DB - 1, last=True)

        sp.wait_ge(pg_used, 2 * PAGES * DB - 4)
        sp.wait_ge(s["a_stored"], 16 * (H - 1))
        sp.dma_start(early[:], mix_d[:, 0:H - 1, :]).then_inc(m_landed[0], 16)
        sp.wait_ge(w_used, U_OUT)
        sp.wait_ge(s["b_stored"], 16 * (H - 1))
        sp.dma_start(xl[:, H - 1:KD - 2, 0:SEQ].bitcast(F32), mix_d[:, H:KD - 1, 0:SEQ]).then_inc(m_landed[1], 16)
        sp.wait_ge(s["bs_done"], DB)
        sp.dma_start(xl[:, H - 1:KD - 2, SEQ:T].bitcast(F32), bsmp[:, 0:H - 1, :]).then_inc(m_landed[1], 16)
        sp.dma_start(xl[:, KD - 1, SEQ:T].bitcast(F32), bsmp[:, H - 1, :]).then_inc(m_landed[3], 16)
        sp.wait_ge(s["a_stored"], 16 * H)
        sp.dma_start(xl[:, KD - 2, :].bitcast(F32), mix_d[:, H - 1, :]).then_inc(m_landed[2], 16)
        sp.wait_ge(s["va_stored"], 16 * H)
        sp.wait_ge(s["b_stored"], 16 * H)
        sp.dma_start(xl[:, KD - 1, 0:SEQ].bitcast(F32), mix_d[:, KD - 1, 0:SEQ]).then_inc(m_landed[3], 16)
        sp.wait_ge(m_lo, KD)
        sp.wait_ge(s["spv_ready"], DB)
        for q in range(4):
            sp.dma_start(xres[:, 4 * q:4 * q + 4, :], xT[:, 4 * q:4 * q + 4, :]).then_inc(r_landed[q], 16)
        with sp.Fori(0, KD // 2) as i:
            for c in range(4):
                w_load(U_OUT, c, 4, i)
        for q in range(4):
            sp.wait_ge(h_done, 4 * q + 4)
            sp.dma_start(h_d[:, 4 * q:4 * q + 4, :], mix[:, 4 * q:4 * q + 4, :]).then_inc(h_stored, 16)
        sp.wait_ge(h_stored, 64)
        sp.wait_ge(h_lo, KD)
        sp.wait_ge(h_sq, KD)
        sp.wait_ge(h_hi, KD)
        sp.wait_ge(ssq_mm, 3)
        sp.dma_start(st[:], state).then_inc(st_landed, 16)

        for c in range(4):
            w_load(U_FFN, c)
        with sp.Fori(0, ROUNDS - 1) as i:
            for c in range(24):
                w_load(U_FFN + 4, c, 24, i)
        for c in range(20 - 5):
            w_load(UNITS - 20, c)
        sp.wait_ge(hist_cp, 2 * KF)
        sp.dma_start(hist_out, hs[:]).then_inc(hist_stored, 16)
        sp.wait_ge(w_used, UNITS - 8)
        for q in range(4):
            sp.dma_start(hres[:, 4 * q:4 * q + 4, :], h_d[:, 4 * q:4 * q + 4, :]).then_inc(hr_landed[q], 16)
        for k in range(0, KD, 2):
            sp.wait_ge(y_done, len([m for m in range(k + 2) if m not in POOL_Y]))
            wait_past(sp, yp_done, len([m for m in POOL_Y if m < k + 2]))
            sp.dma_start(y_out[:, k:k + 2, :], y[:, k:k + 2, :]).then_inc(y_stored, 16)
        sp.wait_ge(y_stored, 16 * KD // 2)
        sp.wait_ge(hist_stored, 16)

    @block.scalar
    def _(act):
        def first_split_hi(u):
            act.wait_ge(w_landed[u % RAW], 16 * (u // RAW + 1))
            sc.activation(wh[:, u, :], wraw[:, u % RAW, :], ACT.Copy).then_inc(w_hi, 1)

        first_split_hi(0)
        act.wait_ge(c_landed, 32)
        def x_squares(k0, k1):
            for k in range(k0, k1):
                wait_past(act, x_acc, k - 1)
                sc.activation(sq0[:, k % 2, :], xraw[:, k, :], ACT.Square).then_inc(x_sq, 1)

        for q, (k0, k1) in enumerate(X_PARTS):
            act.wait_ge(x_landed[q], 16)
            for k in range(k0, k1):
                sc.activation(xh[:, k, :], xraw[:, k, :], ACT.Copy, scale=cs[:, C_PRE + k:C_PRE + k + 1]
                              ).then_inc(x_hi, 1)
            if q:
                x_squares(*X_PARTS[q - 1])
            if q in FIRST_UNITS:
                first_split_hi(FIRST_UNITS[q])
            if q == 4:
                act.wait_ge(lam_sum, 2)
                sc.activation(lt[:, 2:4], lt[:, 0:2], ACT.Exp).then_inc(lam_exp, 1)
        first_split_hi(3)
        x_squares(*X_PARTS[-1])

        def qk_act(j):
            for t in range(2):
                w_split_hi(U_QK, 4 * t, 8, j)
                w_split_hi(U_QK, 4 * t + 1, 8, j)
                if type(j) is int and t == 0:
                    act.wait_ge(ssq_mm, 1)
                    sc.activation(halves(R[:]), tile_out(6), ACT.Sqrt, scale=1.0 / D, bias=EPS
                                  ).then_inc(sq_root, 1)
                act.wait_ge(q_evac, 2 * j + t + 1)
                act.wait_ge(pool_c, 2)
                for z in range(2):
                    o = 2 * DT * t + DT * z
                    sc.activation(
                        qbd[DH * z:DH * z + DH, :, bass.ds(2 * j + t, 1), o:o + DT].rearrange("p b a n -> p b (a n)"),
                        zt[0][DH * z:DH * z + DH, SEQ:T].rearrange("p (b n) -> p b n", b=DB),
                        ACT.Copy).then_inc(smp, 1)
                w_split_hi(U_QK, 4 * t + 2, 8, j)
                w_split_hi(U_QK, 4 * t + 3, 8, j)
                act.wait_ge(k_evac, 2 * j + t + 1)
                act.wait_ge(pool_c, 2)
                sc.activation(kns[:, :, bass.ds(2 * j + t, 1), :].rearrange("p b a n -> p b (a n)"),
                              zt[1][:, SEQ:T].rearrange("p (b n) -> p b n", b=DB), ACT.Copy).then_inc(smp, 1)

        qk_act(0)
        with act.Fori(1, H // 2) as j:
            qk_act(j)
        with act.Fori(0, H // 2) as i:
            for c in range(4):
                w_split_hi(U_V, c, 4, i)

        def batch(j):
            wait_past(act, s["spv_ready"], j)

            def copy_scores(g_):
                act.wait_ge(pg_used, 2 * PAGES * j + 4 * g_ + 4)
                sc.activation(S[:, SEQ * g_:SEQ * (g_ + 1)], pb[:, 2 + g_ % 2, :], ACT.Copy
                              ).then_inc(s["st_copied"], 1)

            def p_exp(g_):
                n = (g_ + 1) * P
                o = g_ * (g_ + 1) // 2 * P
                act.wait_ge(s["pneg_ready"], 4 * j + g_ + 1)
                wait_past(act, s["wT_ready"], 4 * j)
                sc.activation(W[:, o:o + n], pb[:, 6, 0:n], ACT.Exp, scale=SCALE, bias=pneg[:, 0:1],
                              accum_out=psm[:, 2 * g_:2 * g_ + 1]).then_inc(s["pexp_done"], 1)
                wait_past(act, s["pw_done"], 4 * j + g_)
                sc.activation(E2[:, 0:n], pb[:, 7, 0:n], ACT.Exp, scale=SCALE, bias=pneg[:, 1:2],
                              accum_out=psm[:, 2 * g_ + 1:2 * g_ + 2]).then_inc(s["pexp_done"], 1)

            def s_exp(g_):
                z = min(SEQ * (g_ + 1), PAGES * P + DT)
                sc.activation(S[:, SEQ * g_:z], S[:, SEQ * g_:z], ACT.Exp, scale=SCALE, bias=nmx[:, 0:1],
                              accum_out=ssm[:, g_:g_ + 1]).then_inc(s["sexp"], 1)

            for g_ in range(3):
                copy_scores(g_)
                p_exp(g_)
            w_split_hi(U_HEADS, 0, 4, j)
            copy_scores(3)
            act.wait_ge(s["nmx_ready"], j + 1)
            s_exp(0)
            s_exp(1)
            p_exp(3)
            act.wait_ge(s["nmx_ready"], j + 1)
            for g_ in range(2, 5):
                s_exp(g_)
            w_split_hi(U_HEADS, 1, 4, j)
            act.wait_ge(s["va_evac"], j + 1)
            sc.activation(vg[:], vg[:], ACT.Gelu_apprx_tanh).then_inc(s["vgelu"], 1)
            act.wait_ge(s["vgelu"], j + 1)
            sc.activation(vq[:], vg[:], ACT.Square).then_inc(s["vsq_ready"], 1)
            wait_past(act, s["vaT_ready"], j)
            act.wait_ge(c_landed, 32)
            sc.activation(vaT[:], vg[:], ACT.Copy, scale=cs[:, bass.ds(C_VA + j, 1)]).then_inc(s["va_gained"], 1)
            act.wait_ge(s["vssq_ready"], j + 1)
            sc.activation(vr[:, 0:4], pb[:, 3, SSQ_COL:SSQ_COL + 4], ACT.Sqrt, scale=1.0 / HD, bias=EPS
                          ).then_inc(s["vsd_done"], 1)
            sc.activation(vr[0:NS, 4:5], pb[0:NS, 3, SSQ_COL + 4:SSQ_COL + 5], ACT.Sqrt, scale=1.0 / HD, bias=EPS
                          ).then_inc(s["vsd_done"], 1)
            w_split_hi(U_HEADS, 2, 4, j)
            act.wait_ge(s["pv_ready"], j + 1)
            act.wait_ge(s["pw_done"], 4 * j + 4)
            for b4 in range(4):
                sc.activation(E2[:, b4 * P:(b4 + 1) * P], pb[:, 6, b4 * P:(b4 + 1) * P], ACT.Square,
                              accum_out=pr4[:, b4:b4 + 1]).then_inc(s["posq"], 1)
            act.wait_ge(s["posq"], 4 * j + 4)
            sc.activation(pr4[:], pr4[:], ACT.Sqrt, scale=1.0 / HD, bias=EPS).then_inc(s["psd_done"], 1)
            w_split_hi(U_HEADS, 3, 4, j)
            act.wait_ge(s["sss_ready"], j + 1)
            sc.activation(osq[:], pb[:, 4, 0:NS], ACT.Sqrt, scale=1.0 / HD, bias=EPS).then_inc(s["ssd_done"], 1)
            act.wait_ge(s["u_evac"], j + 1)
            sc.activation(ug[:], ug[:], ACT.Gelu_apprx_tanh).then_inc(s["ugelu"], 1)

        batch(0)
        with act.Fori(1, DB) as j:
            batch(j)

        act.wait_ge(w_used, U_OUT)

        for first, end, source, landed, count in MIX_PARTS:
            act.wait_ge(m_landed[landed], count)
            raw = early if source else xl
            with act.Fori(first, end) as k:
                rk = raw[:, bass.ds(k, 1), :].rearrange("p a n -> p (a n)")
                sc.activation(xh[:, bass.ds(k, 1), :].rearrange("p a n -> p (a n)"),
                              rk if source else rk.bitcast(F32), ACT.Copy).then_inc(m_hi, 1)

        def out_squares(i):
            for t in range(2):
                w_split_hi(U_OUT, 2 * t, 4, i)
                w_split_hi(U_OUT, 2 * t + 1, 4, i)
                act.wait_ge(m_copied[t], i + 1)
                wait_past(act, m_acc, 2 * i)
                act.wait_ge(c_landed, 32)
                sc.activation(sqt[:, t, :], mix[:, bass.ds(2 * i + t, 1), :].rearrange("p a n -> p (a n)"),
                              ACT.Square).then_inc(m_sq[t], 1)

        out_squares(0)
        with act.Fori(1, KD // 2) as i:
            out_squares(i)
        act.wait_ge(ssq_mm, 2)
        sc.activation(halves(R[:]), tile_out(4), ACT.Sqrt, scale=1.0 / D, bias=EPS).then_inc(sq_root, 1)

        def h_split(i):
            for t in range(2):
                wait_past(act, h_acc, 2 * i)
                act.wait_ge(h_done, 2 * i + t + 1)
                act.wait_ge(c_landed, 32)
                sc.activation(xh[:, bass.ds(2 * i + t, 1), :].rearrange("p a n -> p (a n)"),
                              mix[:, bass.ds(2 * i + t, 1), :].rearrange("p a n -> p (a n)"), ACT.Copy,
                              scale=cs[:, bass.ds(C_FFN + 2 * i + t, 1)]).then_inc(h_hi, 1)
                sc.activation(sqt[:, t, :], mix[:, bass.ds(2 * i + t, 1), :].rearrange("p a n -> p (a n)"),
                              ACT.Square).then_inc(h_sq, 1)

        h_split(0)
        with act.Fori(1, KD // 2) as i:
            h_split(i)
        act.wait_ge(ssq_mm, 3)
        act.wait_ge(h_lo, KD)
        sc.activation(halves(R[:]), tile_out(6), ACT.Sqrt, scale=1.0 / D, bias=EPS).then_inc(sq_root, 1)

        def conv_tap2(p, t, n):
            act.wait_ge(up_evac[t], n + 1)
            act.wait_ge(st_in, 2 * n + t + 1)
            wait_past(act, gv_done, n)
            act.wait_ge(c_landed, 32)
            f = p + KF * t
            sc.activation(cv[t][:, 0:NC_], ub[t][:, 2:UB], ACT.Identity, scale=cs[:, bass.ds(C_W + 4 * KF + f, 1)],
                          bias=cs[:, bass.ds(C_B + f, 1)]).then_inc(tap, 1)

        def pair_act(p, n, base, c, per=0, i=0):
            w_split_hi(base, c, per, i)
            w_split_hi(base, c + 1, per, i)
            conv_tap2(p, 0, n)
            act.wait_ge(cv_done, 2 * n + 1)
            sc.activation(cv[0][:, 0:NC_], cv[0][:, 0:NC_], ACT.Gelu_apprx_tanh).then_inc(gelu_done, 1)
            w_split_hi(base, c + 2, per, i)
            w_split_hi(base, c + 3, per, i)
            conv_tap2(p, 1, n)

        def g_split_hi(n, slot, groups):
            act.wait_ge(gv_done, n + 1)
            act.wait_ge(w_used, U_FFN + 4 + 24 * groups)
            sc.activation(gh[:, slot, :], gv[:], ACT.Copy).then_inc(g_hi, 1)

        pair_act(0, 0, U_FFN, 0)
        g_split_hi(0, 0, 0)
        with act.Fori(0, ROUNDS - 1) as i:
            for t in range(3):
                pair_act(GRP * i + 1 + t, GRP * i + 1 + t, U_FFN + 4, 4 * t, 24, i)
                g_split_hi(GRP * i + 1 + t, 1 + t, i)
            pair_act(GRP * i + 4, GRP * i + 4, U_FFN + 4, 12, 24, i)
            for c in range(16, 24):
                w_split_hi(U_FFN + 4, c, 24, i)
            g_split_hi(GRP * i + 4, 0, i + 1)
        for t in range(3):
            pair_act(KF - 3 + t, KF - 3 + t, UNITS - 20, 4 * t)
            g_split_hi(KF - 3 + t, 1 + t, ROUNDS - 1)
        for k in range(KD):
            if k % 2 and k < 8:
                w_split_hi(UNITS - 20, 12 + k // 2)
            act.wait_ge(dn_done, KD * (ROUNDS - 1) + k + 2)
            wait_past(act, y_acc, k - 1)
            sc.activation(sql[:, k % 2, :], y[:, k, :], ACT.Square).then_inc(y_sq, 1)
            if k in POOL_Y:
                sc.activation(y[:, k, :], y[:, k, :], ACT.Copy, scale=cs[:, C_LAST + k:C_LAST + k + 1]
                              ).then_inc(y_gain, 1)
        act.wait_ge(ssq_mm, 4)
        sc.activation(halves(R[:]), tile_out(0), ACT.Sqrt, scale=1.0 / D, bias=EPS).then_inc(sq_root, 1)

    @block.gpsimd
    def _(pool):
        pl.memset(ones[:], 1.0).then_inc(ready, 1)
        pl.memset(ident[:], 0.0).then_inc(pool_c, 1)
        pool.wait_ge(pool_c, 1)
        pl.affine_select(out=ident[:], in_=ident[:], compare_op=ALU.not_equal, fill=1.0, base=0,
                         pattern=[[-1, P]], channel_multiplier=1).then_inc(ready, 1)
        pool.wait_ge(w_hi, 1)
        pl.tensor_tensor(wl[:, 0, :], wraw[:, 0, :], wh[:, 0, :].bitcast(F32), ALU.subtract).then_inc(w_lo, 1)
        pool.wait_ge(w_hi, 2)
        pl.tensor_tensor(wl[:, 1, :], wraw[:, 1, :], wh[:, 1, :].bitcast(F32), ALU.subtract).then_inc(w_lo, 1)
        for u in range(2, 4):
            pool.wait_ge(w_hi, u + 1)
            pl.tensor_tensor(wl[:, u, :], wraw[:, u % RAW, :], wh[:, u, :].bitcast(F32),
                             ALU.subtract).then_inc(w_lo, 1)
        pl.memset(qbd[:], 0.0).then_inc(pool_c, 1)
        with pool.Fori(0, H) as j:
            for c in range(4):
                w_split_lo(U_QK, c, 4, j)
        pool.dma_start(ptab_sb[:], ptab).then_inc(p_landed, 16)
        with pool.Fori(0, H // 2) as i:
            for c in range(4):
                w_split_lo(U_V, c, 4, i)
        pool.wait_ge(s_stored, 32)
        pl.memset(maskd[:], 0.0).then_inc(pool_c, 1)
        pool.wait_ge(pool_c, 3)
        pl.affine_select(out=maskd[:], in_=maskd[:], compare_op=ALU.is_ge, fill=NEG, base=0,
                         pattern=[[-1, P]], channel_multiplier=1).then_inc(ready, 1)
        with pool.Fori(0, DB) as j:
            pool.wait_ge(g_landed, 48 * j + 48)
            w_split_lo(U_HEADS, 0, 4, j)
            pl.affine_select(out=ws[:], in_=ws[:], compare_op=ALU.is_ge, fill=0.0, base=0,
                             pattern=[[1, P]], channel_multiplier=-1).then_inc(s["ws_masked"], 1)
            pl.affine_select(out=wb[:], in_=wb[:], compare_op=ALU.is_ge, fill=0.0, base=0,
                             pattern=[[1, NS]], channel_multiplier=-1).then_inc(s["ws_masked"], 1)
            w_split_lo(U_HEADS, 1, 4, j)
            w_split_lo(U_HEADS, 2, 4, j)
            pool.wait_ge(s["vtok_copied"], 2 * j + 2)
            pool.dma_start(va_out[:, bass.ds(j, 1), :].rearrange("p a n -> p (a n)"), vtok[0:NS, 4, :]
                           ).then_inc(s["va_stored"], 16)
            w_split_lo(U_HEADS, 3, 4, j)
            pool.wait_ge(s["b_done"], j + 1)
            pool.dma_start(mix_d[:, bass.ds(H + j, 1), 0:SEQ].rearrange("p a n -> p (a n)"), po[:]
                           ).then_inc(s["b_stored"], 16)
            pool.wait_ge(s["a_done"], j + 1)
            pool.dma_start(mix_d[:, bass.ds(j, 1), :].rearrange("p a n -> p (a n)"), ao[:]).then_inc(s["a_stored"], 16)
        with pool.Fori(0, KD // 2) as i:
            for c in range(4):
                w_split_lo(U_OUT, c, 4, i)
        pool.wait_ge(acc_zero, 2)
        pool.wait_ge(R_ready, 2)
        for k in range(KD):
            if k % 4 == 0:
                ahead = mix[:, k + 3, :]
                pl.tensor_tensor(ahead, ahead, R[:], ALU.mult).then_inc(hp_tmp, 1)
            if k == KD - 1:
                break
            pool.wait_ge(h_sq, k + 1)
            if k:
                wait_past(pool, h_acc, k)
            pl.tensor_tensor(acc[:], acc[:], sqt[:, k % 2, :], ALU.add).then_inc(h_acc, 1)
        pool.wait_ge(h_done, KD)
        pl.memset(y[:], 0.0).then_inc(dn_done, 1)

        def hist(p, n):
            for t in range(2):
                f = p + KF * t
                if n is not None:
                    wait_past(pool, cv_done, 2 * n)
                pl.tensor_copy(ub[t][:, 2 + SEQ:UB].rearrange("p (b n) -> p b n", b=DB)[:, :, 0:2],
                               st[:, bass.ds(f, 1), :].rearrange("p a (b n) -> p (a b) n", b=DB)).then_inc(st_in, 1)

        def hist_new(p, n):
            for t in range(2):
                f = p + KF * t
                pool.wait_ge(up_evac[t], n + 1)
                pl.tensor_copy(hs[:, bass.ds(f, 1), 0:2].rearrange("p a n -> p (a n)"),
                               ub[t][:, SEQ:SEQ + 2])
                pl.tensor_copy(hs[:, bass.ds(f, 1), 2:18].rearrange("p a (b n) -> p (a b) n", b=DB),
                               ub[t][:, 2 + SEQ:UB].rearrange("p (b n) -> p b n", b=DB)[:, :, DT:DT + 2]
                               ).then_inc(hist_cp, 1)

        def g_split_lo(n, slot):
            pool.wait_ge(g_hi, n + 1)
            pl.tensor_tensor(gl[:, slot, :], gv[:], gh[:, slot, :].bitcast(F32), ALU.subtract).then_inc(g_lo, 1)

        pool.wait_ge(st_landed, 16)
        hist(0, None)
        for c in range(4):
            w_split_lo(U_FFN, c)
        hist_new(0, 0)
        g_split_lo(0, 0)
        with pool.Fori(0, ROUNDS - 1) as i:
            for t in range(4):
                p = GRP * i + 1 + t
                hist(p, p)
                for c in range(4):
                    w_split_lo(U_FFN + 4, 4 * t + c, 24, i)
                hist_new(p, p)
                if t < 3:
                    g_split_lo(p, 1 + t)
            for c in range(16, 24):
                w_split_lo(U_FFN + 4, c, 24, i)
            g_split_lo(GRP * i + 4, 0)
        for t in range(3):
            p = KF - 3 + t
            hist(p, p)
            for c in range(4):
                w_split_lo(UNITS - 20, 4 * t + c)
            hist_new(p, p)
            g_split_lo(p, 1 + t)
        for c in range(12, 16):
            w_split_lo(UNITS - 20, c)
        pool.wait_ge(y_gain, len(POOL_Y))
        pool.wait_ge(R_ready, 4)
        for n, k in enumerate(POOL_Y):
            pool.wait_ge(hr_landed[k // 4], 16)
            pl.tensor_tensor(y[:, k, :], y[:, k, :], R[:], ALU.mult).then_inc(yp_tmp, 1)
            pool.wait_ge(yp_tmp, n + 1)
            pl.tensor_tensor(y[:, k, :], y[:, k, :], hres[:, k, :], ALU.add).then_inc(yp_done, 1)

    @block.vector
    def _(dve):
        dve.wait_ge(c_landed, 32)
        for z in range(2):
            v.tensor_tensor_reduce(out=lamin[:, 2 * z, :], in0=lamin[:, 2 * z, :], in1=lamin[:, 2 * z + 1, :],
                                   scale=1.0, scalar=0.0, op0=ALU.mult, op1=ALU.add,
                                   accum_out=lt[:, z:z + 1]).then_inc(lam_sum, 1)
        ch = Chain(dve, dve_c, 0)
        ch.link(v.tensor_scalar(gsub[:], cs[:, C_SUB:C_SUB + 1], 1.0 - LAM_INIT, None, ALU.mult))
        def add_x_squares(k0, k1):
            for k in range(k0, k1):
                dve.wait_ge(x_sq, k + 1)
                if k == 0:
                    v.tensor_copy(acc0[:], sq0[:, 0, :]).then_inc(x_acc, 1)
                else:
                    dve.wait_ge(x_acc, k)
                    v.tensor_tensor(acc0[:], acc0[:], sq0[:, k % 2, :], ALU.add).then_inc(x_acc, 1)

        for q, (k0, k1) in enumerate(X_PARTS):
            dve.wait_ge(x_landed[q], 16)
            for k in range(k0, k1):
                dve.wait_ge(x_hi, k + 1)
                v.scalar_tensor_tensor(out=xl[:, k, :], in0=xraw[:, k, :], scalar=cs[:, C_PRE + k:C_PRE + k + 1],
                                       in1=xh[:, k, :].bitcast(F32), op0=ALU.mult, op1=ALU.subtract
                                       ).then_inc(x_lo, 1)
            if q:
                add_x_squares(*X_PARTS[q - 1])
        add_x_squares(*X_PARTS[-1])
        dve.wait_ge(lam_exp, 1)
        ch.link(v.tensor_tensor(lt[:, 0:1], lt[:, 3:4], lt[:, 2:3], ALU.subtract))
        ch.link(v.tensor_scalar(neglam[:], lt[:, 0:1], -LAM_INIT, None, ALU.add))
        ch.link(v.tensor_scalar(sgn[:], cs[:, C_SEL + 1:C_SEL + 2], neglam[:, 0:1], None, ALU.mult))
        ch.link(v.tensor_tensor(sgn[:], sgn[:], cs[:, C_SEL:C_SEL + 1], ALU.add))
        dve.wait_ge(sq_root, 1)
        v.reciprocal(R[:], R[:]).then_inc(R_ready, 1)
        dve.wait_ge(R_ready, 1)
        Rh = halves(R[:])

        def qk_evac(j):
            tile_done(dve, U_QK, 0, 4, j)
            wait_past(dve, q_stored, 16 * j)
            wait_past(dve, smp, 3 * j)
            v.tensor_tensor(halves(zt[0][:]), tile_out(0), Rh, ALU.mult).then_inc(q_evac, 1)
            tile_done(dve, U_QK, 2, 4, j)
            wait_past(dve, k_stored, 16 * j)
            v.tensor_tensor(halves(zt[1][:]), tile_out(2), Rh, ALU.mult).then_inc(k_evac, 1)

        qk_evac(0)
        with dve.Fori(1, H) as j:
            qk_evac(j)
        dve.wait_ge(q_stored, 16 * H)
        dve.wait_ge(k_stored, 16 * H)
        dve.wait_ge(smp, 3 * H)

        def v_pair(i):
            for t in range(2):
                tile_done(dve, U_V, 2 * t, 4, i)
                wait_past(dve, vT_ready, 2 * i)
                v.tensor_tensor(halves(zt[t][:]), tile_out(2 * t), Rh, ALU.mult).then_inc(v_evac, 1)
            for t in range(2):
                dve.wait_ge(vT_ready, 2 * i + t + 1)
                wait_past(dve, v_stored[t], 32 * i)
                v.tensor_copy(vt[t][:, 0:4, :], pb[:, 4 + t, :].rearrange("p (b n) -> p b n", b=4)
                              )
                v.tensor_copy(vt[t][0:NS, 4, :], pb[0:NS, 6 + t, 0:P]).then_inc(vt_evac, 1)

        v_pair(0)
        with dve.Fori(1, H // 2) as i:
            v_pair(i)

        dve.wait_ge(ready, 3)
        dve.wait_ge(v_stored[0], 16 * H)
        dve.wait_ge(v_stored[1], 16 * H)
        ch.link(v.memset(vr[:], 1.0))
        base = ch.c
        NCH = 31

        def batch(j):
            ch = Chain(dve, dve_c, base, NCH, j)

            def combine(g_):
                n = (g_ + 1) * P
                o = g_ * (g_ + 1) // 2 * P
                dve.wait_ge(s["pexp_done"], 8 * j + 2 * g_ + 2)
                ch.link(v.reciprocal(prs[:], psm[:, 2 * g_:2 * g_ + 2]))
                ch.link(v.tensor_tensor(prs[:, 1:2], prs[:, 1:2], neglam[:], ALU.mult))
                ch.link(v.tensor_scalar(W[:, o:o + n], W[:, o:o + n], prs[:, 0:1], None, ALU.mult))
                v.scalar_tensor_tensor(out=W[:, o:o + n], in0=E2[:, 0:n], scalar=prs[:, 1:2], in1=W[:, o:o + n],
                                       op0=ALU.mult, op1=ALU.add).then_inc(s["pw_done"], 1)

            def s_max(g_):
                dve.wait_ge(s["st_copied"], 4 * j + g_ + 1)
                v.tensor_reduce(mx4[:, g_:g_ + 1], S[:, SEQ * g_:SEQ * (g_ + 1)], AX.X, ALU.max
                                ).then_inc(s["s_max"], 1)

            def copy_wT(g_):
                n = (g_ + 1) * P
                o = g_ * (g_ + 1) // 2 * P
                dve.wait_ge(s["wT_ready"], 4 * j + g_ + 1)
                wait_past(dve, s["pv_ready"], j)
                bank = 4 + (g_ % 2 if g_ < 2 else 1 - g_ % 2)
                v.tensor_copy(wT[:, o:o + n], pb[:, bank, 0:n]).then_inc(s["wT_copied"], 1)

            def copy_sT(g_):
                dve.wait_ge(s["sT_ready"], 5 * j + g_ + 1)
                v.tensor_copy(S[:, SEQ * g_:SEQ * (g_ + 1)], pb[:, 4 + g_ % 2, :]).then_inc(s["sT_copied"], 1)

            def p_max(g_):
                n = (g_ + 1) * P
                dve.wait_ge(s["pscore_ready"], 4 * j + g_ + 1)
                diag = pb[:, 6:8, g_ * P:n]
                ch.link(v.tensor_tensor(diag, diag, maskd[:].rearrange("p (a n) -> p a n", a=1)
                                        .to_broadcast([P, 2, P]), ALU.add))
                ch.link(v.tensor_reduce(pmx[:], pb[:, 6:8, 0:n], AX.X, ALU.max))
                wait_past(dve, s["pexp_done"], 8 * j + 2 * g_)
                v.tensor_scalar(pneg[:], pmx[:], -SCALE, None, ALU.mult).then_inc(s["pneg_ready"], 1)

            p_max(0)
            s_max(0)
            p_max(1)
            s_max(1)
            combine(0)
            p_max(2)
            s_max(2)
            combine(1)
            copy_wT(0)
            s_max(3)
            dve.wait_ge(s["snew_ready"], j + 1)
            v.tensor_tensor(S[:, PAGES * P:], pb[:, 2, 0:DT], cs[:, C_MASK:C_MASK + DT], ALU.add
                            ).then_inc(s["snew_masked"], 1)
            dve.wait_ge(s["snew_masked"], j + 1)
            ch.link(v.tensor_reduce(mx4[:, 4:5], S[:, PAGES * P:], AX.X, ALU.max))
            dve.wait_ge(s["s_max"], 4 * j + 4)
            ch.link(v.tensor_reduce(mx[:], mx4[:], AX.X, ALU.max))
            v.tensor_scalar(nmx[:], mx[:], -SCALE, None, ALU.mult).then_inc(s["nmx_ready"], 1)
            p_max(3)
            combine(2)
            copy_wT(1)
            copy_sT(0)
            tile_done(dve, U_HEADS, 0, 4, j)
            v.tensor_tensor(halves(vg[:]), tile_out(0), Rh, ALU.mult).then_inc(s["va_evac"], 1)
            copy_sT(1)
            combine(3)
            copy_sT(2)
            copy_sT(3)
            dve.wait_ge(s["sT_ready"], 5 * j + 5)
            v.tensor_copy(En[:], pb[0:DT, 4, 0:P]).then_inc(s["sT_copied"], 1)
            copy_wT(2)
            copy_wT(3)
            dve.wait_ge(s["sexp"], 5 * j + 5)
            ch.link(v.tensor_reduce(rs[:, 0:1], ssm[:], AX.X, ALU.add))
            ch.link(v.reciprocal(rs[:, 1:2], rs[:, 0:1]))
            ch.link(v.tensor_tensor(rs[:, 0:1], rs[:, 1:2], sgn[:], ALU.mult))
            dve.wait_ge(s["vsd_done"], 2 * j + 2)
            ch.link(v.reciprocal(vr[:], vr[:]))
            dve.wait_ge(s["vaT_ready"], j + 1)
            wait_past(dve, s["va_stored"], 16 * j)
            v.tensor_tensor(vtok[:, 0:4, :], pb[:, 2, :].rearrange("p (b n) -> p b n", b=4),
                            vr[:, 0:4].rearrange("p (b a) -> p b a", a=1).to_broadcast([P, 4, P]), ALU.mult
                            ).then_inc(s["vtok_copied"], 1)
            v.tensor_scalar(vtok[0:NS, 4, :], pb[0:NS, 3, 0:P], vr[0:NS, 4:5], None, ALU.mult
                            ).then_inc(s["vtok_copied"], 1)
            dve.wait_ge(s["psd_done"], j + 1)
            ch.link(v.reciprocal(pr4[:], pr4[:]))
            v.tensor_tensor(pon[:], pb[:, 6, :].rearrange("p (b n) -> p b n", b=4),
                            pr4[:].rearrange("p (b a) -> p b a", a=1).to_broadcast([P, 4, P]), ALU.mult
                            ).then_inc(s["pon_ready"], 1)
            dve.wait_ge(s["spv_ready"], j + 1)
            v.tensor_scalar(osb[:], pb[:, 7, 0:2 * P], rs[:, 0:1], None, ALU.mult).then_inc(s["osb_ready"], 1)
            dve.wait_ge(s["gm_ready"], j + 1)
            dve.wait_ge(g_landed, 48 * j + 48)
            wait_past(dve, s["a_stored"], 16 * j)
            v.tensor_tensor(ao[:, 0:SEQ].rearrange("p (b n) -> p b n", b=4),
                            pb[:, 2, :].rearrange("p (b n) -> p b n", b=4),
                            bsb[:].rearrange("p (a n) -> p a n", a=1).to_broadcast([P, 4, P]), ALU.add
                            ).then_inc(s["ao_prompt"], 1)
            v.tensor_tensor(ao[:, SEQ:T].rearrange("p (b n) -> p b n", b=DB),
                            pb[:, 3, P:P + NS].rearrange("p (b n) -> p b n", b=DB),
                            bsb[:, 0:DT].rearrange("p (a n) -> p a n", a=1).to_broadcast([P, DB, DT]),
                            ALU.add).then_inc(s["ao_sample"], 1)
            dve.wait_ge(s["poT_ready"], j + 1)
            wait_past(dve, s["b_stored"], 16 * j)
            v.tensor_scalar(po[:], pb[:, 6, :], gsub[:, 0:1], None, ALU.mult).then_inc(s["b_done"], 1)
            dve.wait_ge(s["oT_ready"], j + 1)
            ch.link(v.tensor_copy(oT[:], pb[:, 5, 0:2 * P]))
            for z in range(2):
                o4 = oT[:, P * z:P * z + P].rearrange("p (h y k n) -> p h y k n", h=H // 2, y=2, k=2)
                ch.link(v.tensor_tensor(osm[:].rearrange("p (h y n) -> p h y n", h=H // 2, y=2)[:, :, z, :],
                                        o4[:, :, z, 0, :], o4[:, :, z, 1, :], ALU.add))
            v.tensor_tensor(osq[:], osm[:], osm[:], ALU.mult).then_inc(s["ssq_ready"], 1)
            tile_done(dve, U_HEADS, 2, 4, j)
            wait_past(dve, s["a_done"], j)
            v.tensor_tensor(halves(ug[:]), tile_out(0), Rh, ALU.mult).then_inc(s["u_evac"], 1)
            dve.wait_ge(s["ao_sample"], j + 1)
            dve.wait_ge(s["ugelu"], j + 1)
            v.tensor_tensor(ao[:], ao[:], ug[:], ALU.mult).then_inc(s["a_done"], 1)
            dve.wait_ge(s["ssd_done"], j + 1)
            ch.link(v.reciprocal(osq[:], osq[:]))
            v.scalar_tensor_tensor(out=bsmp[:, :, bass.ds(DT * j, DT)],
                                   in0=osm[:].rearrange("p (h n) -> p h n", h=H), scalar=gsub[:, 0:1],
                                   in1=osq[:].rearrange("p (h n) -> p h n", h=H),
                                   op0=ALU.mult, op1=ALU.mult).then_inc(s["bs_done"], 1)
            ch.close(NCH)

        batch(0)
        with dve.Fori(1, DB) as j:
            batch(j)

        for first, end, source, landed, count in MIX_PARTS:
            dve.wait_ge(m_landed[landed], count)
            with dve.Fori(first, end) as k:
                dve.wait_ge(m_hi, k + 1)
                xk = xl[:, bass.ds(k, 1), :].rearrange("p a n -> p (a n)")
                rk = early[:, bass.ds(k, 1), :].rearrange("p a n -> p (a n)") if source else xk.bitcast(F32)
                v.tensor_tensor(xk, rk, xh[:, bass.ds(k, 1), :].rearrange("p a n -> p (a n)").bitcast(F32),
                                ALU.subtract).then_inc(m_lo, 1)
        v.memset(acc[:], 0.0).then_inc(acc_zero, 1)
        dve.wait_ge(acc_zero, 1)

        def out_pair(i, last=False):
            for t in range(2):
                tile_done(dve, U_OUT, 2 * t, 4, i)
                v.tensor_copy(halves(mix[:, bass.ds(2 * i + t, 1), :].rearrange("p a n -> p (a n)")),
                              tile_out(2 * t)).then_inc(m_copied[t], 1)
                if last and t == 1:
                    return
                dve.wait_ge(m_sq[t], i + 1)
                wait_past(dve, m_acc, 2 * i + t)
                v.tensor_tensor(acc[:], acc[:], sqt[:, t, :], ALU.add).then_inc(m_acc, 1)

        out_pair(0)
        with dve.Fori(1, KD // 2 - 1) as i:
            out_pair(i)
        out_pair(KD // 2 - 1, last=True)
        dve.wait_ge(sq_root, 2)
        v.reciprocal(R[:], R[:]).then_inc(R_ready, 1)
        dve.wait_ge(R_ready, 2)
        v.memset(acc[:], 0.0).then_inc(acc_zero, 1)
        dve.wait_ge(acc_zero, 2)
        dve.wait_ge(m_copied[0], KD // 2)
        dve.wait_ge(m_copied[1], KD // 2)
        for q in range(4):
            dve.wait_ge(r_landed[q], 16)
            for i in range(4 * q, 4 * q + 4, 2):
                for k in range(i, i + 2):
                    mk = mix[:, k, :]
                    if k in POOL_H:
                        dve.wait_ge(hp_tmp, POOL_H.index(k) + 1)
                    else:
                        v.tensor_tensor(mk, mk, R[:], ALU.mult).then_inc(h_tmp, 1)
                        dve.wait_ge(h_tmp, k + 1 - k // 4)
                    v.scalar_tensor_tensor(out=mk, in0=mk, scalar=cs[:, C_POST + k:C_POST + k + 1],
                                           in1=xres[:, k, :], op0=ALU.mult, op1=ALU.add).then_inc(h_done, 1)
                for k in range(i, i + 2):
                    dve.wait_ge(h_done, k + 1)
                    dve.wait_ge(h_hi, k + 1)
                    v.scalar_tensor_tensor(out=xl[:, k, :], in0=mix[:, k, :], scalar=cs[:, C_FFN + k:C_FFN + k + 1],
                                           in1=xh[:, k, :].bitcast(F32), op0=ALU.mult, op1=ALU.subtract
                                           ).then_inc(h_lo, 1)
        dve.wait_ge(sq_root, 3)
        v.reciprocal(R[:], R[:]).then_inc(R_ready, 1)
        dve.wait_ge(R_ready, 3)
        dve.wait_ge(h_stored, 64)
        for t in range(2):
            v.memset(ub[t][:, 0:2], 0.0).then_inc(ub_zero, 1)
        dve.wait_ge(ub_zero, 2)

        def evac_up(t, n, base, c, per, i):
            tile_done(dve, base, c + 2 * t if base > U_FFN else 2, per, i)
            wait_past(dve, cv_done, 2 * n)
            wait_past(dve, hist_cp, 2 * n)
            lo_, hi_ = pb[:, 2 * t, 0:TH], pb[:, 2 * t + 1, 0:TH]
            v.tensor_tensor(ub[t][:, 2:2 + TH], lo_, R[:, 0:TH], ALU.mult)
            v.tensor_tensor(ub[t][:, 2 + TH:2 + SEQ], hi_[:, 0:SEQ - TH], R[:, TH:SEQ], ALU.mult)
            v.tensor_tensor(ub[t][:, 2 + SEQ:UB].rearrange("p (b n) -> p b n", b=DB)[:, :, 2:2 + DT],
                            hi_[:, SEQ - TH:TH].rearrange("p (b n) -> p b n", b=DB),
                            R[:, SEQ:T].rearrange("p (b n) -> p b n", b=DB), ALU.mult).then_inc(up_evac[t], 1)

        def conv(p, t, n):
            f = p + KF * t
            dve.wait_ge(tap, 2 * n + t + 1)
            v.scalar_tensor_tensor(out=cv[t][:, 0:NC_], in0=ub[t][:, 1:UB - 1],
                                   scalar=cs[:, bass.ds(C_W + 2 * KF + f, 1)],
                                   in1=cv[t][:, 0:NC_], op0=ALU.mult, op1=ALU.add).then_inc(tap1, 1)
            dve.wait_ge(tap1, 2 * n + t + 1)
            v.scalar_tensor_tensor(out=cv[t][:, 0:NC_], in0=ub[t][:, 0:NC_],
                                   scalar=cs[:, bass.ds(C_W + f, 1)],
                                   in1=cv[t][:, 0:NC_], op0=ALU.mult, op1=ALU.add).then_inc(cv_done, 1)

        def smp_cols(ap):
            return ap[:, SEQ:SEQ + DB * 10].rearrange("p (b n) -> p b n", b=DB)[:, :, 2:2 + DT]

        def pair_dve(p, n, base, c, per=0, i=0):
            for t in range(2):
                evac_up(t, n, base, c, per, i)
                conv(p, t, n)
            dve.wait_ge(gelu_done, n + 1)
            dve.wait_ge(cv_done, 2 * n + 2)
            wait_past(dve, g_lo, n)
            v.tensor_tensor(gv[:, 0:SEQ], cv[0][:, 0:SEQ], cv[1][:, 0:SEQ], ALU.mult)
            v.tensor_tensor(gv[:, SEQ:T].rearrange("p (b n) -> p b n", b=DB), smp_cols(cv[0]), smp_cols(cv[1]),
                            ALU.mult).then_inc(gv_done, 1)

        def add_squares(k):
            dve.wait_ge(y_sq, k + 1)
            if k == 0:
                v.tensor_copy(accl[:], sql[:, 0, :]).then_inc(y_acc, 1)
            else:
                wait_past(dve, y_acc, k)
                v.tensor_tensor(accl[:], accl[:], sql[:, k % 2, :], ALU.add).then_inc(y_acc, 1)

        def down_dve(r, base, c, per=0, i=0, squares=False):
            for m in range(KD):
                if squares and m:
                    add_squares(m - 1)
                if m % 2:
                    dve.wait_ge(w_used, base + c + m // 2 + 1 + (per * i if per else 0))
                else:
                    dve.wait_ge(dn_even, KD // 2 * r + m // 2 + 1)
                ym = halves(y[:, m, :])
                v.tensor_tensor(ym, ym, tile_out(4 + 2 * (m % 2)), ALU.add).then_inc(dn_done, 1)

        pair_dve(0, 0, U_FFN, 0)
        dve.wait_ge(dn_done, 1)
        with dve.Fori(0, ROUNDS - 1) as i:
            for t in range(4):
                pair_dve(GRP * i + 1 + t, GRP * i + 1 + t, U_FFN + 4, 4 * t, 24, i)
            dve.wait_ge(dn_done, KD * i + 1)
            down_dve(i, U_FFN + 4, 16, 24, i)
        for t in range(3):
            pair_dve(KF - 3 + t, KF - 3 + t, UNITS - 20, 4 * t)
        dve.wait_ge(dn_done, KD * (ROUNDS - 1) + 1)
        dve.wait_ge(w_used, UNITS - 8)

        down_dve(ROUNDS - 1, UNITS - 20, 12, squares=True)
        dve.wait_ge(sq_root, 4)
        v.reciprocal(R[:], R[:]).then_inc(R_ready, 1)
        dve.wait_ge(R_ready, 4)
        for n, k in enumerate(k for k in range(KD) if k not in POOL_Y):
            dve.wait_ge(hr_landed[k // 4], 16)
            v.tensor_tensor(y[:, k, :], y[:, k, :], R[:], ALU.mult).then_inc(y_tmp, 1)
            dve.wait_ge(y_tmp, n + 1)
            v.scalar_tensor_tensor(out=y[:, k, :], in0=y[:, k, :], scalar=cs[:, C_LAST + k:C_LAST + k + 1],
                                   in1=hres[:, k, :], op0=ALU.mult, op1=ALU.add).then_inc(y_done, 1)

    @block.tensor
    def _(pe):
        pe.wait_ge(ready, 2)

        def sum_squares(bank, *parts):
            for p, (landed, count, tile) in enumerate(parts):
                pe.wait_ge(landed, count)
                for n in range(2):
                    m = te.matmul(pb[:, bank + n, 0:TH], ones[:], tile[:, n * TH:(n + 1) * TH],
                                  start=(p == 0), stop=(p == len(parts) - 1))
            m.then_inc(ssq_mm, 1)

        tile_mm(0, U_QK, 0, k_sem=x_lo)
        unit_mm(2, U_QK, 2, xh, xl, 0, 8, True, False).then_inc(w_used, 1)
        sum_squares(6, (x_acc, KD, acc0))
        unit_mm(2, U_QK, 3, xh, xl, 8, 8, False, True).then_inc(w_used, 1)
        with pe.Fori(1, H) as j:
            wait_past(pe, q_evac, j)
            tile_mm(0, U_QK, 0, 4, j)
            wait_past(pe, k_evac, j)
            tile_mm(2, U_QK, 2, 4, j)
        pe.wait_ge(q_evac, H)
        pe.wait_ge(k_evac, H)
        pe.wait_ge(sq_root, 1)

        def v_pair(i):
            wait_past(pe, v_evac, 2 * i)
            for t in range(2):
                tile_mm(2 * t, U_V, 2 * t, 4, i)
            for t in range(2):
                pe.wait_ge(v_evac, 2 * i + t + 1)
                wait_past(pe, vt_evac, 2 * i)
                for b4 in range(4):
                    te.transpose(pb[:, 4 + t, b4 * P:(b4 + 1) * P], zt[t][:, b4 * P:(b4 + 1) * P], ident[:])
                te.transpose(pb[0:NS, 6 + t, 0:P], zt[t][:, SEQ:T], ident[:]).then_inc(vT_ready, 1)

        v_pair(0)
        with pe.Fori(1, H // 2) as i:
            v_pair(i)
        pe.wait_ge(v_evac, H)
        pe.wait_ge(vt_evac, H)

        def batch(j):
            def half_unit(n):
                m = unit_mm(0, U_HEADS, n // 2, xh, xl, 4 * n % KD, 4, n % 4 == 0, n % 4 == 3,
                            col=n % 2 * 4 * P, per=4, j=j)
                if n % 2:
                    m.then_inc(w_used, 1)

            def scores(out, h, rhs):
                r = 32 * (h // 2)
                return te.matmul(out[r:r + 32], qb[:, h, :], rhs, start=(h % 2 == 0), stop=(h % 2 == 1))

            def k_pages(g_):
                slot = 4 * (g_ % 2)
                wait_past(pe, s["st_copied"], 4 * j + max(0, g_ - 1))
                if g_ < 2:
                    wait_past(pe, s["ao_sample"] if g_ else s["ao_prompt"], j)
                for i in range(0, 4, 2):
                    pe.wait_ge(pg_landed[(slot + i) // 2], 128 * j + 32 * (g_ // 2 + 1))
                for y in range(2):
                    for h in range(y, H, 2):
                        m = scores(pb[:, 2 + g_ % 2, :], h, pg[:, slot:slot + 4, h * P:(h + 1) * P])
                m.then_inc(pg_used, 4)

            def p_scores(g_):
                n = (g_ + 1) * P
                if g_ == 0:
                    pe.wait_ge(hq_landed, 32 * j + 32)
                    wait_past(pe, s["b_done"], j)
                    wait_past(pe, s["osb_ready"], j)
                wait_past(pe, s["pexp_done"], 8 * j + 2 * g_)
                te.matmul(pb[:, 6, 0:n], qT[0:DH, g_ * P:n], kT[0:DH, 0:n], start=True, stop=True)
                te.matmul(pb[:, 7, 0:n], qT[DH:P, g_ * P:n], kT[DH:P, 0:n], start=True, stop=True
                          ).then_inc(s["pscore_ready"], 1)

            def w_turn(g_):
                bank = 4 + (g_ % 2 if g_ < 2 else 1 - g_ % 2)
                o = g_ * (g_ + 1) // 2 * P
                pe.wait_ge(s["pw_done"], 4 * j + g_ + 1)
                if g_ < 2:
                    wait_past(pe, s["ssd_done"], j)
                else:
                    pe.wait_ge(s["sT_copied"], 5 * j + 2 + g_)
                for kb in range(g_ + 1):
                    m = te.transpose(pb[:, bank, kb * P:(kb + 1) * P], W[:, o + kb * P:o + (kb + 1) * P],
                                     ident[:])
                m.then_inc(s["wT_ready"], 1)

            def s_turn(g_):
                pe.wait_ge(s["sexp"], 5 * j + g_ + 1)
                if g_ < 2:
                    pe.wait_ge(s["wT_copied"], 4 * j + g_ + 1)
                else:
                    pe.wait_ge(s["sT_copied"], 5 * j + g_ - 1)
                for i in range(4):
                    o = SEQ * g_ + i * P
                    m = te.transpose(pb[:, 4 + g_ % 2, i * P:(i + 1) * P], S[:, o:o + P], ident[:])
                m.then_inc(s["sT_ready"], 1)

            def v_pages(g_):
                slot = 4 * (g_ % 2)
                if g_ == 0:
                    pe.wait_ge(s["pexp_done"], 8 * j + 8)
                pe.wait_ge(s["sT_copied"], 5 * j + g_ + 1)
                for i in range(4):
                    if i % 2 == 0:
                        pe.wait_ge(pg_landed[(slot + i) // 2], 128 * j + 32 * (g_ // 2 + 3))
                    o = SEQ * g_ + i * P
                    for y in range(4):
                        m = te.matmul(pb[32 * y:32 * y + 32, 7, 0:2 * P], S[:, o + 32 * y:o + 32 * y + 32],
                                      pg[:, slot + i, 2 * P * y:2 * P * (y + 1)], start=(g_ == 0 and i == 0),
                                      stop=False)
                    m.then_inc(pg_used, 1)

            pe.wait_ge(sq_landed, 32 * j + 32)
            k_pages(0)
            p_scores(0)
            wait_past(pe, s["u_evac"], j)
            half_unit(0)
            k_pages(1)
            p_scores(1)
            half_unit(1)
            k_pages(2)
            p_scores(2)
            w_turn(0)
            half_unit(2)
            k_pages(3)
            pe.wait_ge(s["st_copied"], 4 * j + 3)
            for y in range(2):
                for h in range(y, H, 2):
                    m = scores(pb[:, 2, 0:DT], h, knew[:, h, :])
            m.then_inc(s["snew_ready"], 1)
            p_scores(3)
            w_turn(1)
            half_unit(3)
            s_turn(0)
            s_turn(1)
            v_pages(0)
            pe.wait_ge(s["va_evac"], j + 1)
            half_unit(4)
            s_turn(2)
            s_turn(3)
            v_pages(1)
            pe.wait_ge(s["vsq_ready"], j + 1)
            pe.wait_ge(s["nmx_ready"], j + 1)
            for b4 in range(4):
                te.matmul(pb[:, 3, SSQ_COL + b4:SSQ_COL + b4 + 1], vq[:, b4 * P:(b4 + 1) * P], ones[:, 0:1],
                          start=True, stop=True)
            te.matmul(pb[0:NS, 3, SSQ_COL + 4:SSQ_COL + 5], vq[:, SEQ:T], ones[:, 0:1], start=True, stop=True
                      ).then_inc(s["vssq_ready"], 1)
            pe.wait_ge(s["sexp"], 5 * j + 5)
            pe.wait_ge(s["sT_copied"], 5 * j + 3)
            te.transpose(pb[0:DT, 4, 0:P], S[:, PAGES * P:], ident[:]).then_inc(s["sT_ready"], 1)
            half_unit(5)
            w_turn(2)
            w_turn(3)
            v_pages(2)
            half_unit(6)
            pe.wait_ge(s["wT_copied"], 4 * j + 4)
            pe.wait_ge(hv_landed, 16 * j + 16)
            for g_ in range(4):
                o = g_ * (g_ + 1) // 2 * P
                for kb in range(g_ + 1):
                    m = te.matmul(pb[:, 6, g_ * P:(g_ + 1) * P], wT[:, o + kb * P:o + (kb + 1) * P], V[:, kb, :],
                                  start=(kb == 0), stop=(kb == g_))
            m.then_inc(s["pv_ready"], 1)
            pe.wait_ge(s["va_gained"], j + 1)
            pe.wait_ge(s["vsd_done"], 2 * j + 2)
            for b4 in range(4):
                te.transpose(pb[:, 2, b4 * P:(b4 + 1) * P], vaT[:, b4 * P:(b4 + 1) * P], ident[:])
            te.transpose(pb[0:NS, 3, 0:P], vaT[:, SEQ:T], ident[:]).then_inc(s["vaT_ready"], 1)
            pe.wait_ge(sv_landed, 16 * j + 16)
            pe.wait_ge(s["sT_copied"], 5 * j + 5)
            v_pages(3)
            for y in range(4):
                m = te.matmul(pb[32 * y:32 * y + 32, 7, 0:2 * P], En[:, 32 * y:32 * y + 32],
                              vnew[:, 2 * P * y:2 * P * (y + 1)], start=False, stop=True)
            m.then_inc(s["spv_ready"], 1)
            pe.wait_ge(s["vtok_copied"], 2 * j + 2)
            pe.wait_ge(s["ws_masked"], 2 * j + 2)
            for b4 in range(4):
                te.matmul(pb[:, 2, b4 * P:(b4 + 1) * P], vtok[:, b4, :], ws[:], start=True, stop=True)
            te.matmul(pb[:, 3, P:P + NS], vtok[0:NS, 4, :], wb[:], start=True, stop=True
                      ).then_inc(s["gm_ready"], 1)
            pe.wait_ge(s["pon_ready"], j + 1)
            for b4 in range(4):
                m = te.transpose(pb[:, 6, b4 * P:(b4 + 1) * P], pon[:, b4, :], ident[:])
            m.then_inc(s["poT_ready"], 1)
            pe.wait_ge(s["osb_ready"], j + 1)
            for z in range(2):
                m = te.transpose(pb[:, 5, z * P:(z + 1) * P], osb[:, z * P:(z + 1) * P], ident[:])
            m.then_inc(s["oT_ready"], 1)
            half_unit(7)
            pe.wait_ge(s["ssq_ready"], j + 1)
            te.matmul(pb[:, 4, 0:NS], ones[:], osq[:], start=True, stop=True).then_inc(s["sss_ready"], 1)

        batch(0)
        with pe.Fori(1, DB) as j:
            batch(j)

        pe.wait_ge(s["u_evac"], DB)
        pe.wait_ge(s["a_done"], DB)

        def out_pair(i):
            for t in range(2):
                wait_past(pe, m_copied[t], i)
                tile_mm(2 * t, U_OUT, 2 * t, 4, i, m_lo if t == 0 else None)

        out_pair(0)
        with pe.Fori(1, KD // 2) as i:
            out_pair(i)

        sum_squares(4, (m_acc, KD - 1, acc), (m_sq[1], KD // 2, sqt[:, 1, :]))
        pe.wait_ge(m_copied[0], KD // 2)
        pe.wait_ge(m_copied[1], KD // 2)

        def pair_pe(n, base, c, per=0, i=0, k_sem=None):
            for t in range(2):
                wait_past(pe, up_evac[t], n)
                tile_mm(2 * t, base, c + 2 * t, per, i, k_sem)

        def down_pe(r, base, c, per=0, i=0, first=0):
            pe.wait_ge(g_lo, GRP * r + GRP)
            for mm in range(first, KD // 2):
                for a in range(2):
                    m = 2 * mm + a
                    pe.wait_ge(dn_done, KD * r + max(1, m))
                    ins = unit_mm(4 + 2 * a, base, c + mm, gh, gl, 0, GRP, True, True, col=a * GRP * P,
                                  per=per, j=i)
                    ins.then_inc(w_used if a else dn_even, 1)

        for half in range(2):
            for k in range(8):
                pe.wait_ge(h_lo, 8 * half + k + 1)
                for t in range(2):
                    m = unit_mm(2 * t, U_FFN, 2 * half + t, xh, xl, 8 * half + k, 1, half == 0 and k == 0,
                                half == 1 and k == 7, col=k * P)
                    if k == 7:
                        m.then_inc(w_used, 1)
        sum_squares(6, (h_acc, KD - 1, acc), (h_sq, KD, sqt[:, 1, :]))
        pe.wait_ge(sq_root, 3)
        with pe.Fori(0, ROUNDS - 1) as i:
            for t in range(4):
                pair_pe(GRP * i + 1 + t, U_FFN + 4, 4 * t, 24, i)
            down_pe(i, U_FFN + 4, 16, 24, i)
        for t in range(3):
            pair_pe(KF - 3 + t, UNITS - 20, 4 * t)
        pe.wait_ge(dn_done, KD * (ROUNDS - 1) + 1)
        for k0, nk in ((0, GRP - 1), (GRP - 1, 1)):
            pe.wait_ge(g_lo, GRP * (ROUNDS - 1) + k0 + nk)
            for a in range(2):
                ins = unit_mm(4 + 2 * a, UNITS - 20, 12, gh, gl, k0, nk, k0 == 0, k0 > 0, col=(a * GRP + k0) * P)
                if k0:
                    ins.then_inc(w_used if a else dn_even, 1)
        down_pe(ROUNDS - 1, UNITS - 20, 12, first=1)
        pe.wait_ge(up_evac[0], KF)
        sum_squares(0, (y_acc, KD - 1, accl), (y_sq, KD, sql[:, 1, :]))

    block.__exit__(None, None, None)


_OUTS = [((P, KD, T), "y"), ((H, P, T), "k"), ((H, 4, P, P), "v"), ((NS, H, P), "vs"), ((NS, H, P), "va"),
         ((P, 2 * KF, 18), "hist")]


def _tiles(w):
    return w.reshape(w.shape[0] // P, P, w.shape[1] // P, P).transpose(2, 0, 1, 3)


def _units(tiles):
    n = tiles.shape[0]
    return tiles.reshape(n, 2, 8, P, P).transpose(0, 1, 3, 2, 4).reshape(2 * n, P, UNIT)


def _weights(w_in, w_out, w_up, w_down):
    w = _tiles(w_in)
    parts = [_units(w[[o + h for h in range(H) for o in (16, 24)]]), _units(w[32:40]),
             _units(w[[o + h for h in range(H) for o in (8, 0)]]), _units(_tiles(w_out)[:, MIX_ORDER])]
    up = _tiles(w_up)
    pairs = [_units(up[[p, KF + p]]) for p in range(KF)]
    dn = _tiles(w_down).reshape(KD // 2, 2, ROUNDS, GRP, P, P).transpose(2, 0, 4, 1, 3, 5)
    dn = dn.reshape(ROUNDS, KD // 2, P, UNIT)
    parts.append(pairs[0][[0, 2, 1, 3]])
    for r in range(ROUNDS - 1):
        parts += pairs[GRP * r + 1:GRP * r + 5] + [dn[r]]
    parts += pairs[KF - 3:] + [dn[ROUNDS - 1]]
    return np.concatenate(parts).reshape(UNITS * P, UNIT)


def _feature_major(prompt, sample):
    x = np.concatenate([prompt, sample]).T
    return x.reshape(x.shape[0] // P, P, T).transpose(1, 0, 2)


def kernel(**inputs):
    import concourse.bacc as _bacc
    from concourse.bass_utils import run_bass_kernel_spmd as _run

    i = {k: np.asarray(a) for k, a in inputs.items()}
    col = lambda a: a.reshape(-1, P).T
    wb = np.zeros((H, DB, DT, DB, DT), np.float32)
    wst = i["w_s"][0].transpose(0, 2, 1)
    for b in range(DB):
        wb[:, b, :, b, :] = wst[:, 0:DT, 0:DT]
    row = np.arange(P)
    row_consts = np.concatenate([np.where(np.arange(DT)[None] > row[:, None] % DT, NEG, 0.0),
                                 (row[:, None] // DT % 2 == np.arange(2)[None])], axis=1).astype(np.float32)
    lay = {
        "xT": _feature_major(i["x_prompt"][0], i["x_sample"].reshape(NS, D)),
        "wstream": _weights(i["w_in"][0], i["w_out"][0], i["w_up"][0], i["w_down"][0]),
        "kpages": i["cache_k"][0].transpose(0, 3, 2, 1).reshape(N_PHYS, P, H * P),
        "vpages": i["cache_v"][0].reshape(N_PHYS, P, H * P),
        "state": i["state_conv"][0].reshape(DB * 2, 2 * KF, P).transpose(2, 1, 0),
        "ptab": i["page_table"].reshape(1, DB * PAGES),
        "consts": np.concatenate([col(i["g_pre_mix"]), col(i["g_post_mix"]), col(i["g_pre_ffn"]),
                                  col(i["g_post_ffn"]), i["g_v_a"][0].T, col(i["g_subln"]), col(i["b_conv"]),
                                  col(i["w_conv"][0]), row_consts], axis=1),
        "lams": np.stack([i[n][0] for n in ("lam_q1", "lam_k1", "lam_q2", "lam_k2")])[None],
        "wsT": wst,
        "wblk": wb.reshape(H, NS, NS),
        "bs": i["b_s"][0],
    }
    nc = _bacc.Bacc("TRN2", target_bir_lowering=False, num_devices=1)
    arrays, args = {}, []
    for name, x in lay.items():
        x = np.ascontiguousarray(x)
        arrays[f"in_{name}"] = x
        args.append(nc.dram_tensor(f"in_{name}", x.shape, mybir.dt.from_np(x.dtype), kind="ExternalInput").ap())
    for shape, name in _OUTS:
        args.append(nc.dram_tensor(f"out_{name}", shape, F32, kind="ExternalOutput").ap())
    build(nc, *args)
    r = _run(nc, [arrays], core_ids=[0]).results[0]
    y, k, v, vs, va, hist = (r[f"out_{name}"] for _, name in _OUTS)
    y = y.transpose(2, 1, 0).reshape(T, D)
    k = k.transpose(2, 0, 1)
    v = v.transpose(1, 2, 0, 3).reshape(SEQ, H, HD)
    hist = hist.transpose(2, 1, 0).reshape(18, 2 * FF)
    out = (y[:SEQ].reshape(1, SEQ, D), y[SEQ:].reshape(DB, DT, D),
           k[:SEQ].reshape(1, 1, SEQ, H, HD), v.reshape(1, 1, SEQ, H, HD), hist[:2].reshape(1, 1, 2, 2 * FF),
           k[SEQ:].reshape(1, DB, DT, H, HD), vs.reshape(1, DB, DT, H, HD), hist[2:].reshape(1, DB, 2, 2 * FF),
           va.reshape(1, DB, DT, H, HD))
    return tuple(np.ascontiguousarray(a) for a in out)
```
